# Optimizing a Trainium2 kernel written in Bass

```python
import math
import jax, jax.numpy as jnp
from jax import lax
import numpy as np

D_MODEL = 2048
BATCH = 1
SEQ = 256
DEPTH = 1
DEC_BATCH = 8
DEC_SEQ = 4
PAST_LEN = 2048
PAGE_SIZE = 128

HEAD_DIM = 128
N_HEADS_A = 8
N_HEADS_B = 8
N_KV_B = 2
HPG = N_HEADS_B // N_KV_B
D_A = N_HEADS_A * HEAD_DIM
D_B = N_HEADS_B * HEAD_DIM
D_KV_B = N_KV_B * HEAD_DIM
ROPE_DIM = HEAD_DIM // 4
ROPE_THETA = 500000.0
SB_QBLOCK = 128
CMP_LEN = 32
CMP_STRIDE = 16
SLC_BLOCK = 64
N_SELECT = 16
WINDOW = 512
NSA_QBLOCK = 32
WIN_QBLOCK = 128
FORCE_SCORE = 1.0e4
PEER_HEADS = 8
PEER_NKEYS = 128
PEER_N = PEER_NKEYS * PEER_NKEYS
PEER_QDIM = 256
PEER_TOPK = 16
PEER_TBLOCK = 128
ALPHA = (2 * DEPTH) ** 0.25
BETA = (8 * DEPTH) ** -0.25
LN_EPS = 1e-5
IN_SIZES = (D_A, D_A, D_A, D_B, D_KV_B, D_KV_B, D_KV_B, D_KV_B, D_KV_B, D_KV_B, 3 * N_HEADS_B)
VALUE_PARTS = (2, 5, 7, 9)
IN_COLS = 3 * D_A + D_B + 6 * D_KV_B + 3 * N_HEADS_B

kernel_name = "sb_nsa_peer_hybrid_step"

def layer_norm(x, g, b):
    xf = x.astype(jnp.float32)
    mu = jnp.mean(xf, axis=-1, keepdims=True)
    var = jnp.mean(jnp.square(xf - mu), axis=-1, keepdims=True)
    return ((xf - mu) * lax.rsqrt(var + LN_EPS) * g + b).astype(x.dtype)

def partial_rope(x, pos):
    half = ROPE_DIM // 2
    inv = ROPE_THETA ** (-jnp.arange(half, dtype=jnp.float32) / half)
    ang = pos.astype(jnp.float32)[:, None] * inv[None, :]
    cos, sin = jnp.cos(ang)[:, None, :], jnp.sin(ang)[:, None, :]
    xr = x[..., :ROPE_DIM].astype(jnp.float32)
    x1, x2 = xr[..., :half], xr[..., half:]
    rot = jnp.concatenate([x1 * cos - x2 * sin, x2 * cos + x1 * sin], axis=-1)
    return jnp.concatenate([rot.astype(x.dtype), x[..., ROPE_DIM:]], axis=-1)

def masked_softmax(s, mask):
    s = jnp.where(mask, s.astype(jnp.float32), -1e30)
    m = jnp.max(s, axis=-1, keepdims=True)
    e = jnp.where(mask, jnp.exp(s - m), 0.0)
    return e / jnp.maximum(jnp.sum(e, axis=-1, keepdims=True), 1e-30)

def project(x, w_in, pos):
    B, T = x.shape[:2]
    offsets = np.cumsum(IN_SIZES)[:-1].tolist()
    qa, ka, va, qb, kc, vc, ks, vs, kw, vw, g = jnp.split(x @ w_in, offsets, axis=-1)
    ha = lambda t: t.reshape(B, T, N_HEADS_A, HEAD_DIM)
    hb = lambda t: t.reshape(B, T, N_KV_B, HEAD_DIM)
    qb = partial_rope(qb.reshape(B, T, N_HEADS_B, HEAD_DIM), pos).reshape(B, T, N_KV_B, HPG, HEAD_DIM)
    kc, ks, kw = partial_rope(hb(kc), pos), partial_rope(hb(ks), pos), partial_rope(hb(kw), pos)
    gates = jax.nn.sigmoid(g).reshape(B, T, N_KV_B, HPG, 3)
    return ha(qa), ha(ka), ha(va), qb, kc, hb(vc), ks, hb(vs), kw, hb(vw), gates

def stick_breaking(q, k, v, q_pos, k_pos):
    z = jnp.einsum('bqhd,bkhd->bhqk', q, k).astype(jnp.float32) / math.sqrt(HEAD_DIM)
    mask = k_pos[None, :] < q_pos[:, None]
    log_beta = jax.nn.log_sigmoid(z)
    log_rest = jnp.where(mask, jax.nn.log_sigmoid(-z), 0.0)
    nxt = jnp.concatenate([log_rest[..., 1:], jnp.zeros_like(log_rest[..., :1])], axis=-1)
    after = lax.cumsum(nxt, axis=3, reverse=True)
    w = jnp.where(mask, jnp.exp(log_beta + after), 0.0)
    return jnp.einsum('bhqk,bkhd->bqhd', w.astype(v.dtype), v)

def sb_prompt(q, k, v, pos):
    B, T = q.shape[:2]
    nb = T // SB_QBLOCK
    qb = jnp.moveaxis(q.reshape(B, nb, SB_QBLOCK, N_HEADS_A, HEAD_DIM), 1, 0)
    out = lax.map(lambda a: stick_breaking(a[0], k, v, a[1], pos), (qb, pos.reshape(nb, SB_QBLOCK)))
    return jnp.moveaxis(out, 0, 1).reshape(B, T, N_HEADS_A, HEAD_DIM)

def compress(rows, pe, w1, w2):
    L = rows.shape[1]
    n_cmp = (L - CMP_LEN) // CMP_STRIDE + 1
    idx = np.arange(n_cmp)[:, None] * CMP_STRIDE + np.arange(CMP_LEN)[None, :]
    blk = rows[:, idx] + pe[None, None, :, None, :]
    h = jax.nn.gelu(jnp.einsum('bnlgd,lde->bnge', blk, w1))
    return jnp.einsum('bnge,ef->bngf', h, w2)

def cmp_to_slc(n_cmp, n_sel):
    i = np.arange(n_cmp)[:, None]
    j = np.arange(n_sel)[None, :]
    lo = np.maximum(i * CMP_STRIDE, j * SLC_BLOCK)
    hi = np.minimum(i * CMP_STRIDE + CMP_LEN, (j + 1) * SLC_BLOCK)
    return jnp.asarray((np.maximum(hi - lo, 0) / CMP_STRIDE).astype(np.float32))

def to_sel_blocks(rows):
    B, L, G, d = rows.shape
    n_sel = -(-L // SLC_BLOCK)
    rows = jnp.pad(rows, ((0, 0), (0, n_sel * SLC_BLOCK - L), (0, 0), (0, 0)))
    return rows.reshape(B, n_sel, SLC_BLOCK, G, d).transpose(0, 3, 1, 2, 4)

def nsa_cmp_slc(q, q_pos, kcmp, vcmp, ks_blk, vs_blk):
    B, Tq = q.shape[:2]
    n_cmp, n_sel = kcmp.shape[1], ks_blk.shape[2]
    scale = 1.0 / math.sqrt(HEAD_DIM)
    cmp_end = jnp.arange(n_cmp, dtype=jnp.int32) * CMP_STRIDE + (CMP_LEN - 1)
    cmask = (cmp_end[None, :] <= q_pos[:, None])[None, :, None, None, :]
    s = jnp.einsum('btghd,bngd->btghn', q, kcmp).astype(jnp.float32) * scale
    p = masked_softmax(s, cmask)
    o_cmp = jnp.einsum('btghn,bngd->btghd', p.astype(vcmp.dtype), vcmp)
    imp = jnp.einsum('btghn,nj->btgj', p, cmp_to_slc(n_cmp, n_sel))
    j = jnp.arange(n_sel, dtype=jnp.int32)[None, :]
    qblk = (q_pos // SLC_BLOCK)[:, None]
    forced = ((j == 0) | (j == qblk) | (j == qblk - 1))[None, :, None, :]
    valid = (j * SLC_BLOCK <= q_pos[:, None])[None, :, None, :]
    imp = jnp.where(forced, FORCE_SCORE, jnp.where(valid, imp, -FORCE_SCORE))
    n_top = min(N_SELECT, n_sel)
    _, sel = lax.top_k(imp, n_top)
    b_i = jnp.arange(B)[:, None, None, None]
    g_i = jnp.arange(N_KV_B)[None, None, :, None]
    ks = ks_blk[b_i, g_i, sel]
    vs = vs_blk[b_i, g_i, sel]
    kpos = sel[..., None] * SLC_BLOCK + jnp.arange(SLC_BLOCK, dtype=jnp.int32)
    smask = (kpos <= q_pos[None, :, None, None, None]).reshape(B, Tq, N_KV_B, 1, n_top * SLC_BLOCK)
    s2 = jnp.einsum('btghd,btgnld->btghnl', q, ks).astype(jnp.float32) * scale
    p2 = masked_softmax(s2.reshape(B, Tq, N_KV_B, HPG, n_top * SLC_BLOCK), smask)
    o_slc = jnp.einsum('btghk,btgkd->btghd', p2.astype(vs.dtype),
                       vs.reshape(B, Tq, N_KV_B, n_top * SLC_BLOCK, HEAD_DIM))
    return o_cmp, o_slc

def band_attend(q, q_pos, k, v, k_pos):
    s = jnp.einsum('bnqghd,bnkgd->bnghqk', q, k).astype(jnp.float32) / math.sqrt(HEAD_DIM)
    dlt = q_pos[:, :, None] - k_pos[:, None, :]
    mask = (dlt >= 0) & (dlt < WINDOW) & (k_pos[:, None, :] >= 0)
    p = masked_softmax(s, mask[None, :, None, None])
    return jnp.einsum('bnghqk,bnkgd->bnqghd', p.astype(v.dtype), v)

def window_prompt(q, kw, vw):
    B, T = q.shape[:2]
    nb, nw = T // WIN_QBLOCK, WINDOW // WIN_QBLOCK
    pad = ((0, 0), (WINDOW, 0), (0, 0), (0, 0))
    kpb = jnp.pad(kw, pad).reshape(B, nb + nw, WIN_QBLOCK, N_KV_B, HEAD_DIM)
    vpb = jnp.pad(vw, pad).reshape(B, nb + nw, WIN_QBLOCK, N_KV_B, HEAD_DIM)
    k_slab = jnp.concatenate([kpb[:, i:i + nb] for i in range(nw + 1)], axis=2)
    v_slab = jnp.concatenate([vpb[:, i:i + nb] for i in range(nw + 1)], axis=2)
    q_pos = jnp.arange(T, dtype=jnp.int32).reshape(nb, WIN_QBLOCK)
    k_pos = (jnp.arange(nb, dtype=jnp.int32) * WIN_QBLOCK)[:, None] - WINDOW + jnp.arange(WINDOW + WIN_QBLOCK, dtype=jnp.int32)[None, :]
    o = band_attend(q.reshape(B, nb, WIN_QBLOCK, N_KV_B, HPG, HEAD_DIM), q_pos, k_slab, v_slab, k_pos)
    return o.reshape(B, T, N_KV_B, HPG, HEAD_DIM)

def nsa_merge(o_c, o_s, o_w, gates):
    return gates[..., 0:1] * o_c + gates[..., 1:2] * o_s + gates[..., 2:3] * o_w

def mixers_prompt(x, w_in, cmp_pe_k, cmp_w1_k, cmp_w2_k, cmp_pe_v, cmp_w1_v, cmp_w2_v):
    B, T, _ = x.shape
    pos = jnp.arange(T, dtype=jnp.int32)
    qa, ka, va, qb, kc, vc, ks, vs, kw, vw, gates = project(x, w_in, pos)
    o_a = sb_prompt(qa, ka, va, pos)
    kcmp = compress(kc, cmp_pe_k, cmp_w1_k, cmp_w2_k)
    vcmp = compress(vc, cmp_pe_v, cmp_w1_v, cmp_w2_v)
    ks_blk, vs_blk = to_sel_blocks(ks), to_sel_blocks(vs)
    nb = T // NSA_QBLOCK
    q_blocks = jnp.moveaxis(qb.reshape(B, nb, NSA_QBLOCK, N_KV_B, HPG, HEAD_DIM), 1, 0)
    o_c, o_s = lax.map(lambda a: nsa_cmp_slc(a[0], a[1], kcmp, vcmp, ks_blk, vs_blk),
                       (q_blocks, pos.reshape(nb, NSA_QBLOCK)))
    unblock = lambda t: jnp.moveaxis(t, 0, 1).reshape(B, T, N_KV_B, HPG, HEAD_DIM)
    o_w = window_prompt(qb, kw, vw)
    o_b = nsa_merge(unblock(o_c), unblock(o_s), o_w, gates)
    mix = jnp.concatenate([o_a.reshape(B, T, D_A), o_b.reshape(B, T, D_B)], axis=-1)
    new_a = jnp.stack([ka, va], axis=2)
    new_nsa = jnp.stack([kc, vc, ks, vs], axis=2)
    new_win = jnp.stack([kw, vw], axis=2)[:, T - min(WINDOW, T):]
    return mix, new_a, new_nsa, new_win

def mixers_sample(x, cache_a, cache_nsa, state_win, page_table, w_in,
                  cmp_pe_k, cmp_w1_k, cmp_w2_k, cmp_pe_v, cmp_w1_v, cmp_w2_v):
    B, T, _ = x.shape
    past = page_table.shape[1] * PAGE_SIZE
    pos = past + jnp.arange(T, dtype=jnp.int32)
    k_pos = jnp.arange(past + T, dtype=jnp.int32)
    qa, ka, va, qb, kc, vc, ks, vs, kw, vw, gates = project(x, w_in, pos)
    past_a = cache_a[page_table].reshape(B, past, 2, N_HEADS_A, HEAD_DIM)
    o_a = stick_breaking(qa, jnp.concatenate([past_a[:, :, 0], ka], axis=1),
                         jnp.concatenate([past_a[:, :, 1], va], axis=1), pos, k_pos)
    past_n = cache_nsa[page_table].reshape(B, past, 4, N_KV_B, HEAD_DIM)
    rows = [jnp.concatenate([past_n[:, :, i], new], axis=1) for i, new in enumerate((kc, vc, ks, vs))]
    kcmp = compress(rows[0], cmp_pe_k, cmp_w1_k, cmp_w2_k)
    vcmp = compress(rows[1], cmp_pe_v, cmp_w1_v, cmp_w2_v)
    o_c, o_s = nsa_cmp_slc(qb, pos, kcmp, vcmp, to_sel_blocks(rows[2]), to_sel_blocks(rows[3]))
    slab = jnp.concatenate([state_win, jnp.stack([kw, vw], axis=2)], axis=1)
    n_buf = state_win.shape[1]
    w_pos = past - n_buf + jnp.arange(n_buf + T, dtype=jnp.int32)
    o_w = band_attend(qb[:, None], pos[None], slab[:, None, :, 0], slab[:, None, :, 1], w_pos[None])[:, 0]
    o_b = nsa_merge(o_c, o_s, o_w, gates)
    mix = jnp.concatenate([o_a.reshape(B, T, D_A), o_b.reshape(B, T, D_B)], axis=-1)
    new_a = jnp.stack([ka, va], axis=2)
    new_nsa = jnp.stack([kc, vc, ks, vs], axis=2)
    keep = min(WINDOW, past + T)
    new_win = slab[:, slab.shape[1] - keep:]
    return mix, new_a, new_nsa, new_win

def peer_ffn(x, w_query, sub_keys, u_tab, v_tab):
    B, T, D = x.shape
    n = B * T
    xt = jnp.pad(x.reshape(n, D), ((0, -n % PEER_TBLOCK), (0, 0)))
    K = PEER_TOPK

    def block(xc):
        q = (xc @ w_query).reshape(PEER_TBLOCK, PEER_HEADS, 2, PEER_QDIM // 2)
        s = jnp.einsum('thcd,ckd->thck', q, sub_keys).astype(jnp.float32)
        top_s, top_i = lax.top_k(s, K)
        cand_s = (top_s[:, :, 0, :, None] + top_s[:, :, 1, None, :]).reshape(PEER_TBLOCK, PEER_HEADS, K * K)
        cand_i = (top_i[:, :, 0, :, None] * PEER_NKEYS + top_i[:, :, 1, None, :]).reshape(PEER_TBLOCK, PEER_HEADS, K * K)
        best_s, best_j = lax.top_k(cand_s, K)
        experts = jnp.take_along_axis(cand_i, best_j, axis=-1)
        gate = jax.nn.softmax(best_s, axis=-1)
        act = jax.nn.gelu(jnp.einsum('thkd,td->thk', u_tab[experts], xc))
        v = v_tab[experts]
        return jnp.einsum('thk,thkd->td', (gate * act).astype(v.dtype), v)

    y = lax.map(block, xt.reshape(-1, PEER_TBLOCK, D)).reshape(-1, D)[:n]
    return y.reshape(B, T, D)

def post_norm_block(x, mix, w_out, ln1_g, ln1_b, peer_w_query, peer_sub_keys, peer_u, peer_v, ln2_g, ln2_b):
    h = layer_norm(ALPHA * x + mix @ w_out, ln1_g, ln1_b)
    return layer_norm(ALPHA * h + peer_ffn(h, peer_w_query, peer_sub_keys, peer_u, peer_v), ln2_g, ln2_b)

def setup_inputs(seed: int = 0) -> dict:
    key = jax.random.key(seed)
    ks = jax.random.split(key, 24)
    f32 = jnp.float32
    nrm = lambda k, shape, scale: jax.random.normal(k, shape, f32) * scale
    n_pages = PAST_LEN // PAGE_SIZE
    n_used = DEC_BATCH * n_pages
    n_pool = (5 * n_used + 3) // 4
    page_table = jax.random.permutation(ks[0], n_pool)[:n_used].reshape(DEC_BATCH, n_pages).astype(jnp.int32)
    col_scale = np.concatenate([np.full(s, BETA if i in VALUE_PARTS else 1.0, np.float32)
                                for i, s in enumerate(IN_SIZES)])
    w_in = nrm(ks[1], (DEPTH, D_MODEL, IN_COLS), D_MODEL ** -0.5) * jnp.asarray(col_scale)
    return {
        'x_prompt': nrm(ks[2], (BATCH, SEQ, D_MODEL), 1.0),
        'x_sample': nrm(ks[3], (DEC_BATCH, DEC_SEQ, D_MODEL), 1.0),
        'cache_a': nrm(ks[4], (DEPTH, n_pool, PAGE_SIZE, 2, N_HEADS_A, HEAD_DIM), 1.0),
        'cache_nsa': nrm(ks[5], (DEPTH, n_pool, PAGE_SIZE, 4, N_KV_B, HEAD_DIM), 1.0),
        'state_win': nrm(ks[6], (DEPTH, DEC_BATCH, min(WINDOW, PAST_LEN), 2, N_KV_B, HEAD_DIM), 1.0),
        'page_table': page_table,
        'w_in': w_in,
        'cmp_pe_k': nrm(ks[7], (DEPTH, CMP_LEN, HEAD_DIM), 0.02),
        'cmp_w1_k': nrm(ks[8], (DEPTH, CMP_LEN, HEAD_DIM, HEAD_DIM), (CMP_LEN * HEAD_DIM) ** -0.5),
        'cmp_w2_k': nrm(ks[9], (DEPTH, HEAD_DIM, HEAD_DIM), HEAD_DIM ** -0.5),
        'cmp_pe_v': nrm(ks[10], (DEPTH, CMP_LEN, HEAD_DIM), 0.02),
        'cmp_w1_v': nrm(ks[11], (DEPTH, CMP_LEN, HEAD_DIM, HEAD_DIM), (CMP_LEN * HEAD_DIM) ** -0.5),
        'cmp_w2_v': nrm(ks[12], (DEPTH, HEAD_DIM, HEAD_DIM), HEAD_DIM ** -0.5),
        'w_out': nrm(ks[13], (DEPTH, D_MODEL, D_MODEL), BETA * D_MODEL ** -0.5),
        'ln1_g': 1.0 + nrm(ks[14], (DEPTH, D_MODEL), 0.02),
        'ln1_b': nrm(ks[15], (DEPTH, D_MODEL), 0.02),
        'peer_w_query': nrm(ks[16], (DEPTH, D_MODEL, PEER_HEADS * PEER_QDIM), D_MODEL ** -0.5),
        'peer_sub_keys': nrm(ks[17], (DEPTH, 2, PEER_NKEYS, PEER_QDIM // 2), (PEER_QDIM // 2) ** -0.5),
        'peer_u': nrm(ks[18], (DEPTH, PEER_N, D_MODEL), D_MODEL ** -0.5),
        'peer_v': nrm(ks[19], (DEPTH, PEER_N, D_MODEL), BETA),
        'ln2_g': 1.0 + nrm(ks[20], (DEPTH, D_MODEL), 0.02),
        'ln2_b': nrm(ks[21], (DEPTH, D_MODEL), 0.02),
    }

def reference(x_prompt, x_sample, cache_a, cache_nsa, state_win, page_table, w_in,
              cmp_pe_k, cmp_w1_k, cmp_w2_k, cmp_pe_v, cmp_w1_v, cmp_w2_v, w_out, ln1_g, ln1_b,
              peer_w_query, peer_sub_keys, peer_u, peer_v, ln2_g, ln2_b):
    yp, ys = x_prompt, x_sample
    a_p, n_p, w_p, a_s, n_s, w_s = [], [], [], [], [], []
    for l in range(DEPTH):
        cmp_args = (cmp_pe_k[l], cmp_w1_k[l], cmp_w2_k[l], cmp_pe_v[l], cmp_w1_v[l], cmp_w2_v[l])
        ffn_args = (w_out[l], ln1_g[l], ln1_b[l], peer_w_query[l], peer_sub_keys[l], peer_u[l], peer_v[l], ln2_g[l], ln2_b[l])
        mix_p, na_p, nn_p, nw_p = mixers_prompt(yp, w_in[l], *cmp_args)
        mix_s, na_s, nn_s, nw_s = mixers_sample(ys, cache_a[l], cache_nsa[l], state_win[l], page_table, w_in[l], *cmp_args)
        yp = post_norm_block(yp, mix_p, *ffn_args)
        ys = post_norm_block(ys, mix_s, *ffn_args)
        a_p.append(na_p); n_p.append(nn_p); w_p.append(nw_p)
        a_s.append(na_s); n_s.append(nn_s); w_s.append(nw_s)
    return (yp, ys, jnp.stack(a_p), jnp.stack(n_p), jnp.stack(w_p), jnp.stack(a_s), jnp.stack(n_s), jnp.stack(w_s))


_drawn_inputs = setup_inputs


def setup_inputs(seed=0):
    import zlib

    import numpy as np

    out = dict(_drawn_inputs(seed))
    spreads = {}
    factors = {'cmp_pe_k': 38.645, 'cmp_pe_v': 4.43, 'ln2_g': 8.144, 'ln2_b': 7.891}
    for name, (base, spread) in spreads.items():
        noise = np.random.default_rng([zlib.crc32(name.encode()), seed]).standard_normal(out[name].shape)
        drawn = base * np.exp(spread * noise) if base else spread * noise
        out[name] = __import__('jax').numpy.asarray(drawn.astype(out[name].dtype))
    for name, factor in factors.items():
        out[name] = (out[name] * factor).astype(out[name].dtype)
    return out
```

```python
from contextlib import ExitStack, contextmanager

import numpy as np

import concourse.bass as bass
from concourse import mybir

F32 = mybir.dt.float32
U32 = mybir.dt.uint32
I32 = mybir.dt.int32
ALU = mybir.AluOpType
ACT = mybir.ActivationFunctionType
AX = mybir.AxisListType

P = 128
DM = 2048
KT = DM // P
NPROMPT = 256
NB, NT = 8, 4
NSMP = NB * NT
T = NPROMPT + NSMP
PAST, PAGE, NPAGE = 2048, 128, 16
HD = 128
NH = 8
NG, HPG = 2, 4
ROPE = 32
SEL_BLOCK, NSEL, NTOP = 64, 33, 16
WIN = 512
NCP = (NPROMPT - 32) // 16 + 1
NCS = (PAST + NT - 32) // 16 + 1
PTOK, PNEW = NPROMPT, NSMP
SCALE = 1.0 / float(np.sqrt(HD))
ALPHA = 2.0 ** 0.25
EPS = 1e-5
NEG = -1.0e30
FORCE = 1.0e4
GELU_A, GELU_C = 0.044715, 2.0 * float(np.sqrt(2.0 / np.pi))
SLOTS = 128

QA, KA, VA, QB, KC, VC, KS, VS, KW, VW = 0, 8, 16, 24, 32, 34, 36, 38, 40, 42
NM = 44
ROPED = list(range(QB, QB + NH)) + [KC, KC + 1, KS, KS + 1, KW, KW + 1]
VTILES = list(range(VA, VA + NH)) + [VS, VS + 1, VW, VW + 1]

CONST_COLS = {"ident": 128, "ones": 128, "suffix": 128, "swap": 128, "strict": 128, "causal": 256,
              "new_sb": 32, "new_add": 64, "win_add": 4, "cmp_add": 30, "cmp_mul": 30, "cmp_slc": 33,
              "group": 128, "lower": NSEL * NSEL, "fold": 32, "tok_row": 256, "head_row": 8, "iota16": 16}
CONST_AT = {}
_at = 0
for _name, _n in CONST_COLS.items():
    CONST_AT[_name] = _at
    _at += _n
NCONST = _at


def constants():
    c = np.zeros((P, NCONST), np.float32)

    def put(name, a):
        c[:a.shape[0], CONST_AT[name]:CONST_AT[name] + a.shape[1]] = a

    p = np.arange(P)
    put("ident", np.eye(P))
    put("ones", np.ones((P, P)))
    put("suffix", (p[:, None] >= p[None, :]).astype(np.float32))
    swap = np.zeros((P, P))
    half = ROPE // 2
    for m in range(half):
        swap[m + half, m] = -1.0
        swap[m, m + half] = 1.0
    put("swap", swap)
    put("strict", (p[:, None] < p[None, :]).astype(np.float32))
    causal = np.zeros((P, 2 * P))
    causal[:, P:] = np.where(p[None, :] > p[:, None], NEG, 0.0)
    put("causal", causal)
    tok = np.arange(NSMP)
    b, t = tok // NT, tok % NT
    put("new_sb", ((b[:, None] == b[None, :]) & (t[:, None] < t[None, :])).astype(np.float32))
    row_t, row_b = p % NT, p // 32
    new = np.zeros((P, 2, NSMP))
    rows = np.zeros((NSMP, 2, P))
    for h in range(2):
        same = (row_b[:, None] + 4 * h) == b[None, :]
        new[:, h] = np.where(same & (t[None, :] <= row_t[:, None]), 0.0, NEG)
        rows[:, h] = (tok[:, None] == ((row_b + 4 * h) * NT + row_t)[None, :])
    put("new_add", new.reshape(P, -1))
    put("tok_row", rows.reshape(NSMP, -1))
    put("win_add", np.where(np.arange(4)[None, :] <= row_t[:, None], NEG, 0.0))
    q = np.arange(2)[None, :, None] * P + p[:, None, None]
    seen = (np.arange(NCP)[None, None, :] * 16 + 31) <= q
    put("cmp_add", np.where(seen, 0.0, NEG).reshape(P, -1))
    put("cmp_mul", seen.astype(np.float32).reshape(P, -1))
    i, j = np.arange(NCS)[:, None], np.arange(NSEL)[None, :]
    lo, hi = np.maximum(i * 16, j * SEL_BLOCK), np.minimum(i * 16 + 32, (j + 1) * SEL_BLOCK)
    put("cmp_slc", (np.maximum(hi - lo, 0) / 16).astype(np.float32))
    put("group", ((p[:, None] // 16 == p[None, :] // 16) & (p[:, None] % NT == p[None, :] % NT)).astype(np.float32))
    s = np.arange(NSEL)
    put("lower", np.broadcast_to((s[None, :] < s[:, None]).astype(np.float32).reshape(1, -1), (P, NSEL * NSEL)))
    put("fold", (p[:, None] % NSMP == np.arange(NSMP)[None, :]).astype(np.float32))
    put("head_row", ((p[:, None] % 32) // NT == np.arange(NH)[None, :]).astype(np.float32))
    put("iota16", np.broadcast_to(np.arange(16, dtype=np.float32)[None], (P, 16)))
    return c


def rope_tables():
    half = ROPE // 2
    inv = (np.float32(500000.0) ** (-np.arange(half, dtype=np.float32) / np.float32(half))).astype(np.float32)
    pos = np.concatenate([np.arange(NPROMPT), PAST + np.tile(np.arange(NT), NB)]).astype(np.float32)
    ang = (pos[None, :] * inv[:, None]).astype(np.float32).astype(np.float64)
    cs = np.zeros((P, 2, T), np.float32)
    cs[:, 0] = 1.0
    cs[:ROPE, 0] = np.tile(np.cos(ang), (2, 1))
    cs[:ROPE, 1] = np.tile(np.sin(ang), (2, 1))
    return cs


RING = 8
ROUND = RING
STREAM = [("w_in", NM, 1), ("cmp", 32, 8), ("ks", 16, 8), ("kw", 4, 1), ("vs", 16, 8), ("vw", 4, 1),
          ("ak", 64, 2), ("av", 64, 2), ("wo", 16, 1), ("wq", 16, 1)]


class Stream:

    def __init__(self):
        self.first, self.before, self.dmas = {}, {}, {}
        n, full = 0, [0] * RING
        for name, count, dmas in STREAM:
            self.first[name], self.before[name], self.dmas[name] = n, list(full), dmas
            for j in range(count):
                full[(n + j) % RING] += 16 * dmas
            n += count
        self.total = n

    def slot(self, name, k):
        return (self.first[name] + k) % RING

    def full(self, name, it, k):
        return self.before[name][self.slot(name, k)] + 16 * self.dmas[name] * (it + 1)

    def room(self, name, it, k):
        return self.first[name] + 8 * it + k + 1

    def used(self, name, it, k):
        return RING + self.first[name] + 8 * it + k + 1


class Chain:

    def __init__(self, eng, sem):
        self.eng, self.sem, self.n, self.loop = eng, sem, 0, None

    def value(self):
        if self.loop is None:
            return self.n
        i, base, per = self.loop
        return i * per + self.n

    def do(self, ins):
        ins.then_inc(self.sem, 1)
        self.n += 1
        self.eng.wait_ge(self.sem, self.value())

    def tell(self, ins, sem, value):
        ins.then_inc(sem, 1)
        self.eng.wait_ge(sem, value)

    @contextmanager
    def rounds(self, count, per):
        with self.eng.Fori(0, count) as i:
            base = self.n
            self.loop = (i, base, per)
            yield i
            self.loop = None
            assert self.n - base == per, (self.n - base, per)
        self.n = base + count * per


AT_CONST = 0
AT_SMALL = 2880
AT_H = AT_SMALL + 1344
AT_PROJ = AT_H + 3 * DM
AT_X = AT_PROJ + NM * T
AT_RING = AT_X + KT * T
AT_T = AT_RING + RING * 2048
WORDS = 53200

OUTS = {"out_y": (T, DM), "out_a": (P, 16, T), "out_n": (P, 12, T),
        "out_win_k": (NB // 2, P, 2, NG * WIN), "out_win_v": (NB // 2, P, 2, 4, NG * P)}


def hybrid_step(nc, dram, outs):
    stream = Stream()
    with ExitStack() as ctx:
        def sem(name):
            return ctx.enter_context(nc.semaphore(name))

        sb = ctx.enter_context(nc.sbuf_tensor("sb", [P, WORDS], F32))
        bank = [ctx.enter_context(nc.psum_tensor(f"bank{i}", [P, 512], F32)) for i in range(8)]

        def words(at, *shape):
            n = int(np.prod(shape))
            v = sb[:, at:at + n]
            if len(shape) == 1:
                return v
            names = " ".join("abcd"[:len(shape)])
            return v.rearrange(f"p ({names}) -> p {names}", **{"abcd"[i]: s for i, s in enumerate(shape)})

        const = {k: words(AT_CONST + a, CONST_COLS[k]) for k, a in CONST_AT.items()}
        ident, ones = const["ident"], const["ones"]
        _small = [AT_SMALL]

        def small(*shape):
            at = _small[0]
            _small[0] += int(np.prod(shape))
            assert _small[0] <= AT_H
            return words(at, *shape)

        cmp_w2 = small(2, P)
        cmp_pe = small(2, 32)
        pe_bias = small(2)
        prompt_kcmp = small(NG, 16)
        prompt_vcmp = small(NG, P)
        prompt_gate = small(2, 24)
        smp_gate_tok = small(24)
        smp_gate = small(2, 3)
        gate_tmp = small(2, 24)
        soft = small(64)
        pages_sb = sb[0:1, _small[0]:_small[0] + P].bitcast(I32)
        _small[0] += P
        _ = small(1)

        proj = words(AT_PROJ, NM, T)
        x_t = words(AT_X, KT, T)
        mix_t = x_t
        ring = [words(AT_RING + 2048 * s, 2048) for s in range(RING)]

        vcmp = words(AT_H, NB, NG * P)
        kcmp_t = words(AT_H + 2048, NB, NG * P)
        v_new = words(AT_H + 4608, 12, P)
        w_gate = words(AT_H + 4096, KT, 24)
        x_cmp = words(AT_H + 4096, 256)
        e_cmp = words(AT_H + 4352, 256)
        w1 = words(AT_T, 2, 32, P)
        rope = words(AT_T + 8192, 2, T)
        h_cmp = [words(AT_T + 8192 + 256 * k, 256) for k in range(2)]
        u_cmp = words(AT_T + 8704, 256)
        rope_tmp = words(AT_H, 2, T)

        item_used = sem("item_used")
        ring_full = [sem(f"ring_full{s}") for s in range(RING)]
        consts_in, x_in, wg_in, rope_in, w1_in, pages_in = (sem(n) for n in (
            "consts_in", "x_in", "wg_in", "rope_in", "w1_in", "pages_in"))
        dve_step, act_step = sem("dve_step"), sem("act_step")
        proj_evac = sem("proj_evac")
        gate_raw, gate_exp, gate_tok, gate_rows = (sem(n) for n in ("gate_raw", "gate_exp", "gate_tok", "gate_rows"))
        swapped, roped = sem("swapped"), sem("roped")
        rows_out = sem("rows_out")
        bias_ready, bias_sb = sem("bias_ready"), sem("bias_sb")
        v_turned, v_new_in = sem("v_turned"), sem("v_new_in")
        ab_free, gelu_arg, gelu_exp, gelu_out = (sem(n) for n in ("ab_free", "gelu_arg", "gelu_exp", "gelu_out"))
        cmp_mm, cmp_in = sem("cmp_mm"), sem("cmp_in")

        s_slc = words(AT_T, 2, 2080)
        p_slc_t = words(AT_T + 4160, 17, 2, P)
        q_pad = words(AT_T + 8512, NB, NG, 32)
        s_win = words(AT_H + 2048, 2, 544)
        p_win_t = words(AT_H + 3136, 5, 2, P)
        s_cmp = words(AT_X, 2, P)
        sum_cmp_t = words(AT_X + 256, 2, P)
        p_cmp_t = words(AT_X + 512, 2, P)
        imp = words(AT_X + 768, 2, NSEL)
        rank = words(AT_X + 840, 2, NSEL)
        sel_add = words(AT_X + 912, 2, NSEL)
        above = words(AT_X + 984, NSEL, NSEL)
        ties = words(AT_X + 984 + 1089, NSEL, NSEL)
        pc_ab, pc_mm, pc_in = sem("pc_ab"), sem("pc_mm"), sem("pc_in")
        q_pad_in, cmp_scored, cmp_neg, cmp_exp, cmp_p = (sem(n) for n in ("q_pad_in", "cmp_scored", "cmp_neg", "cmp_exp", "cmp_p"))
        cmp_sum, cmp_sum_in, imp_ready, imp_in = (sem(n) for n in ("cmp_sum", "cmp_sum_in", "imp_ready", "imp_in"))
        cmp_pg, slc_evac, new_scored, new_evac, win_evac = (sem(n) for n in (
            "cmp_pg", "slc_evac", "new_scored", "new_evac", "win_evac"))
        soft_neg, soft_exp, soft_p, turned, turned_in = (sem(n) for n in (
            "soft_neg", "soft_exp", "soft_p", "turned", "turned_in"))
        mix_nsa = sem("mix_nsa")
        o_nsa = words(AT_T, 2, NG * P)
        o_nsa_in, o_nsa_t, padded = sem("o_nsa_in"), sem("o_nsa_t"), sem("padded")
        v_a = words(AT_T, 2, NH, P)
        s_pr = words(AT_T + 2048, HPG, 2, 2 * P)
        p_pr_t = words(AT_T + 4096, 2, 2, HPG, P)
        p_prc_t = words(AT_T + 6144, HPG, P)
        s_prc = words(AT_T + 6656, HPG, 16)
        v_b = words(AT_H, 2, 4, P)
        pr_max = words(AT_T + 6720, 12)
        pr_sum = words(AT_T + 6732, 12)
        z_pr = words(AT_T + 2048, NH, 3 * P)
        sp_pr = words(AT_T + 2048 + 3072, NH, 3 * P)
        e_pr = words(AT_H + 1024, NH, 3 * P)
        vp_turned, vp_in = sem("vp_turned"), sem("vp_in")
        pb_scored, pb_neg, pb_negc, pb_exp, pb_p, pb_turned, pb_turned_in, pb_pv, pb_out = (sem(n) for n in (
            "pb_scored", "pb_neg", "pb_negc", "pb_exp", "pb_p", "pb_turned", "pb_turned_in", "pb_pv", "pb_out"))
        pa_z, pa_z_in, pa_neg, pa_log, pa_sp, pa_g, pa_arg, pa_exp, pa_w, pa_pv, pa_out = (sem(n) for n in (
            "pa_z", "pa_z_in", "pa_neg", "pa_log", "pa_sp", "pa_g", "pa_arg", "pa_exp", "pa_w", "pa_pv", "pa_out"))
        z_t = words(AT_T, 2, NPAGE, P)
        sp_t = words(AT_T + 4096, 2, NPAGE, P)
        e_t = words(AT_H, 2, NPAGE, P)
        later = e_t
        o_a = words(AT_H, 2, 2, 512)
        q_pad_a = words(AT_PROJ + QB * T, 4, NH, 32)
        z_nat = [words(AT_PROJ + QB * T + 1024 + 512 * k, 512) for k in range(2)]
        z_new = words(AT_PROJ + KC * T, NH, NSMP)
        sp_new = words(AT_PROJ + KC * T + 256, NH, NSMP)
        e_new = words(AT_PROJ + KC * T + 512, NH, NSMP)
        sn_z, sn_z_in, sn_neg, sn_log, sn_sp, sn_g, sn_arg, sn_exp, sn_w, sn_pv, sn_out = (sem(n) for n in (
            "sn_z", "sn_z_in", "sn_neg", "sn_log", "sn_sp", "sn_g", "sn_arg", "sn_exp", "sn_w", "sn_pv", "sn_out"))
        q_pad_a_in, z_nat_in, z_turned, z_t_in, sa_neg, sa_log, sa_later, sa_g, sa_arg, sa_w = (sem(n) for n in (
            "q_pad_a_in", "z_nat_in", "z_turned", "z_t_in", "sa_neg", "sa_log", "sa_later", "sa_g", "sa_arg", "sa_w"))
        o_a_in, o_a_t, mix_a = sem("o_a_in"), sem("o_a_t"), sem("mix_a")
        h_nat = words(AT_H, 3, DM)
        h_t = x_t
        norm = words(AT_PROJ, 4, DM)
        s_key = [words(AT_T, 16, P), words(AT_T + 2048, 16, P), words(AT_PROJ + 8192, 16, P)]
        q_t = words(AT_T + 4096, 16, T)
        one_hot = words(AT_T + 6144, P, 16)
        h_rep = words(AT_T + 6144, DM)
        _tail = [AT_PROJ + 10240]

        def tail(*shape):
            at = _tail[0]
            _tail[0] += int(np.prod(shape))
            return words(at, *shape)

        top_s = tail(3, 16, 16)
        top_i = tail(3, 16, 16).bitcast(U32)
        best_s = tail(3, P)
        best_j = tail(3, P).bitcast(U32)
        assert _tail[0] <= AT_X
        _tail[0] = AT_PROJ
        work, cand, top_f = tail(256), tail(256), tail(16, 16)
        j_a, j_b = tail(P).bitcast(U32), tail(P).bitcast(U32)
        f_a, f_b, i_a, i_b, soft_sum = tail(P), tail(P), tail(P), tail(P), tail(16)
        expert = tail(288).bitcast(U32)
        peer_gate = tail(288)
        expert_s, gate_s = tail(P).bitcast(U32), tail(P)
        act16, w16 = tail(2, 16), tail(2, 16)
        u16, e16 = tail(16), tail(16)
        idx_u, idx_v = tail(2, 16).bitcast(U32), tail(2, 16).bitcast(U32)
        diag = [tail(P) for _ in range(4)]
        zeros = tail(P)
        assert _tail[0] <= AT_PROJ + 4096
        ln = words(AT_SMALL + 512, 64)
        sub_keys = words(AT_SMALL, 2, P)
        u_ring, v_ring = ring[0:4], ring[4:8]

        tok_in, norm_in, sub_in = sem("tok_in"), sem("norm_in"), sem("sub_in")
        wo_evac, ln_mu, ln_sq, ln_var, ln_sd, h_in, h_turned, h_t_in = (sem(n) for n in (
            "wo_evac", "ln_mu", "ln_sq", "ln_var", "ln_sd", "h_in", "h_turned", "h_t_in"))
        q_in, s_mm, s_in, picked, gate_arg, gate_e, chosen = (sem(n) for n in ("q_in", "s_mm", "s_in", "picked", "gate_arg", "gate_e", "chosen"))
        u_full = [sem(f"u_full{k}") for k in range(4)]
        v_full = [sem(f"v_full{k}") for k in range(4)]
        idx_in, u_used, v_used, act_arg, act_e, w_ready, diag_in, tile_out, y_out = (sem(n) for n in (
            "idx_in", "u_used", "v_used", "act_arg", "act_e", "w_ready", "diag_in", "tile_out", "y_out"))
        y_ready, held = sem("y_ready"), sem("held")
        rows_of = [P, P, NSMP]
        TOPK_IN = {r: {3: [(1, 2 * r)], 11: [(1, 2 * r + 1)]} for r in range(4)}
        TOPK_IN[4] = {7: [(2, 0)], 12: [(2, 1)]}
        TOPK_IN[5] = {2: [(2, 2)], 7: [(2, 3)], 12: [(2, 4)]}
        TOPK_IN[6] = {2: [(2, 5)], 7: [(2, 6)], 12: [(2, 7)]}
        GATES_IN = {4: 1, 7: 2}
        block = ctx.enter_context(nc.Block())

        @block.sync
        def _(sp):
            def room(name, it, k):
                sp.wait_ge(item_used, stream.room(name, it, k))

            sp.dma_start(pages_sb, dram["pages"]).then_inc(pages_in, 16)

            sp.dma_start(outs["out_win_k"], dram["win_k"]).then_inc(rows_out, 16)
            sp.dma_start(outs["out_win_v"], dram["win_v"]).then_inc(rows_out, 16)

            def load_w(it, k):
                room("w_in", it, k)
                s = stream.slot("w_in", k)
                src = dram["w_in"][bass.ds(8 * it + k, 1)].rearrange("m p k n -> (m p) (k n)")
                sp.dma_start(ring[s], src).then_inc(ring_full[s], 16)

            with sp.Fori(0, 5) as it:
                for k in range(8):
                    load_w(it, k)
            for k in range(4):
                load_w(5, k)

            def page(n):
                return sp.value_load(pages_sb[0:1, bass.ds(n, 1)], min_val=0, max_val=dram["a_k"].shape[0] - 1)

            sp.wait_ge(pages_in, 16)
            with sp.Fori(0, 4) as it:
                for k in range(8):
                    s = stream.slot("cmp", k)
                    b2, kv, half = k // 4, (k // 2) % 2, k % 2
                    found = [page(it * 32 + (b2 * 16 + half * 8 + j)) for j in range(8)]
                    room("cmp", it, k)
                    for j, pg in enumerate(found):
                        sp.dma_start(ring[s][:, 256 * j:256 * j + 256],
                                     dram["nsa_t"][bass.ds(pg, 1), kv].rearrange("a p n -> (a p) n")
                                     ).then_inc(ring_full[s], 16)
            sp.wait_ge(roped, len(ROPED))
            sp.dma_start(outs["out_a"], proj[:, KA:QB, :]).then_inc(rows_out, 16)
            sp.dma_start(outs["out_n"], proj[:, KC:NM, :]).then_inc(rows_out, 16)
            def load_pages(name, src, it, k, at):
                s = stream.slot(name, k)
                found = [page(at + j) for j in range(8)]
                room(name, it, k)
                for j, pg in enumerate(found):
                    sp.dma_start(ring[s][:, 256 * j:256 * j + 256], src(pg)).then_inc(ring_full[s], 16)

            with sp.Fori(0, 2) as it:
                for k in range(8):
                    load_pages("ks", lambda pg: dram["nsa_t"][bass.ds(pg, 1), 2].rearrange("a p n -> (a p) n"),
                               it, k, it * 64 + ((k % 4) * 16 + (k // 4) * 8))
            for k in range(4):
                room("kw", 0, k)
                s = stream.slot("kw", k)
                sp.dma_start(ring[s], dram["win_k"][k].rearrange("p b n -> p (b n)")).then_inc(ring_full[s], 16)
            with sp.Fori(0, 2) as it:
                for k in range(8):
                    load_pages("vs", lambda pg: dram["nsa_v"][bass.ds(pg, 1)].rearrange("a p n -> (a p) n"),
                               it, k, it * 64 + ((k % 4) * 16 + (k // 4) * 8))
            for k in range(4):
                room("vw", 0, k)
                s = stream.slot("vw", k)
                sp.dma_start(ring[s], dram["win_v"][k].rearrange("p b k n -> p (b k n)")).then_inc(ring_full[s], 16)
            def load_pair(name, src, it, k, half):
                s = stream.slot(name, k)
                found = [page(it * 4 + (48 * half + (k % 4) * 16 + (k // 4) * 2 + j)) for j in range(2)]
                room(name, it, k)
                for j, pg in enumerate(found):
                    sp.dma_start(ring[s][:, 1024 * j:1024 * j + 1024],
                                 dram[src][bass.ds(pg, 1)].rearrange("a p n -> (a p) n")).then_inc(ring_full[s], 16)

            for name, src in (("ak", "a_k"), ("av", "a_v")):
                for half in range(2):
                    with sp.Fori(4 * half, 4 * half + 4) as it:
                        for k in range(8):
                            load_pair(name, src, it, k, half)
            with sp.Fori(0, 2) as it:
                for k in range(8):
                    room("wo", it, k)
                    s = stream.slot("wo", k)
                    src = dram["w_out"].rearrange("n q p k c -> (n q) p (k c)")[bass.ds(8 * it + k, 1)].rearrange("a p c -> (a p) c")
                    sp.dma_start(ring[s], src).then_inc(ring_full[s], 16)
            with sp.Fori(0, 2) as it:
                for k in range(8):
                    room("wq", it, k)
                    s = stream.slot("wq", k)
                    src = dram["w_query"][bass.ds(8 * it + k, 1)].rearrange("m p k n -> (m p) (k n)")
                    sp.dma_start(ring[s], src).then_inc(ring_full[s], 16)
            for tt in range(3):
                n = rows_of[tt]
                sp.wait_ge(y_ready, tt + 1)
                sp.dma_start(outs["out_y"][P * tt:P * tt + n, :], h_nat[0:n, tt, :]).then_inc(y_out, 16)
            sp.wait_ge(y_out, 48)
            sp.wait_ge(rows_out, 64)

        @block.scalar
        def _(act):
            ch = Chain(act, act_step)
            act.dma_start(x_t, dram["tokens_t"]).then_inc(x_in, 16)
            act.dma_start(words(AT_CONST, NCONST), dram["consts"]).then_inc(consts_in, 16)
            act.dma_start(w_gate, dram["w_gate"]).then_inc(wg_in, 16)
            act.dma_start(rope, dram["rope"]).then_inc(rope_in, 16)
            act.dma_start(w1, dram["cmp_w1"]).then_inc(w1_in, 16)
            act.dma_start(cmp_w2, dram["cmp_w2"]).then_inc(w1_in, 16)
            act.dma_start(cmp_pe, dram["cmp_pe"]).then_inc(w1_in, 16)
            act.sem_inc(proj_evac, 2)
            act.sem_inc(cmp_in, 2)

            def evacuate(it, k):
                act.wait_ge(item_used, stream.used("w_in", it, k))
                act.activation(proj[:, bass.ds(8 * it + k, 1), :], bank[k % 2][:, None, 0:T], ACT.Copy).then_inc(proj_evac, 1)

            with act.Fori(0, 5) as it:
                for k in range(8):
                    evacuate(it, k)
            for k in range(4):
                evacuate(5, k)
            act.wait_ge(gate_raw, 1)
            act.activation(gate_tmp, bank[0][:, 0:48].rearrange("p (a b) -> p a b", a=2), ACT.Exp, scale=-1.0).then_inc(gate_exp, 1)
            act.activation(smp_gate_tok[0:NSMP], bank[0][0:NSMP, 48:72], ACT.Exp, scale=-1.0).then_inc(gate_exp, 1)

            with act.Fori(0, 4) as it:
                for st in range(4):
                    b2, kv = st // 2, st % 2
                    act.wait_ge(gelu_arg, 4 * it + st + 1)
                    act.activation(e_cmp, u_cmp, ACT.Exp, scale=-GELU_C).then_inc(gelu_exp, 1)
                    act.wait_ge(cmp_mm, 4 * it + st + 3)
                    dst = vcmp if kv else kcmp_t
                    act.activation(dst[:, bass.ds(2 * it + b2, 1), :], bank[4 + kv][:, None, 0:256], ACT.Copy).then_inc(cmp_in, 1)
            act.wait_ge(gelu_arg, 17)
            act.activation(e_cmp[:, 0:64], u_cmp[:, 0:64], ACT.Exp, scale=-GELU_C).then_inc(gelu_exp, 1)
            act.wait_ge(pc_mm, 1)
            act.activation(prompt_kcmp, bank[6][:, 0:32].rearrange("p (g n) -> p g n", g=NG), ACT.Copy).then_inc(pc_in, 1)
            act.activation(prompt_vcmp[0:NCP], bank[7][0:NCP, 0:256].rearrange("p (g n) -> p g n", g=NG), ACT.Copy).then_inc(pc_in, 1)

            for h in range(2):
                act.wait_ge(cmp_neg, h + 1)
                act.activation(s_cmp[:, h, 0:NCS], bank[h][:, 0:NCS], ACT.Exp, bias=soft[:, 2 + h:3 + h], scale=SCALE,
                               accum_out=soft[:, 4 + h:5 + h]).then_inc(cmp_exp, 1)
            act.wait_ge(cmp_sum, 1)
            act.activation(sum_cmp_t[0:NCS], bank[2][0:NCS, 0:256].rearrange("p (h n) -> p h n", h=2), ACT.Copy).then_inc(cmp_sum_in, 1)

            def soft_exps(h):
                act.wait_ge(soft_neg, 2 * h + 1)
                act.activation(s_slc[:, h], s_slc[:, h], ACT.Exp, bias=soft[:, 8 + h:9 + h], scale=SCALE,
                               accum_out=soft[:, 12 + h:13 + h]).then_inc(soft_exp, 1)
                act.wait_ge(soft_neg, 2 * h + 2)
                act.activation(s_win[:, h], s_win[:, h], ACT.Exp, bias=soft[:, 10 + h:11 + h], scale=SCALE,
                               accum_out=soft[:, 14 + h:15 + h]).then_inc(soft_exp, 1)

            soft_exps(0)
            soft_exps(1)
            for h in range(2):
                for n in range(6):
                    act.wait_ge(turned, 6 * h + n + 1)
                    src = bank[n % 4]
                    if n < 4:
                        ins = act.activation(p_slc_t[:, 4 * n:4 * n + 4, h, :], src[:, :].rearrange("p (a b) -> p a b", a=4), ACT.Copy)
                    elif n == 4:
                        ins = act.activation(p_win_t[:, 0:4, h, :], src[:, :].rearrange("p (a b) -> p a b", a=4), ACT.Copy)
                    else:
                        act.wait_ge(padded, 2)
                        ch.do(act.activation(p_slc_t[0:NSMP, 16, h, :], src[0:NSMP, 0:P], ACT.Copy))
                        ch.do(act.activation(p_win_t[0:NSMP, 4, h, :], src[0:NSMP, P:2 * P], ACT.Copy))
                        ins = act.activation(p_cmp_t[0:NCS, h, :], src[0:NCS, 2 * P:3 * P], ACT.Copy)
                    ins.then_inc(turned_in, 1)
            for n in range(6):
                act.wait_ge(vp_turned, n + 1)
                dst = (v_a[:, n // 2, 4 * (n % 2):4 * (n % 2) + 4] if n < 4 else v_b[:, n - 4])
                act.activation(dst, bank[n][:, :].rearrange("p (a b) -> p a b", a=4), ACT.Copy).then_inc(vp_in, 1)
            for u in range(4):
                qt, g = u // 2, u % 2
                nk = P * (qt + 1)
                act.wait_ge(pb_neg, u + 1)
                for hp in range(HPG):
                    for br in range(2):
                        n = 2 * hp + br
                        act.activation(s_pr[:, hp, br, 0:nk], s_pr[:, hp, br, 0:nk], ACT.Exp, bias=pr_max[:, n:n + 1], scale=SCALE,
                                       accum_out=pr_sum[:, n:n + 1]).then_inc(pb_exp, 1)
                act.wait_ge(pb_negc, u + 1)
                act.activation(s_prc[:, :, 0:NCP], s_prc[:, :, 0:NCP], ACT.Exp, scale=SCALE).then_inc(pb_exp, 1)
                for n in range(2 * (qt + 1)):
                    br, kt = n // (qt + 1), n % (qt + 1)
                    act.wait_ge(pb_turned, u // 2 * 5 + (u % 2) * (3 + 2 * qt) + (u // 2) + n + 1)
                    act.activation(p_pr_t[:, br, kt], bank[n][:, :].rearrange("p (a b) -> p a b", a=4), ACT.Copy).then_inc(pb_turned_in, 1)
                n = 2 * (qt + 1)
                act.wait_ge(pb_turned, u // 2 * 5 + (u % 2) * (3 + 2 * qt) + (u // 2) + n + 1)
                act.activation(p_prc_t[0:NCP], bank[4][0:NCP, :].rearrange("p (a b) -> p a b", a=4), ACT.Copy).then_inc(pb_turned_in, 1)

            for u in range(2):
                hs = slice(4 * u, 4 * u + 4)
                for j in range(4):
                    act.wait_ge(pa_z, 4 * u + j + 1)
                    act.activation(z_pr[:, 4 * u + j], bank[4 * u + j][:, 0:3 * P], ACT.Copy, scale=SCALE).then_inc(pa_z_in, 1)
            for u in range(2):
                hs = slice(4 * u, 4 * u + 4)
                act.wait_ge(pa_neg, u + 1)
                ch.do(act.activation(e_pr[:, hs], e_pr[:, hs], ACT.Exp))
                act.activation(e_pr[:, hs], e_pr[:, hs], ACT.Ln, bias=1.0).then_inc(pa_log, 1)
            for u in range(2):
                hs = slice(4 * u, 4 * u + 4)
                act.wait_ge(pa_arg, 4 * u + 4)
                act.activation(z_pr[:, hs], z_pr[:, hs], ACT.Exp).then_inc(pa_exp, 1)
            act.wait_ge(sn_z, 1)
            act.activation(z_new[0:NSMP], bank[0][0:NSMP, 0:256].rearrange("p (h n) -> p h n", h=NH), ACT.Copy, scale=SCALE).then_inc(sn_z_in, 1)
            act.wait_ge(sn_neg, 1)
            ch.do(act.activation(e_new[0:NSMP], e_new[0:NSMP], ACT.Exp))
            act.activation(e_new[0:NSMP], e_new[0:NSMP], ACT.Ln, bias=1.0).then_inc(sn_log, 1)
            act.wait_ge(sn_arg, 1)
            act.activation(z_new[0:NSMP], z_new[0:NSMP], ACT.Exp).then_inc(sn_exp, 1)

            def scores_out(half):
                with act.Fori(2 * half, 2 * half + 2) as it:
                    for k in range(2):
                        act.wait_ge(item_used, stream.used("ak", 2 * it + k, 7))
                        act.activation(z_nat[k], bank[3 + k][:, :], ACT.Copy, scale=SCALE).then_inc(z_nat_in, 1)

            def logs(half):
                act.wait_ge(sa_neg, half + 1)
                ch.do(act.activation(e_t[:, half], e_t[:, half], ACT.Exp))
                act.activation(e_t[:, half], e_t[:, half], ACT.Ln, bias=1.0).then_inc(sa_log, 1)

            act.sem_inc(z_nat_in, 2)
            scores_out(0)
            logs(0)
            scores_out(1)
            logs(1)
            for n in range(8):
                act.wait_ge(sa_arg, n + 1)
                zz = z_t[:, n // 4, 4 * (n % 4):4 * (n % 4) + 4]
                act.activation(zz, zz, ACT.Exp).then_inc(sa_w, 1)
            for half in range(2):
                act.wait_ge(item_used, stream.used("av", 4 * half + 3, 7))
                for c in range(2):
                    act.activation(o_a[:, half, c], bank[2 * half + c][:, :], ACT.Copy).then_inc(o_a_in, 1)
            def norm_act(n, tt, c):
                act.wait_ge(ln_mu, c)
                act.activation(words(AT_T, DM)[0:n], h_nat[0:n, tt, :], ACT.Square, bias=ln[0:n, 8 + tt:9 + tt],
                               accum_out=ln[0:n, 12 + tt:13 + tt]).then_inc(ln_sq, 1)
                act.wait_ge(ln_var, c)
                act.activation(ln[0:n, 16 + tt:17 + tt], ln[0:n, 12 + tt:13 + tt], ACT.Sqrt).then_inc(ln_sd, 1)

            for tt in range(3):
                norm_act(rows_of[tt], tt, tt + 1)
            for tt in range(3):
                n = rows_of[tt]
                for c in range(4):
                    act.wait_ge(h_turned, 4 * tt + c + 1)
                    act.activation(h_t[:, 4 * c:4 * c + 4, P * tt:P * tt + n],
                                   bank[6 + c % 2][:, :].rearrange("p (a b) -> p a b", a=4)[:, :, 0:n], ACT.Copy).then_inc(h_t_in, 1)
            for m in range(17):
                if m < 16:
                    act.wait_ge(item_used, stream.used("wq", m // 8, m % 8))
                    act.activation(q_t[:, m, :], bank[m % 2][:, 0:T], ACT.Copy).then_inc(q_in, 1)
                if m:
                    act.wait_ge(s_mm, m)
                    for tt in range(3):
                        n = rows_of[tt]
                        act.activation(s_key[tt][0:n, m - 1, :], bank[2 + (m - 1) % 2][0:n, P * tt:P * tt + P], ACT.Copy).then_inc(s_in, 1)
            def exp_of_gates(tt):
                n = rows_of[tt]
                act.wait_ge(gate_arg, tt + 1)
                act.activation(best_s[0:n, tt], best_s[0:n, tt], ACT.Exp).then_inc(gate_e, 1)

            exp_of_gates(0)

            def gelu_exp16(r):
                act.wait_ge(act_arg, r + 1)
                act.activation(e16, u16, ACT.Exp, scale=-GELU_C).then_inc(act_e, 1)

            def diagonals(r, par, folded):
                for j in range(16):
                    if j == 0:
                        act.wait_ge(w_ready, r + 1)
                    act.wait_ge(v_used, 16 * r + j + 1)
                    w = w16[:, par, j:j + 1]
                    if folded:
                        act.activation(diag[j % 4][:, 0:NSMP], const["fold"], ACT.Copy, scale=w).then_inc(diag_in, 1)
                    else:
                        act.activation(diag[j % 4], ident, ACT.Copy, scale=w).then_inc(diag_in, 1)

            act.sem_inc(diag_in, 32)
            with act.Fori(0, 2) as it:
                for par in range(2):
                    gelu_exp16(2 * it + par)
                    diagonals(2 * it + par, par, False)
            for r in range(4, 8):
                gelu_exp16(r)
                if r in GATES_IN:
                    exp_of_gates(GATES_IN[r])
                diagonals(r, r % 2, False)
            with act.Fori(4, 8) as it:
                for par in range(2):
                    gelu_exp16(2 * it + par)
                    diagonals(2 * it + par, par, False)
            for par in range(2):
                gelu_exp16(16 + par)
                if par == 0:
                    norm_act(P, 0, 4)
                diagonals(16 + par, par, True)
            norm_act(P, 1, 5)
            norm_act(NSMP, 2, 6)

        @block.tensor
        def _(pe):
            pe.sem_inc(item_used, RING)

            def arrived(name, it, k):
                s = stream.slot(name, k)
                pe.wait_ge(ring_full[s], stream.full(name, it, k))
                return ring[s]

            pe.wait_ge(x_in, 16)

            def project(it, k):
                w = arrived("w_in", it, k)
                pe.wait_ge(proj_evac, 8 * it + k + 1)
                for kt in range(KT):
                    mm = pe.matmul(bank[k % 2][:, 0:T], w[:, kt * P:(kt + 1) * P], x_t[:, kt, :],
                                   start=(kt == 0), stop=(kt == KT - 1))
                mm.then_inc(item_used, 1)

            with pe.Fori(0, 5) as it:
                for k in range(8):
                    project(it, k)
            for k in range(4):
                project(5, k)
            pe.wait_ge(wg_in, 16)
            pe.wait_ge(proj_evac, 2 + NM)
            for tt in range(3):
                n = P if tt < 2 else NSMP
                for kt in range(KT):
                    mm = pe.matmul(bank[0][0:n, 24 * tt:24 * tt + 24], x_t[:, kt, tt * P:tt * P + n], w_gate[:, kt, :],
                                   start=(kt == 0), stop=(kt == KT - 1), skip_group_check=True)
            mm.then_inc(gate_raw, 1)
            pe.wait_ge(consts_in, 16)
            for n, m in enumerate(ROPED):
                if n >= 2:
                    pe.wait_ge(roped, n - 1)
                pe.matmul(bank[2 + n % 2][:, 0:T], const["swap"], proj[:, m, :], start=True, stop=True).then_inc(swapped, 1)
            pe.wait_ge(gate_tok, 1)
            for h in range(2):
                mm = pe.matmul(bank[1][:, 24 * h:24 * h + 24], const["tok_row"][0:NSMP, P * h:P * h + P],
                               smp_gate_tok[0:NSMP], start=True, stop=True, skip_group_check=True)
            mm.then_inc(gate_rows, 1)
            for n, m in enumerate(VTILES):
                mm = pe.transpose(bank[5 + n // 4][0:NSMP, P * (n % 4):P * (n % 4) + P], proj[:, m, PTOK:T], ident)
            mm.then_inc(v_turned, 1)
            pe.wait_ge(w1_in, 48)
            for kv in range(2):
                for l in range(32):
                    mm = pe.matmul(bank[4][:, kv:kv + 1], w1[:, kv, l, :], cmp_pe[:, kv, l:l + 1],
                                   start=(l == 0), stop=(l == 31), skip_group_check=True)
            mm.then_inc(bias_ready, 1)
            pe.wait_ge(roped, len(ROPED))
            pe.wait_ge(v_new_in, 3)
            pe.wait_ge(bias_sb, 1)
            pe.sem_inc(cmp_mm, 2)

            def halves(it, st):
                kv = st % 2
                pe.wait_ge(ab_free, 4 * it + st + 1)
                ab = bank[2 + kv]
                for half in range(2):
                    k = 2 * st + half
                    rows = arrived("cmp", it, k).rearrange("p (c l) -> p c l", l=16)
                    for part in range(2):
                        for l in range(16):
                            mm = pe.matmul(ab[:, 256 * part + 128 * half:256 * part + 128 * half + 128],
                                           w1[:, kv, 16 * part + l, :], rows[:, :, l],
                                           start=(l == 0), stop=(l == 15), skip_group_check=True)
                    mm.then_inc(item_used, 1)

            def second(it, st):
                kv = st % 2
                pe.wait_ge(gelu_out, 4 * it + st + 1)
                pe.wait_ge(cmp_in, 4 * it + st + 1)
                if kv == 0:
                    mm = pe.matmul(bank[4][:, 0:256], cmp_w2[:, 0, :], h_cmp[0], start=True, stop=True)
                else:
                    for g in range(NG):
                        mm = pe.matmul(bank[5][:, P * g:P * g + P], h_cmp[1][:, P * g:P * g + P], cmp_w2[:, 1, :],
                                       start=True, stop=True, skip_group_check=True)
                mm.then_inc(cmp_mm, 1)

            with pe.Fori(0, 4) as it:
                halves(it, 0)
                for st in range(1, 4):
                    halves(it, st)
                    second(it, st - 1)
                second(it, 3)
            for kv in range(2):
                for part in range(2):
                    for l in range(16):
                        at = 64 * kv + 32 * part
                        rows = proj[:, KC + 2 * kv:KC + 2 * kv + 2, 0:NPROMPT].rearrange("p g (c l) -> p g c l", l=16)
                        mm = pe.matmul(bank[6][:, at:at + 32], w1[:, kv, 16 * part + l, :], rows[:, :, :, l],
                                       start=(l == 0), stop=(l == 15), skip_group_check=True)
            mm.then_inc(pc_ab, 1)
            pe.wait_ge(gelu_out, 17)
            pe.matmul(bank[6][:, 0:32], cmp_w2[:, 0, :], h_cmp[0][:, 0:32], start=True, stop=True)
            for g in range(NG):
                mm = pe.matmul(bank[7][0:16, P * g:P * g + P], h_cmp[0][:, 32 + 16 * g:48 + 16 * g], cmp_w2[:, 1, :],
                               start=True, stop=True, skip_group_check=True)
            mm.then_inc(pc_mm, 1)

            pe.wait_ge(q_pad_in, 1)
            pe.wait_ge(cmp_in, 2 + 16)
            for h in range(2):
                for b4 in range(4):
                    for g in range(NG):
                        mm = pe.matmul(bank[h][32 * b4:32 * b4 + 32, 0:P], q_pad[:, 4 * h + b4, g], kcmp_t[:, 4 * h + b4, P * g:P * g + P],
                                       start=(g == 0), stop=(g == 1))
                mm.then_inc(cmp_scored, 1)
            pe.wait_ge(cmp_p, 2)
            for h in range(2):
                mm = pe.matmul(bank[2][0:NCS, P * h:P * h + P], s_cmp[:, h, 0:NCS], const["group"], start=True, stop=True, skip_group_check=True)
            mm.then_inc(cmp_sum, 1)
            pe.wait_ge(cmp_sum_in, 1)
            for h in range(2):
                mm = pe.matmul(bank[3][:, NSEL * h:NSEL * h + NSEL], sum_cmp_t[0:NCS, h, :], const["cmp_slc"][0:NCS], start=True, stop=True,
                               skip_group_check=True)
            mm.then_inc(imp_ready, 1)
            pe.wait_ge(pc_in, 2)
            for h in range(2):
                for ph in range(2):
                    if h:
                        pe.wait_ge(slc_evac, 2 * ph + 2)
                    for b4 in range(4):
                        rows = arrived("ks", h, 4 * ph + b4).rearrange("p (q g n) -> p q g n", q=8, g=NG)
                        for c in range(2):
                            for g in range(NG):
                                mm = pe.matmul(bank[4 + 2 * ph + c][32 * b4:32 * b4 + 32, :], q_pad[:, 4 * h + b4, g],
                                               rows[:, 4 * c:4 * c + 4, g, :], start=(g == 0), stop=(g == 1))
                        mm.then_inc(item_used, 1)
            pe.wait_ge(imp_in, 1)
            for h in range(2):
                for b4 in range(4):
                    for n, m in enumerate((KS, KW)):
                        for g in range(NG):
                            at = 64 * n + 32 * h
                            mm = pe.matmul(bank[3][32 * b4:32 * b4 + 32, at:at + 32], q_pad[:, 4 * h + b4, g], proj[:, m + g, PTOK:T],
                                           start=(g == 0), stop=(g == 1), skip_group_check=True)
            mm.then_inc(new_scored, 1)
            pe.wait_ge(cmp_exp, 2)
            for k in range(4):
                rows = arrived("kw", 0, k).rearrange("p (b g n) -> p b g n", b=2, g=NG)
                for b2 in range(2):
                    b = 2 * k + b2
                    for g in range(NG):
                        mm = pe.matmul(bank[b // 4][32 * (b % 4):32 * (b % 4) + 32, :], q_pad[:, b, g], rows[:, b2, g, :],
                                       start=(g == 0), stop=(g == 1))
                mm.then_inc(item_used, 1)
            pe.wait_ge(win_evac, 4)
            pe.wait_ge(new_evac, 4)
            pe.wait_ge(cmp_pg, 2)
            for h in range(2):
                pe.wait_ge(soft_p, 2 * h + 2)
                for n in range(6):
                    if 6 * h + n >= 4:
                        pe.wait_ge(turned_in, 6 * h + n - 3 if n >= 4 else 6 * h)
                    dst = bank[n % 4]
                    if n < 5:
                        src = s_slc[:, h, 512 * n:512 * n + 512] if n < 4 else s_win[:, h, 0:512]
                        for j in range(4):
                            mm = pe.transpose(dst[:, P * j:P * j + P], src[:, P * j:P * j + P], ident)
                    else:
                        pe.transpose(dst[0:NSMP, 0:P], s_slc[:, h, PAST:], ident)
                        pe.transpose(dst[0:NSMP, P:2 * P], s_win[:, h, WIN:], ident)
                        mm = pe.transpose(dst[0:NCS, 2 * P:3 * P], s_cmp[:, h, 0:NCS], ident)
                    mm.then_inc(turned, 1)
            pe.wait_ge(turned_in, 12)
            pe.wait_ge(slc_evac, 8)
            pv = bank[7]
            for h in range(2):
                out = pv[:, 256 * h:256 * h + 256]
                parts = [(p_cmp_t[0:NCS, h], lambda b: vcmp[0:NCS, b, :]),
                         (p_slc_t[:, 16, h], lambda b: v_new[:, 8:10, :]),
                         (p_win_t[:, 4, h], lambda b: v_new[:, 10:12, :])]
                for n, (wt, val) in enumerate(parts):
                    for b4 in range(4):
                        r = slice(32 * b4, 32 * b4 + 32)
                        pe.matmul(out[r], wt[:, r], val(4 * h + b4), start=(n == 0 and h == 0), stop=False, skip_group_check=True)
            for h in range(2):
                out = pv[:, 256 * h:256 * h + 256]
                for ph in range(2):
                    rows = [arrived("vs", h, 4 * ph + b4) for b4 in range(4)]
                    for j in range(8):
                        for b4 in range(4):
                            r = slice(32 * b4, 32 * b4 + 32)
                            mm = pe.matmul(out[r], p_slc_t[:, 8 * ph + j, h, r], rows[b4][:, 256 * j:256 * j + 256], start=False, stop=False,
                                           skip_group_check=True)
                            if j == 7:
                                mm.then_inc(item_used, 1)
            for h in range(2):
                out = pv[:, 256 * h:256 * h + 256]
                rows = [arrived("vw", 0, 2 * h + k).rearrange("p (b k n) -> p b k n", b=2, k=4) for k in range(2)]
                for j in range(4):
                    for b4 in range(4):
                        r = slice(32 * b4, 32 * b4 + 32)
                        mm = pe.matmul(out[r], p_win_t[:, j, h, r], rows[b4 // 2][:, b4 % 2, j, :], start=False, stop=(j == 3),
                                       skip_group_check=True)
                        if j == 3 and b4 % 2:
                            mm.then_inc(item_used, 1)
            pe.wait_ge(o_nsa_in, 1)
            for h in range(2):
                for g in range(NG):
                    mm = pe.transpose(bank[h][:, P * g:P * g + P], o_nsa[:, h, P * g:P * g + P], ident)
            mm.then_inc(o_nsa_t, 1)
            pe.wait_ge(mix_nsa, 4)
            for n in range(6):
                for j in range(4):
                    kt, m = (n // 2, VA + 4 * (n % 2) + j) if n < 4 else (n - 4, (VS, VS + 1, VW, VW + 1)[j])
                    mm = pe.transpose(bank[n][:, P * j:P * j + P], proj[:, m, P * kt:P * kt + P], ident)
                mm.then_inc(vp_turned, 1)

            done_turned = 0
            for u in range(4):
                qt, g = u // 2, u % 2
                nk = P * (qt + 1)
                pe.wait_ge(vp_in, 6)
                if u:
                    pe.wait_ge(pb_turned_in, done_turned)
                for hp in range(HPG):
                    q = proj[:, QB + HPG * g + hp, P * qt:P * qt + P]
                    pe.matmul(bank[hp][:, 0:nk], q, proj[:, KS + g, 0:nk], start=True, stop=True, skip_group_check=True)
                    pe.matmul(bank[hp][:, 256:256 + nk], q, proj[:, KW + g, 0:nk], start=True, stop=True, skip_group_check=True)
                    mm = pe.matmul(bank[4][:, 16 * hp:16 * hp + NCP], q, prompt_kcmp[:, g, 0:NCP], start=True, stop=True, skip_group_check=True)
                mm.then_inc(pb_scored, 1)
                pe.wait_ge(pb_p, 2 * u + 2)
                for n in range(2 * (qt + 1)):
                    br, kt = n // (qt + 1), n % (qt + 1)
                    for hp in range(HPG):
                        mm = pe.transpose(bank[n][:, P * hp:P * hp + P], s_pr[:, hp, br, P * kt:P * kt + P], ident)
                    mm.then_inc(pb_turned, 1)
                for hp in range(HPG):
                    mm = pe.transpose(bank[4][0:NCP, P * hp:P * hp + P], s_prc[:, hp, 0:NCP], ident)
                mm.then_inc(pb_turned, 1)
                done_turned += 2 * (qt + 1) + 1
                pe.wait_ge(pb_turned_in, done_turned)
                if u >= 2:
                    pe.wait_ge(pb_out, u - 1)
                out = bank[5 + u % 2]
                for hp in range(HPG):
                    for br in range(2):
                        for kt in range(qt + 1):
                            pe.matmul(out[:, P * hp:P * hp + P], v_b[:, kt, 2 * br + g, :], p_pr_t[:, br, kt, hp, :],
                                      start=(br == 0 and kt == 0), stop=False, skip_group_check=True)
                    mm = pe.matmul(out[:, P * hp:P * hp + P], prompt_vcmp[0:NCP, g, :], p_prc_t[0:NCP, hp, :], start=False, stop=True,
                                   skip_group_check=True)
                mm.then_inc(pb_pv, 1)

            pe.wait_ge(pb_out, 4)
            for h in range(NH):
                pe.matmul(bank[h][:, 0:2 * P], proj[:, KA + h, 0:P], proj[:, QA + h, 0:2 * P], start=True, stop=True, skip_group_check=True)
                pe.matmul(bank[h][:, 2 * P:3 * P], proj[:, KA + h, P:2 * P], proj[:, QA + h, P:2 * P], start=True, stop=True,
                          skip_group_check=True).then_inc(pa_z, 1)
            for u in range(2):
                pe.wait_ge(pa_sp, u + 1)
                for h in range(4 * u, 4 * u + 4):
                    pe.wait_ge(pa_z_in, h + 1)
                    pe.matmul(bank[h][:, 0:2 * P], const["suffix"], sp_pr[:, h, 0:2 * P], start=True, stop=False, skip_group_check=True)
                    pe.matmul(bank[h][:, P:2 * P], ones, sp_pr[:, h, 2 * P:3 * P], start=False, stop=False, skip_group_check=True)
                    pe.matmul(bank[h][:, 2 * P:3 * P], const["suffix"], sp_pr[:, h, 2 * P:3 * P], start=False, stop=True,
                              skip_group_check=True).then_inc(pa_g, 1)
            for u in range(2):
                pe.wait_ge(pa_w, u + 1)
                for h in range(4 * u, 4 * u + 4):
                    pe.matmul(bank[h][:, 0:2 * P], v_a[:, 0, h, :], z_pr[:, h, 0:2 * P], start=True, stop=False, skip_group_check=True)
                    pe.matmul(bank[h][:, P:2 * P], v_a[:, 1, h, :], z_pr[:, h, 2 * P:3 * P], start=False, stop=True,
                              skip_group_check=True).then_inc(pa_pv, 1)
            pe.wait_ge(pa_out, NH)
            for h in range(NH):
                mm = pe.matmul(bank[0][0:NSMP, NSMP * h:NSMP * h + NSMP], proj[:, KA + h, PTOK:T], proj[:, QA + h, PTOK:T], start=True, stop=True,
                               skip_group_check=True)
            mm.then_inc(sn_z, 1)
            pe.wait_ge(sn_sp, 1)
            pe.matmul(bank[1][0:NSMP, 0:256], const["suffix"][0:NSMP, 0:NSMP], sp_new[0:NSMP].rearrange("p h n -> p (h n)"), start=True,
                      stop=True).then_inc(sn_g, 1)
            pe.wait_ge(sn_w, 1)
            for h in range(NH):
                mm = pe.matmul(bank[2][:, NSMP * h:NSMP * h + NSMP], v_new[0:NSMP, h, :], z_new[0:NSMP, h, :], start=True, stop=True,
                               skip_group_check=True)
            mm.then_inc(sn_pv, 1)
            for half in range(2):
                pe.wait_ge(q_pad_a_in, half + 1)
                with pe.Fori(2 * half, 2 * half + 2) as it:
                    for k in range(2):
                        pe.wait_ge(z_nat_in, 2 * it + k + 1)
                        for pp in range(2):
                            rows = [arrived("ak", 2 * it + k, 4 * pp + b4).rearrange("p (q h n) -> p q h n", q=2, h=NH) for b4 in range(4)]
                            for h in range(NH):
                                for b4 in range(4):
                                    mm = pe.matmul(bank[3 + k][32 * b4:32 * b4 + 32, 256 * pp:256 * pp + 256], q_pad_a[:, b4, h],
                                                   rows[b4][:, :, h, :], start=(h == 0), stop=(h == NH - 1), skip_group_check=True)
                                    if h == NH - 1:
                                        mm.then_inc(item_used, 1)
                    for k in range(2):
                        pe.wait_ge(z_nat_in, 2 * it + k + 3)
                        pe.wait_ge(z_t_in, 2 * it + k + 1)
                        for j in range(4):
                            mm = pe.transpose(bank[5 + k][:, P * j:P * j + P], z_nat[k][:, P * j:P * j + P], ident)
                        mm.then_inc(z_turned, 1)
            for n in range(8):
                half, q = n // 4, n % 4
                if q == 0:
                    pe.wait_ge(sa_later, half + 1)
                    pe.wait_ge(z_t_in, 2 + 8)
                if n >= 4:
                    pe.wait_ge(sa_arg, n - 3)
                bk = bank[4 + n % 4]
                pe.matmul(bk[:, :], const["suffix"], sp_t[:, half, 4 * q:4 * q + 4].rearrange("p q r -> p (q r)"), start=True, stop=False)
                pe.matmul(bk[:, :], ones, later[:, half, 4 * q:4 * q + 4].rearrange("p q r -> p (q r)"), start=False, stop=True).then_inc(sa_g, 1)
            for half in range(2):
                for pp in range(8):
                    if pp % 2 == 0:
                        pe.wait_ge(sa_w, 4 * half + pp // 2 + 1)
                    rows = [arrived("av", 4 * half + pp // 2, 4 * (pp % 2) + b4) for b4 in range(4)]
                    for j in range(2):
                        for c in range(2):
                            for b4 in range(4):
                                r = slice(32 * b4, 32 * b4 + 32)
                                mm = pe.matmul(bank[2 * half + c][r, :], z_t[:, half, 2 * pp + j, r],
                                               rows[b4][:, 1024 * j + 512 * c:1024 * j + 512 * c + 512],
                                               start=(pp == 0 and j == 0), stop=(pp == 7 and j == 1))
                                if j == 1 and c == 1:
                                    mm.then_inc(item_used, 1)
            for half in range(2):
                pe.wait_ge(o_a_in, 2 * half + 2)
                for c in range(2):
                    for j in range(4):
                        mm = pe.transpose(bank[4 + 2 * half + c][:, P * j:P * j + P], o_a[:, half, c, P * j:P * j + P], ident)
                    mm.then_inc(o_a_t, 1)
            pe.wait_ge(mix_a, 16)
            for it in range(2):
                for k in range(8):
                    n, kq = (8 * it + k) // 4, k % 4
                    w = arrived("wo", it, k).rearrange("p (k c) -> p k c", k=4)
                    if kq == 0 and n >= 2:
                        pe.wait_ge(wo_evac, 3 * (n - 1))
                    for kt in range(4):
                        for tt in range(3):
                            r = rows_of[tt]
                            mm = pe.matmul(bank[3 * (n % 2) + tt][0:r, :], mix_t[:, 4 * kq + kt, P * tt:P * tt + r], w[:, kt, :],
                                           start=(kq == 0 and kt == 0), stop=(kq == 3 and kt == 3))
                    mm.then_inc(item_used, 1)
            for tt in range(3):
                n = rows_of[tt]
                pe.wait_ge(h_in, tt + 1)
                for c in range(4):
                    if 4 * tt + c >= 2:
                        pe.wait_ge(h_t_in, 4 * tt + c - 1)
                    for j in range(4):
                        kt = 4 * c + j
                        mm = pe.transpose(bank[6 + c % 2][:, P * j:P * j + n], h_nat[0:n, tt, P * kt:P * kt + P], ident[0:n, 0:n])
                    mm.then_inc(h_turned, 1)
            pe.wait_ge(h_t_in, 12)
            pe.wait_ge(sub_in, 16)

            def score(m):
                pe.wait_ge(q_in, m + 1)
                if m >= 2:
                    pe.wait_ge(s_in, 3 * (m - 1))
                for tt in range(3):
                    n = rows_of[tt]
                    mm = pe.matmul(bank[2 + m % 2][0:n, P * tt:P * tt + P], q_t[:, m, P * tt:P * tt + n], sub_keys[:, m % 2, :],
                                   start=True, stop=True, skip_group_check=True)
                mm.then_inc(s_mm, 1)

            for m in range(16):
                w = arrived("wq", m // 8, m % 8)
                if m >= 2:
                    pe.wait_ge(q_in, m - 1)
                for kt in range(KT):
                    mm = pe.matmul(bank[m % 2][:, 0:T], w[:, P * kt:P * kt + P], h_t[:, kt, :], start=(kt == 0), stop=(kt == KT - 1))
                mm.then_inc(item_used, 1)
                if m:
                    score(m - 1)
            score(15)
            pe.wait_ge(s_in, 48)
            pe.wait_ge(chosen, 1)
            pe.sem_inc(v_used, 4)

            def value_rows(r, tt, it_r):
                n = rows_of[tt]
                banks = bank[4 * (tt % 2):4 * (tt % 2) + 4]
                for j in range(16):
                    pe.wait_ge(v_full[j % 4], 16 * (4 * r + j // 4 + 1))
                    pe.wait_ge(diag_in, 32 + 16 * r + j + 1)
                    for c in range(4):
                        mm = pe.matmul(banks[c][0:n, :], diag[j % 4][:, 0:n], v_ring[j % 4][:, 512 * c:512 * c + 512], start=False, stop=True,
                                       skip_group_check=True)
                    mm.then_inc(v_used, 1)

            def open_banks(tt):
                n = rows_of[tt]
                for c in range(4):
                    pe.matmul(bank[4 * (tt % 2) + c][0:n, :], zeros[:, 0:n], h_nat[:, 0, 512 * c:512 * c + 512] if tt == 0 else norm[:, 2, 512 * c:512 * c + 512],
                              start=True, stop=True, skip_group_check=True)

            for tt in range(2):
                open_banks(tt)
                with pe.Fori(4 * tt, 4 * tt + 4) as it:
                    for par in range(2):
                        value_rows(2 * it + par, tt, None)
            pe.wait_ge(tile_out, 1)
            open_banks(2)
            for par in range(2):
                value_rows(16 + par, 2, None)

        @block.vector
        def _(dve):
            ch = Chain(dve, dve_step)
            dve.wait_ge(gate_exp, 2)
            ch.do(dve.tensor_scalar_add(gate_tmp, gate_tmp, 1.0))
            ch.do(dve.tensor_scalar_add(smp_gate_tok[0:NSMP], smp_gate_tok[0:NSMP], 1.0))
            ch.do(dve.reciprocal(prompt_gate, gate_tmp))
            dve.reciprocal(smp_gate_tok[0:NSMP], smp_gate_tok[0:NSMP]).then_inc(gate_tok, 1)
            dve.wait_ge(consts_in, 16)
            dve.wait_ge(rope_in, 16)
            for n, m in enumerate(ROPED):
                dve.wait_ge(swapped, n + 1)
                ch.do(dve.tensor_tensor(rope_tmp[:, n % 2], bank[2 + n % 2][:, 0:T], rope[:, 1, :], ALU.mult))
                ch.do(dve.tensor_tensor(proj[:, m, :], proj[:, m, :], rope[:, 0, :], ALU.mult))
                ch.tell(dve.tensor_tensor(proj[:, m, :], proj[:, m, :], rope_tmp[:, n % 2], ALU.add), roped, n + 1)
            dve.wait_ge(gate_rows, 1)
            for h in range(2):
                own = gate_tmp[:, h].rearrange("p (h b) -> p h b", b=3)
                ch.do(dve.tensor_tensor(own, bank[1][:, 24 * h:24 * h + 24].rearrange("p (h b) -> p h b", b=3),
                                        const["head_row"][:, :, None].to_broadcast([P, NH, 3]), ALU.mult))
                ch.do(dve.tensor_reduce(smp_gate[:, h], gate_tmp[:, h].rearrange("p (h b) -> p b h", b=3), AX.X, ALU.add))
            dve.wait_ge(v_turned, 1)
            ch.do(dve.memset(v_new, 0.0))
            for n in range(3):
                dve.tensor_copy(v_new[0:NSMP, 4 * n:4 * n + 4, :],
                                bank[5 + n][0:NSMP, :].rearrange("p (a b) -> p a b", a=4)).then_inc(v_new_in, 1)
            dve.wait_ge(bias_ready, 1)
            dve.tensor_copy(pe_bias, bank[4][:, 0:2]).then_inc(bias_sb, 1)
            dve.wait_ge(bias_sb, 1)
            ch.do(dve.memset(h_cmp[0], 0.0))
            ch.do(dve.memset(h_cmp[1], 0.0))
            dve.sem_inc(ab_free, 2)

            def gelu(x, u, e, h, arg, exp, out, done):
                ch.do(dve.tensor_tensor(u, x, x, ALU.mult))
                ch.do(dve.tensor_scalar(u, u, GELU_A, 1.0, ALU.mult, ALU.add))
                ch.tell(dve.tensor_tensor(u, u, x, ALU.mult), arg, done)
                dve.wait_ge(exp, done)
                ch.do(dve.tensor_scalar_add(e, e, 1.0))
                ch.do(dve.reciprocal(e, e))
                ch.tell(dve.tensor_tensor(h, x, e, ALU.mult), out, done)

            with ch.rounds(4, 28) as it:
                for st in range(4):
                    kv = st % 2
                    ab = bank[2 + kv]
                    a = ab[:, 0:256].rearrange("p (q g j) -> p q g j", g=NG, j=8)
                    b = x_cmp.rearrange("p (q g j) -> p q g j", g=NG, j=8)
                    h = h_cmp[kv].rearrange("p (g q j) -> p q g j", g=NG, j=8)
                    dve.wait_ge(item_used, stream.used("cmp", it, 2 * st + 1))
                    dve.wait_ge(cmp_mm, 4 * it + st + 1)
                    ch.do(dve.tensor_copy(x_cmp, ab[:, 256:512]))
                    ch.do(dve.tensor_tensor(h[:, :, :, 0:7], a[:, :, :, 0:7], b[:, :, :, 1:8], ALU.add))
                    ch.tell(dve.tensor_tensor(h[:, 0:15, :, 7], a[:, 0:15, :, 7], b[:, 1:16, :, 0], ALU.add), ab_free,
                            4 * it + st + 3)
                    ch.do(dve.tensor_scalar(x_cmp, h_cmp[kv], pe_bias[:, kv:kv + 1], None, ALU.add))
                    gelu(x_cmp, u_cmp, e_cmp, h_cmp[kv], gelu_arg, gelu_exp, gelu_out, 4 * it + st + 1)
            dve.wait_ge(cmp_mm, 2 + 16)
            ch.do(dve.memset(h_cmp[0][:, 0:64], 0.0))
            dve.wait_ge(pc_ab, 1)
            for kv in range(2):
                at = 64 * kv
                a = bank[6][:, at:at + 32].rearrange("p (g c) -> p g c", g=NG)
                b = x_cmp[:, 0:32].rearrange("p (g c) -> p g c", g=NG)
                h = h_cmp[0][:, 32 * kv:32 * kv + 32].rearrange("p (g c) -> p g c", g=NG)
                ch.do(dve.tensor_copy(x_cmp[:, 0:32], bank[6][:, at + 32:at + 64]))
                ch.do(dve.tensor_tensor(h[:, :, 0:NCP], a[:, :, 0:NCP], b[:, :, 1:NCP + 1], ALU.add))
            for kv in range(2):
                ch.do(dve.tensor_scalar(x_cmp[:, 32 * kv:32 * kv + 32], h_cmp[0][:, 32 * kv:32 * kv + 32], pe_bias[:, kv:kv + 1], None, ALU.add))
            gelu(x_cmp[:, 0:64], u_cmp[:, 0:64], e_cmp[:, 0:64], h_cmp[0][:, 0:64], gelu_arg, gelu_exp, gelu_out, 17)
            dve.wait_ge(pc_mm, 1)
            ch.tell(dve.memset(p_slc_t[:, 16], 0.0), padded, 1)
            ch.do(dve.memset(q_pad, 0.0))
            for g in range(NG):
                dst = q_pad[:, :, g, 16 * g:16 * g + 16].rearrange("p b (h t) -> p b h t", t=NT)
                src = proj[:, QB + HPG * g:QB + HPG * g + HPG, PTOK:T].rearrange("p h (b t) -> p b h t", t=NT)
                ins = dve.tensor_copy(dst, src)
                ch.do(ins) if g == 0 else ch.tell(ins, q_pad_in, 1)
            for h in range(2):
                dve.wait_ge(cmp_scored, h + 1)
                ch.do(dve.tensor_reduce(soft[:, h:h + 1], bank[h][:, 0:NCS], AX.X, ALU.max))
                ch.tell(dve.tensor_scalar(soft[:, 2 + h:3 + h], soft[:, h:h + 1], -SCALE, None, ALU.mult), cmp_neg, h + 1)
            dve.wait_ge(cmp_exp, 2)
            ch.do(dve.tensor_scalar_max(soft[:, 4:6], soft[:, 4:6], 1e-30))
            ch.do(dve.reciprocal(soft[:, 4:6], soft[:, 4:6]))
            for h in range(2):
                ch.tell(dve.tensor_scalar(s_cmp[:, h, 0:NCS], s_cmp[:, h, 0:NCS], soft[:, 4 + h:5 + h], None, ALU.mult), cmp_p, h + 1)
            dve.wait_ge(imp_ready, 1)
            ch.tell(dve.tensor_copy(imp, bank[3][:, 0:2 * NSEL].rearrange("p (h n) -> p h n", h=2)), imp_in, 1)
            ch.do(dve.memset(imp[:, :, 0:1], FORCE))
            ch.do(dve.memset(imp[:, :, NSEL - 2:NSEL], FORCE))
            for h in range(2):
                other = imp[:, h, None, :].to_broadcast([P, NSEL, NSEL])
                own = imp[:, h, :, None].to_broadcast([P, NSEL, NSEL])
                ch.do(dve.tensor_tensor(above, other, own, ALU.is_gt))
                ch.do(dve.tensor_tensor(ties, other, own, ALU.is_equal))
                ch.do(dve.tensor_tensor(ties, ties, const["lower"].rearrange("p (a b) -> p a b", a=NSEL), ALU.mult))
                ch.do(dve.tensor_tensor(above, above, ties, ALU.add))
                ch.do(dve.tensor_reduce(rank[:, h], above, AX.X, ALU.add))
            ch.do(dve.tensor_scalar(sel_add, rank, NTOP - 0.5, NEG, ALU.is_gt, ALU.mult))
            for h in range(2):
                dve.wait_ge(cmp_sum, 1)
                ch.tell(dve.tensor_scalar(s_cmp[:, h, 0:NCS], s_cmp[:, h, 0:NCS], smp_gate[:, h, 0:1], None, ALU.mult), cmp_pg, h + 1)

            def slc_out(h):
                for ph in range(2):
                    dve.wait_ge(item_used, stream.used("ks", h, 4 * ph + 3))
                    for c in range(2):
                        at = 1024 * ph + 512 * c
                        add = sel_add[:, h, at // SEL_BLOCK:at // SEL_BLOCK + 8, None].to_broadcast([P, 8, SEL_BLOCK])
                        ch.tell(dve.tensor_tensor(s_slc[:, h, at:at + 512].rearrange("p (a b) -> p a b", a=8),
                                                  bank[4 + 2 * ph + c][:, :].rearrange("p (a b) -> p a b", a=8), add, ALU.add),
                                slc_evac, 4 * h + 2 * ph + c + 1)

            slc_out(0)
            slc_out(1)
            new_add = const["new_add"].rearrange("p (h n) -> p h n", h=2)
            dve.wait_ge(new_scored, 1)
            for h in range(2):
                for n, s in enumerate((s_slc[:, h, PAST:], s_win[:, h, WIN:])):
                    ch.tell(dve.tensor_tensor(s, bank[3][:, 64 * n + 32 * h:64 * n + 32 * h + 32], new_add[:, h], ALU.add),
                            new_evac, 2 * h + n + 1)
            ch.tell(dve.memset(p_win_t[:, 4], 0.0), padded, 2)
            for h in range(2):
                dve.wait_ge(item_used, stream.used("kw", 0, 2 * h + 1))
                ch.tell(dve.tensor_copy(s_win[:, h, 4:WIN], bank[h][:, 4:WIN]), win_evac, 2 * h + 1)
                ch.tell(dve.tensor_tensor(s_win[:, h, 0:4], bank[h][:, 0:4], const["win_add"], ALU.add), win_evac, 2 * h + 2)
            for h in range(2):
                for n, s in enumerate((s_slc, s_win)):
                    ch.do(dve.tensor_reduce(soft[:, 16:17], s[:, h], AX.X, ALU.max))
                    ch.tell(dve.tensor_scalar(soft[:, 8 + 2 * n + h:9 + 2 * n + h], soft[:, 16:17], -SCALE, None, ALU.mult),
                            soft_neg, 2 * h + n + 1)
            for h in range(2):
                for n, s in enumerate((s_slc, s_win)):
                    dve.wait_ge(soft_exp, 2 * h + n + 1)
                    f = soft[:, 12 + 2 * n + h:13 + 2 * n + h]
                    ch.do(dve.tensor_scalar_max(f, f, 1e-30))
                    ch.do(dve.reciprocal(f, f))
                    ch.do(dve.tensor_tensor(f, f, smp_gate[:, h, 1 + n:2 + n], ALU.mult))
                    ch.tell(dve.tensor_scalar(s[:, h], s[:, h], f, None, ALU.mult), soft_p, 2 * h + n + 1)
            dve.wait_ge(item_used, stream.used("vw", 0, 3))
            ch.tell(dve.tensor_copy(o_nsa, bank[7][:, :].rearrange("p (h n) -> p h n", h=2)), o_nsa_in, 1)
            dve.wait_ge(o_nsa_t, 1)
            for h in range(2):
                for g in range(NG):
                    src = bank[h][:, P * g:P * g + P].rearrange("p (b g h t) -> p g h b t", b=4, g=NG, h=HPG)[:, g]
                    dst = mix_t[:, NH + HPG * g:NH + HPG * g + HPG, PTOK + 16 * h:PTOK + 16 * h + 16].rearrange("p h (b t) -> p h b t", t=NT)
                    ch.tell(dve.tensor_copy(dst, src), mix_nsa, 2 * h + g + 1)

            causal = const["causal"]
            cmp_add = const["cmp_add"].rearrange("p (q n) -> p q n", q=2)
            cmp_mul = const["cmp_mul"].rearrange("p (q n) -> p q n", q=2)
            for u in range(4):
                qt, g = u // 2, u % 2
                nk = P * (qt + 1)
                dve.wait_ge(pb_scored, u + 1)
                for hp in range(HPG):
                    src = bank[hp][:, :].rearrange("p (r k) -> p r k", r=2)[:, :, 0:nk]
                    ch.do(dve.tensor_tensor(s_pr[:, hp, :, 0:nk], src, causal[:, None, 2 * P - nk:].to_broadcast([P, 2, nk]), ALU.add))
                src = bank[4][:, 0:64].rearrange("p (h n) -> p h n", n=16)[:, :, 0:NCP]
                ch.do(dve.tensor_tensor(s_prc[:, :, 0:NCP], src, cmp_add[:, qt, None, :].to_broadcast([P, HPG, NCP]), ALU.add))
                ch.do(dve.tensor_reduce(pr_max[:, 0:8].rearrange("p (a b) -> p a b", a=4), s_pr[:, :, :, 0:nk], AX.X, ALU.max))
                ch.tell(dve.tensor_scalar(pr_max[:, 0:8], pr_max[:, 0:8], -SCALE, None, ALU.mult), pb_neg, u + 1)
                ch.do(dve.tensor_reduce(pr_max[:, 8:12], s_prc[:, :, 0:NCP], AX.X, ALU.max))
                ch.tell(dve.tensor_tensor(s_prc[:, :, 0:NCP], s_prc[:, :, 0:NCP], pr_max[:, 8:12, None].to_broadcast([P, HPG, NCP]), ALU.subtract),
                        pb_negc, u + 1)
                dve.wait_ge(pb_exp, 9 * u + 9)
                ch.do(dve.tensor_tensor(s_prc[:, :, 0:NCP], s_prc[:, :, 0:NCP], cmp_mul[:, qt, None, :].to_broadcast([P, HPG, NCP]), ALU.mult))
                ch.do(dve.tensor_reduce(pr_sum[:, 8:12], s_prc[:, :, 0:NCP], AX.X, ALU.add))
                ch.do(dve.tensor_scalar_max(pr_sum, pr_sum, 1e-30))
                ch.do(dve.reciprocal(pr_sum, pr_sum))
                gate = prompt_gate[:, qt, 12 * g:12 * g + 12].rearrange("p (h b) -> p h b", b=3)
                f = pr_sum[:, 0:8].rearrange("p (h b) -> p h b", b=2)
                ch.do(dve.tensor_tensor(f, f, gate[:, :, 1:3], ALU.mult))
                ch.do(dve.tensor_tensor(pr_sum[:, 8:12], pr_sum[:, 8:12], gate[:, :, 0], ALU.mult))
                fb = pr_sum[:, 0:8, None].to_broadcast([P, 8, nk])
                sv = s_pr.rearrange("p h b n -> p (h b) n")[:, :, 0:nk]
                ch.tell(dve.tensor_tensor(sv, sv, fb, ALU.mult), pb_p, 2 * u + 1)
                ch.tell(dve.tensor_tensor(s_prc[:, :, 0:NCP], s_prc[:, :, 0:NCP], pr_sum[:, 8:12, None].to_broadcast([P, HPG, NCP]), ALU.mult),
                        pb_p, 2 * u + 2)
                dve.wait_ge(pb_pv, u + 1)
                dve.tensor_copy(mix_t[:, NH + HPG * g:NH + HPG * g + HPG, P * qt:P * qt + P],
                                bank[5 + u % 2][:, :].rearrange("p (a b) -> p a b", a=4)).then_inc(pb_out, 1)

            dve.wait_ge(pb_out, 4)
            strict = const["strict"][:, None, None, :].to_broadcast([P, 4, 2, P])

            def diagonal(t, u):
                return t[:, 4 * u:4 * u + 4].rearrange("p h (a n) -> p h a n", a=3)[:, :, 0:3:2, :]

            for u in range(2):
                hs = slice(4 * u, 4 * u + 4)
                dve.wait_ge(pa_z_in, 4 * u + 4)
                ch.tell(dve.scalar_tensor_tensor(out=e_pr[:, hs], in0=z_pr[:, hs], scalar=-1.0, in1=z_pr[:, hs], op0=ALU.mult, op1=ALU.min),
                        pa_neg, u + 1)
            for u in range(2):
                hs = slice(4 * u, 4 * u + 4)
                dve.wait_ge(pa_log, u + 1)
                ch.do(dve.scalar_tensor_tensor(out=sp_pr[:, hs], in0=z_pr[:, hs], scalar=0.0, in1=e_pr[:, hs], op0=ALU.max, op1=ALU.add))
                ch.tell(dve.tensor_tensor(diagonal(sp_pr, u), diagonal(sp_pr, u), strict, ALU.mult), pa_sp, u + 1)
            for h in range(NH):
                dve.wait_ge(pa_g, h + 1)
                ch.tell(dve.tensor_tensor(z_pr[:, h], z_pr[:, h], bank[h][:, 0:3 * P], ALU.subtract), pa_arg, h + 1)
            for u in range(2):
                dve.wait_ge(pa_exp, u + 1)
                ch.tell(dve.tensor_tensor(diagonal(z_pr, u), diagonal(z_pr, u), strict, ALU.mult), pa_w, u + 1)
            for h in range(NH):
                dve.wait_ge(pa_pv, h + 1)
                dve.tensor_copy(mix_t[:, h, 0:NPROMPT], bank[h][:, 0:NPROMPT]).then_inc(pa_out, 1)

            dve.wait_ge(mix_nsa, 4)
            ch.do(dve.memset(sp_new, 0.0))
            dve.wait_ge(sn_z_in, 1)
            zn, en, sn = z_new[0:NSMP], e_new[0:NSMP], sp_new[0:NSMP]
            seen = const["new_sb"][0:NSMP, None, :].to_broadcast([NSMP, NH, NSMP])
            ch.tell(dve.scalar_tensor_tensor(out=en, in0=zn, scalar=-1.0, in1=zn, op0=ALU.mult, op1=ALU.min), sn_neg, 1)
            dve.wait_ge(sn_log, 1)
            ch.do(dve.scalar_tensor_tensor(out=sn, in0=zn, scalar=0.0, in1=en, op0=ALU.max, op1=ALU.add))
            ch.tell(dve.tensor_tensor(sn, sn, seen, ALU.mult), sn_sp, 1)
            dve.wait_ge(sn_g, 1)
            ch.tell(dve.tensor_tensor(zn, zn, bank[1][0:NSMP, 0:256].rearrange("p (h n) -> p h n", h=NH), ALU.subtract), sn_arg, 1)
            dve.wait_ge(sn_exp, 1)
            ch.tell(dve.tensor_tensor(zn, zn, seen, ALU.mult), sn_w, 1)
            dve.wait_ge(sn_pv, 1)
            ch.tell(dve.tensor_copy(mix_t[:, 0:NH, PTOK:T], bank[2][:, 0:256].rearrange("p (h n) -> p h n", h=NH)), sn_out, 1)
            dve.sem_inc(z_t_in, 2)
            ch.do(dve.memset(q_pad_a, 0.0))
            for half in range(2):
                if half:
                    dve.wait_ge(item_used, stream.used("ak", 3, 7))
                for h in range(NH):
                    src = proj[:, QA + h, PTOK + 16 * half:PTOK + 16 * half + 16].rearrange("p (b t) -> p b t", t=NT)
                    ins = dve.tensor_copy(q_pad_a[:, :, h, NT * h:NT * h + NT], src)
                    ch.do(ins) if h < NH - 1 else ch.tell(ins, q_pad_a_in, half + 1)
                with dve.Fori(2 * half, 2 * half + 2) as it:
                    for k in range(2):
                        dve.wait_ge(z_turned, 2 * it + k + 1)
                        dst = z_t.rearrange("p a q r -> p (a q) r")[:, bass.ds(8 * it + 4 * k, 4), :]
                        ch.tell(dve.tensor_copy(dst, bank[5 + k][:, :].rearrange("p (q r) -> p q r", q=4)), z_t_in, 2 * it + k + 3)
                z, e, s, lt = z_t[:, half], e_t[:, half], sp_t[:, half], later[:, half]
                ch.tell(dve.scalar_tensor_tensor(out=e, in0=z, scalar=-1.0, in1=z, op0=ALU.mult, op1=ALU.min), sa_neg, half + 1)
                dve.wait_ge(sa_log, half + 1)
                ch.do(dve.scalar_tensor_tensor(out=s, in0=z, scalar=0.0, in1=e, op0=ALU.max, op1=ALU.add))
                ch.do(dve.tensor_copy(lt[:, NPAGE - 1].rearrange("p (b h t) -> p h b t", b=4, h=NH),
                                      sp_new[:, :, 16 * half:16 * half + 16].rearrange("p h (b t) -> p h b t", t=NT)))
                for q in range(NPAGE - 2, -1, -1):
                    ins = dve.tensor_tensor(lt[:, q], lt[:, q + 1], s[:, q + 1], ALU.add)
                    ch.do(ins) if q else ch.tell(ins, sa_later, half + 1)
            for n in range(8):
                dve.wait_ge(sa_g, n + 1)
                zz = z_t[:, n // 4, 4 * (n % 4):4 * (n % 4) + 4]
                dve.tensor_tensor(zz, zz, bank[4 + n % 4][:, :].rearrange("p (q r) -> p q r", q=4), ALU.subtract).then_inc(sa_arg, 1)
            for half in range(2):
                for h in range(NH):
                    if h % 4 == 0:
                        dve.wait_ge(o_a_t, 2 * half + h // 4 + 1)
                    rows = mix_t[:, h, PTOK + 16 * half:PTOK + 16 * half + 16].rearrange("p (b t) -> p b t", t=NT)
                    own = bank[4 + 2 * half + h // 4][:, P * (h % 4):P * (h % 4) + P].rearrange("p (b h t) -> p b h t", b=4, h=NH)[:, :, h]
                    dve.tensor_tensor(rows, rows, own, ALU.add).then_inc(mix_a, 1)

            dve.wait_ge(tok_in, 32)
            for n in range(4):
                dve.wait_ge(item_used, stream.used("wo", n // 2, 4 * (n % 2) + 3))
                for tt in range(3):
                    r = rows_of[tt]
                    hh = h_nat[0:r, tt, 512 * n:512 * n + 512]
                    ch.tell(dve.scalar_tensor_tensor(out=hh, in0=hh, scalar=ALPHA, in1=bank[3 * (n % 2) + tt][0:r, :], op0=ALU.mult, op1=ALU.add,
                                                     accum_out=ln[0:r, 20 + 4 * tt + n:21 + 4 * tt + n]), wo_evac, 3 * n + tt + 1)
            dve.wait_ge(norm_in, 64)

            def norm_dve(n, tt, gain, c, done, count):
                x = h_nat[0:n, tt, :]
                ch.do(dve.tensor_reduce(ln[0:n, 4 + tt:5 + tt], ln[0:n, 20 + 4 * tt:24 + 4 * tt], AX.X, ALU.add))
                ch.tell(dve.tensor_scalar(ln[0:n, 8 + tt:9 + tt], ln[0:n, 4 + tt:5 + tt], -1.0 / DM, None, ALU.mult), ln_mu, c)
                dve.wait_ge(ln_sq, c)
                v, sd, mu = ln[0:n, 12 + tt:13 + tt], ln[0:n, 16 + tt:17 + tt], ln[0:n, 8 + tt:9 + tt]
                ch.tell(dve.tensor_scalar(v, v, 1.0 / DM, EPS, ALU.mult, ALU.add), ln_var, c)
                dve.wait_ge(ln_sd, c)
                ch.do(dve.reciprocal(sd, sd))
                ch.do(dve.tensor_scalar(x, x, mu, sd, ALU.add, ALU.mult))
                ch.do(dve.tensor_tensor(x, x, norm[0:n, gain, :], ALU.mult))
                ch.tell(dve.tensor_tensor(x, x, norm[0:n, gain + 1, :], ALU.add), done, count)

            for tt in range(3):
                norm_dve(rows_of[tt], tt, 0, tt + 1, h_in, tt + 1)

            def top16(n, values, s, i):
                ch.do(dve.max(s[:, 0:8], values))
                ch.do(dve.max_index(i[:, 0:8], s[:, 0:8], values))
                w = work[0:n, 0:values.shape[-1]]
                ch.do(dve.match_replace(w, s[:, 0:8], values, -3.0e38))
                ch.do(dve.max(s[:, 8:16], w))
                ch.do(dve.max_index(i[:, 8:16], s[:, 8:16], w))

            def head_topk(tt, h):
                n = rows_of[tt]
                for m in (2 * h, 2 * h + 1):
                    dve.wait_ge(s_in, 3 * m + tt + 1)
                    top16(n, s_key[tt][0:n, m, :], top_s[0:n, tt, m, :], top_i[0:n, tt, m, :])
                ch.do(dve.tensor_tensor(cand[0:n].rearrange("p (a b) -> p a b", a=16),
                                        top_s[0:n, tt, 2 * h, :, None].to_broadcast([n, 16, 16]),
                                        top_s[0:n, tt, 2 * h + 1, None, :].to_broadcast([n, 16, 16]), ALU.add))
                top16(n, cand[0:n], best_s[0:n, tt, 16 * h:16 * h + 16], best_j[0:n, tt, 16 * h:16 * h + 16])

            def experts_of(tt):
                n = rows_of[tt]
                bs = best_s[0:n, tt].rearrange("p (h k) -> p h k", h=NH)
                ch.do(dve.tensor_copy(f_a[0:n, 0:8], bs[:, :, 0]))
                ch.tell(dve.tensor_tensor(bs, bs, f_a[0:n, 0:8, None].to_broadcast([n, NH, 16]), ALU.subtract), gate_arg, tt + 1)
                ch.do(dve.tensor_single_scalar(j_a[0:n], best_j[0:n, tt], 4, ALU.logical_shift_right))
                ch.do(dve.tensor_single_scalar(j_b[0:n], best_j[0:n, tt], 15, ALU.bitwise_and))
                ch.do(dve.tensor_copy(f_a[0:n], j_a[0:n]))
                ch.do(dve.tensor_copy(f_b[0:n], j_b[0:n]))
                ch.do(dve.tensor_copy(top_f[0:n], top_i[0:n, tt]))
                for f, i, c in ((f_a, i_a, 0), (f_b, i_b, 1)):
                    oh = one_hot[0:n]
                    ch.do(dve.tensor_tensor(oh, f[0:n, :, None].to_broadcast([n, P, 16]),
                                            const["iota16"][0:n, None, :].to_broadcast([n, P, 16]), ALU.is_equal))
                    oh4 = oh.rearrange("p (h k) a -> p h k a", h=NH)
                    keys = top_f[0:n].rearrange("p (h c) a -> p h c a", c=2)[:, :, c, None, :].to_broadcast([n, NH, 16, 16])
                    ch.do(dve.tensor_tensor(oh4, oh4, keys, ALU.mult))
                    ch.do(dve.tensor_reduce(i[0:n], oh, AX.X, ALU.add))
                ex = expert[:, P * tt:P * tt + P] if tt < 2 else expert_s[0:n]
                ins = dve.scalar_tensor_tensor(out=ex, in0=i_a[0:n], scalar=float(P), in1=i_b[0:n], op0=ALU.mult, op1=ALU.add)
                ch.tell(ins, chosen, tt + 1) if tt < 2 else ch.do(ins)

            def gates_of(tt):
                n = rows_of[tt]
                bs = best_s[0:n, tt].rearrange("p (h k) -> p h k", h=NH)
                gt = peer_gate[:, P * tt:P * tt + P] if tt < 2 else gate_s[0:n]
                dve.wait_ge(gate_e, tt + 1)
                ch.do(dve.tensor_reduce(soft_sum[0:n, 0:8], bs, AX.X, ALU.add))
                ch.do(dve.reciprocal(soft_sum[0:n, 0:8], soft_sum[0:n, 0:8]))
                ch.do(dve.tensor_tensor(gt.rearrange("p (h k) -> p h k", h=NH), bs, soft_sum[0:n, 0:8, None].to_broadcast([n, NH, 16]), ALU.mult))

            def fold_samples():
                for q in range(4):
                    r = slice(32 * q, 32 * q + 32)
                    ch.do(dve.tensor_copy(expert[r, 256:288], expert_s[0:NSMP, 32 * q:32 * q + 32]))
                    ch.do(dve.tensor_copy(peer_gate[r, 256:288], gate_s[0:NSMP, 32 * q:32 * q + 32]))
                    ins = dve.tensor_copy(h_rep[r], h_nat[0:NSMP, 2, :])
                    ch.do(ins) if q < 3 else ch.tell(ins, chosen, 3)

            ch.do(dve.memset(zeros, 0.0))
            for h in range(NH):
                head_topk(0, h)
            dve.wait_ge(s_mm, 16)
            experts_of(0)
            gates_of(0)

            dve.sem_inc(u_used, 4)

            def slots(r, par, x, between={}, experts_at=None):
                for j in range(16):
                    dve.wait_ge(u_full[j % 4], 16 * (4 * r + j // 4 + 1))
                    dve.tensor_tensor_reduce(out=u_ring[j % 4], in0=u_ring[j % 4], in1=x, scale=1.0, scalar=0.0, op0=ALU.mult, op1=ALU.add,
                                             accum_out=act16[:, par, j:j + 1]).then_inc(u_used, 1)
                    for tt, h in between.get(j, ()):
                        head_topk(tt, h)
                    if j == 3 and experts_at is not None:
                        experts_of(experts_at)
                dve.wait_ge(u_used, 4 + 16 * r + 16)
                a = act16[:, par]
                ch.do(dve.tensor_tensor(u16, a, a, ALU.mult))
                ch.do(dve.tensor_scalar(u16, u16, GELU_A, 1.0, ALU.mult, ALU.add))
                ch.tell(dve.tensor_tensor(u16, u16, a, ALU.mult), act_arg, r + 1)
                ch.do(dve.tensor_tensor(a, a, peer_gate[:, bass.ds(16 * r, 16)], ALU.mult))
                dve.wait_ge(act_e, r + 1)
                ch.do(dve.tensor_scalar_add(e16, e16, 1.0))
                ch.do(dve.reciprocal(e16, e16))
                dve.wait_ge(diag_in, 16 * r + 16)
                ch.tell(dve.tensor_tensor(w16[:, par], a, e16, ALU.mult), w_ready, r + 1)

            def finish(tt, c):
                n = rows_of[tt]
                for q in range(4):
                    hh = h_nat[0:n, tt, 512 * q:512 * q + 512]
                    ins = dve.scalar_tensor_tensor(out=hh, in0=hh, scalar=ALPHA, in1=bank[4 * (tt % 2) + q][0:n, :], op0=ALU.mult, op1=ALU.add,
                                                   accum_out=ln[0:n, 20 + 4 * tt + q:21 + 4 * tt + q])
                    ch.do(ins) if q < 3 else ch.tell(ins, tile_out, tt + 1)
                norm_dve(n, tt, 2, c, y_ready, tt + 1)

            for r in range(8):
                slots(r, r % 2, h_nat[:, 0, :], TOPK_IN.get(r, {}), GATES_IN.get(r))
                if r in GATES_IN:
                    gates_of(GATES_IN[r])
            fold_samples()
            with ch.rounds(4, 10) as it:
                for par in range(2):
                    slots(8 + 2 * it + par, par, h_nat[:, 1, :])
            slots(16, 0, h_rep)
            dve.wait_ge(v_used, 4 + 16 * 8)
            finish(0, 4)
            slots(17, 1, h_rep)
            dve.wait_ge(v_used, 4 + 16 * 16)
            finish(1, 5)
            dve.wait_ge(v_used, 4 + 16 * 18)
            finish(2, 6)

        @block.gpsimd
        def _(pool):
            pool.wait_ge(consts_in, 16)
            pool.wait_ge(o_a_t, 4)
            pool.wait_ge(mix_a, 16)
            pool.dma_start(h_nat[:, 0:2, :], dram["tokens"][0:NPROMPT].rearrange("(t p) d -> p t d", p=P)).then_inc(tok_in, 16)
            pool.dma_start(h_nat[0:NSMP, 2, :], dram["tokens"][NPROMPT:T]).then_inc(tok_in, 16)
            for i in range(4):
                pool.dma_start(norm[:, i, :], dram["norms"][i:i + 1, :].to_broadcast([P, DM])).then_inc(norm_in, 16)
            pool.dma_start(sub_keys, dram["sub_keys"]).then_inc(sub_in, 16)
            pool.wait_ge(chosen, 1)
            pool.wait_ge(item_used, RING + stream.total)

            def hold(signal, value):
                pool.wait_ge(signal, value)
                pool.sem_inc(held, 1)

            def indices(dst, r, par, n):
                pool.tensor_copy(dst[:, par], expert[:, bass.ds(16 * r, 16)]).then_inc(idx_in, 1)
                hold(idx_in, n)

            def gather(table, rows, idx, full, used, r, j):
                hold(used, 16 * r + j + 1)
                pool.indirect_dma_start(rows[j % 4], None, dram[table], bass.IndirectOffsetOnAxis(ap=idx, axis=0)).then_inc(full[j % 4], 16)

            def u_of(r, par, j):
                gather("peer_u", u_ring, idx_u[:, par, j:j + 1], u_full, u_used, r, j)

            def v_of(r, par, j):
                gather("peer_v", v_ring, idx_v[:, par, j:j + 1], v_full, v_used, r, j)

            def both(r, par):
                indices(idx_u, r, par, 2 * r)
                indices(idx_v, r - 1, 1 - par, 2 * r + 1)
                for j in range(16):
                    u_of(r, par, j)
                    v_of(r - 1, 1 - par, j)

            indices(idx_u, 0, 0, 1)
            for j in range(16):
                u_of(0, 0, j)
            both(1, 1)
            for tt in range(2):
                with pool.Fori(1 + 3 * tt, 4 + 4 * tt) as it:
                    for par in range(2):
                        both(2 * it + par, par)
                pool.wait_ge(chosen, tt + 2)
            for par in range(2):
                both(16 + par, par)
            indices(idx_v, 17, 1, 36)
            for j in range(16):
                v_of(17, 1, j)


def kernel(**inputs):
    import numpy as _np
    import concourse.bacc as _bacc
    from concourse import mybir as _mybir
    from concourse.bass_utils import run_bass_kernel_spmd as _run

    x = {k: _np.asarray(v) for k, v in inputs.items()}
    w = x["w_in"][0]
    n_pool = x["cache_a"].shape[1]
    tokens = _np.concatenate([x["x_prompt"].reshape(NPROMPT, DM), x["x_sample"].reshape(NSMP, DM)])
    by_tile = lambda a: a.reshape(KT, P, -1).transpose(1, 0, 2)
    ca, cn, sw = x["cache_a"][0], x["cache_nsa"][0], x["state_win"][0]
    arrays = {
        "tokens": tokens,
        "tokens_t": by_tile(tokens.T),
        "w_in": w[:, :NM * P].reshape(KT, P, NM, P).transpose(2, 1, 0, 3),
        "w_gate": by_tile(w[:, NM * P:]),
        "rope": rope_tables(),
        "consts": constants(),
        "pages": x["page_table"].reshape(1, -1),
        "a_k": ca[:, :, 0].transpose(0, 3, 2, 1).reshape(n_pool, P, NH * P),
        "a_v": ca[:, :, 1].reshape(n_pool, P, NH * P),
        "nsa_t": cn[:, :, 0:3].transpose(0, 2, 4, 3, 1).reshape(n_pool, 3, P, NG * P),
        "nsa_v": cn[:, :, 3].reshape(n_pool, P, NG * P),
        "win_k": sw[:, :, 0].transpose(0, 3, 2, 1).reshape(NB // 2, 2, P, NG * WIN).transpose(0, 2, 1, 3),
        "win_v": sw[:, :, 1].reshape(NB // 2, 2, 4, P, NG * P).transpose(0, 3, 1, 2, 4),
        "cmp_w1": _np.stack([x["cmp_w1_k"][0], x["cmp_w1_v"][0]]).transpose(2, 0, 1, 3),
        "cmp_w2": _np.stack([x["cmp_w2_k"][0], x["cmp_w2_v"][0]]).transpose(1, 0, 2),
        "cmp_pe": _np.stack([x["cmp_pe_k"][0], x["cmp_pe_v"][0]]).transpose(2, 0, 1),
        "w_out": x["w_out"][0].reshape(4, 4, P, 4, 512).transpose(3, 0, 2, 1, 4),
        "w_query": x["peer_w_query"][0].reshape(KT, P, 16, P).transpose(2, 1, 0, 3),
        "sub_keys": x["peer_sub_keys"][0].transpose(2, 0, 1),
        "norms": _np.stack([x[k][0] for k in ("ln1_g", "ln1_b", "ln2_g", "ln2_b")]),
        "peer_u": x["peer_u"][0],
        "peer_v": x["peer_v"][0],
    }
    arrays = {k: _np.ascontiguousarray(a) for k, a in arrays.items()}
    nc = _bacc.Bacc("TRN2", target_bir_lowering=False, num_devices=1)
    dram = {k: nc.dram_tensor("in_" + k, a.shape, _mybir.dt.from_np(a.dtype), kind="ExternalInput").ap()
            for k, a in arrays.items()}
    outs = {k: nc.dram_tensor(k, s, F32, kind="ExternalOutput").ap() for k, s in OUTS.items()}
    hybrid_step(nc, dram, outs)
    r = _run(nc, [{"in_" + k: a for k, a in arrays.items()}], core_ids=[0]).results[0]
    y, pa, pn = r["out_y"], r["out_a"], r["out_n"]
    kw, vw = r["out_win_k"], r["out_win_v"]
    rows_a = pa.transpose(2, 1, 0).reshape(T, 2, NH, HD)
    rows_n = pn.transpose(2, 1, 0)
    nsa = rows_n[:, :8].reshape(T, 4, NG, HD)
    new_win = rows_n[:, 8:].reshape(T, 2, NG, HD)
    old_k = kw.transpose(0, 2, 1, 3).reshape(NB, P, NG, WIN).transpose(0, 3, 2, 1)
    old_v = vw.transpose(0, 2, 3, 1, 4).reshape(NB, WIN, NG, P)
    old = _np.stack([old_k, old_v], axis=2)
    smp = lambda a: a[NPROMPT:].reshape((1, NB, NT) + a.shape[1:])
    win_s = _np.concatenate([old[:, NT:], new_win[NPROMPT:].reshape(NB, NT, 2, NG, HD)], axis=1)[None]
    return (y[:NPROMPT].reshape(1, NPROMPT, DM), y[NPROMPT:].reshape(NB, NT, DM),
            rows_a[:NPROMPT][None, None], nsa[:NPROMPT][None, None], new_win[:NPROMPT][None, None],
            smp(rows_a), smp(nsa), win_s)
```

```python
from contextlib import ExitStack, contextmanager

import numpy as np

import concourse.bass as bass
from concourse import mybir

F32 = mybir.dt.float32
U32 = mybir.dt.uint32
I32 = mybir.dt.int32
ALU = mybir.AluOpType
ACT = mybir.ActivationFunctionType
AX = mybir.AxisListType

P = 128
DM = 2048
KT = DM // P
NPROMPT = 256
NB, NT = 8, 4
NSMP = NB * NT
T = NPROMPT + NSMP
PAST, PAGE, NPAGE = 2048, 128, 16
HD = 128
NH = 8
NG, HPG = 2, 4
ROPE = 32
SEL_BLOCK, NSEL, NTOP = 64, 33, 16
WIN = 512
NCP = (NPROMPT - 32) // 16 + 1
NCS = (PAST + NT - 32) // 16 + 1
PTOK, PNEW = NPROMPT, NSMP
SCALE = 1.0 / float(np.sqrt(HD))
ALPHA = 2.0 ** 0.25
EPS = 1e-5
NEG = -1.0e30
FORCE = 1.0e4
GELU_A, GELU_C = 0.044715, 2.0 * float(np.sqrt(2.0 / np.pi))
SLOTS = 128

QA, KA, VA, QB, KC, VC, KS, VS, KW, VW = 0, 8, 16, 24, 32, 34, 36, 38, 40, 42
NM = 44
ROPED = list(range(QB, QB + NH)) + [KC, KC + 1, KS, KS + 1, KW, KW + 1]
VTILES = list(range(VA, VA + NH)) + [VS, VS + 1, VW, VW + 1]

CONST_COLS = {"ident": 128, "ones": 128, "suffix": 128, "swap": 128, "strict": 128, "causal": 256,
              "new_sb": 32, "new_add": 64, "win_add": 4, "cmp_add": 30, "cmp_mul": 30, "cmp_slc": 33,
              "group": 128, "lower": NSEL * NSEL, "fold": 32, "tok_row": 256, "head_row": 8, "iota16": 16}
CONST_AT = {}
_at = 0
for _name, _n in CONST_COLS.items():
    CONST_AT[_name] = _at
    _at += _n
NCONST = _at


def constants():
    c = np.zeros((P, NCONST), np.float32)

    def put(name, a):
        c[:a.shape[0], CONST_AT[name]:CONST_AT[name] + a.shape[1]] = a

    p = np.arange(P)
    put("ident", np.eye(P))
    put("ones", np.ones((P, P)))
    put("suffix", (p[:, None] >= p[None, :]).astype(np.float32))
    swap = np.zeros((P, P))
    half = ROPE // 2
    for m in range(half):
        swap[m + half, m] = -1.0
        swap[m, m + half] = 1.0
    put("swap", swap)
    put("strict", (p[:, None] < p[None, :]).astype(np.float32))
    causal = np.zeros((P, 2 * P))
    causal[:, P:] = np.where(p[None, :] > p[:, None], NEG, 0.0)
    put("causal", causal)
    tok = np.arange(NSMP)
    b, t = tok // NT, tok % NT
    put("new_sb", ((b[:, None] == b[None, :]) & (t[:, None] < t[None, :])).astype(np.float32))
    row_t, row_b = p % NT, p // 32
    new = np.zeros((P, 2, NSMP))
    rows = np.zeros((NSMP, 2, P))
    for h in range(2):
        same = (row_b[:, None] + 4 * h) == b[None, :]
        new[:, h] = np.where(same & (t[None, :] <= row_t[:, None]), 0.0, NEG)
        rows[:, h] = (tok[:, None] == ((row_b + 4 * h) * NT + row_t)[None, :])
    put("new_add", new.reshape(P, -1))
    put("tok_row", rows.reshape(NSMP, -1))
    put("win_add", np.where(np.arange(4)[None, :] <= row_t[:, None], NEG, 0.0))
    q = np.arange(2)[None, :, None] * P + p[:, None, None]
    seen = (np.arange(NCP)[None, None, :] * 16 + 31) <= q
    put("cmp_add", np.where(seen, 0.0, NEG).reshape(P, -1))
    put("cmp_mul", seen.astype(np.float32).reshape(P, -1))
    i, j = np.arange(NCS)[:, None], np.arange(NSEL)[None, :]
    lo, hi = np.maximum(i * 16, j * SEL_BLOCK), np.minimum(i * 16 + 32, (j + 1) * SEL_BLOCK)
    put("cmp_slc", (np.maximum(hi - lo, 0) / 16).astype(np.float32))
    put("group", ((p[:, None] // 16 == p[None, :] // 16) & (p[:, None] % NT == p[None, :] % NT)).astype(np.float32))
    s = np.arange(NSEL)
    put("lower", np.broadcast_to((s[None, :] < s[:, None]).astype(np.float32).reshape(1, -1), (P, NSEL * NSEL)))
    put("fold", (p[:, None] % NSMP == np.arange(NSMP)[None, :]).astype(np.float32))
    put("head_row", ((p[:, None] % 32) // NT == np.arange(NH)[None, :]).astype(np.float32))
    put("iota16", np.broadcast_to(np.arange(16, dtype=np.float32)[None], (P, 16)))
    return c


def rope_tables():
    half = ROPE // 2
    inv = (np.float32(500000.0) ** (-np.arange(half, dtype=np.float32) / np.float32(half))).astype(np.float32)
    pos = np.concatenate([np.arange(NPROMPT), PAST + np.tile(np.arange(NT), NB)]).astype(np.float32)
    ang = (pos[None, :] * inv[:, None]).astype(np.float32).astype(np.float64)
    cs = np.zeros((P, 2, T), np.float32)
    cs[:, 0] = 1.0
    cs[:ROPE, 0] = np.tile(np.cos(ang), (2, 1))
    cs[:ROPE, 1] = np.tile(np.sin(ang), (2, 1))
    return cs


RING = 8
ROUND = RING
STREAM = [("w_in", NM, 1), ("cmp", 32, 8), ("ks", 16, 8), ("kw", 4, 1), ("vs", 16, 8), ("vw", 4, 1),
          ("ak", 64, 2), ("av", 64, 2), ("wo", 16, 1), ("wq", 16, 1)]
BY_POOL = ("ks", "vs")
FULL_SEMS = RING + RING // 2


class Stream:

    def __init__(self):
        self.first, self.before, self.dmas = {}, {}, {}
        n, full = 0, [0] * FULL_SEMS
        for name, count, dmas in STREAM:
            self.first[name], self.before[name], self.dmas[name] = n, list(full), dmas
            for j in range(count):
                full[self.full_index(name, j)] += 16 * dmas
            n += count
        self.total = n

    def full_index(self, name, k):
        s = self.slot(name, k)
        return RING + s // 2 if name in BY_POOL and k % 2 else s

    def slot(self, name, k):
        if name == "wq":
            return k % 4
        return (self.first[name] + k) % RING

    def full(self, name, it, k):
        turn = 2 * it + k // 4 if name == "wq" else it
        return self.before[name][self.full_index(name, k)] + 16 * self.dmas[name] * (turn + 1)

    def room(self, name, it, k):
        return self.first[name] + 8 * it + k + 1 + (4 if name == "wq" else 0)

    def used(self, name, it, k):
        return RING + self.first[name] + 8 * it + k + 1


class Chain:

    def __init__(self, eng, sem):
        self.eng, self.sem, self.n, self.loop = eng, sem, 0, None

    def value(self):
        if self.loop is None:
            return self.n
        i, base, per = self.loop
        return i * per + self.n

    def do(self, ins):
        ins.then_inc(self.sem, 1)
        self.n += 1
        self.eng.wait_ge(self.sem, self.value())

    def tell(self, ins, sem, value):
        ins.then_inc(sem, 1)
        self.eng.wait_ge(sem, value)

    @contextmanager
    def rounds(self, count, per):
        with self.eng.Fori(0, count) as i:
            base = self.n
            self.loop = (i, base, per)
            yield i
            self.loop = None
            assert self.n - base == per, (self.n - base, per)
        self.n = base + count * per


AT_CONST = 0
AT_SMALL = 2880
AT_H = AT_SMALL + 1344
AT_PROJ = AT_H + 3 * DM
AT_X = AT_PROJ + NM * T
AT_RING = AT_X + KT * T
AT_T = AT_RING + RING * 2048
WORDS = 53200

OUTS = {"out_y": (T, DM), "out_a": (P, 16, T), "out_n": (P, 12, T),
        "out_win_k": (NB // 2, P, 2, NG * WIN), "out_win_v": (NB // 2, P, 2, 4, NG * P)}


def hybrid_step(nc, dram, outs):
    stream = Stream()
    with ExitStack() as ctx:
        def sem(name):
            return ctx.enter_context(nc.semaphore(name))

        sb = ctx.enter_context(nc.sbuf_tensor("sb", [P, WORDS], F32))
        bank = [ctx.enter_context(nc.psum_tensor(f"bank{i}", [P, 512], F32)) for i in range(8)]

        def words(at, *shape):
            n = int(np.prod(shape))
            v = sb[:, at:at + n]
            if len(shape) == 1:
                return v
            names = " ".join("abcd"[:len(shape)])
            return v.rearrange(f"p ({names}) -> p {names}", **{"abcd"[i]: s for i, s in enumerate(shape)})

        const = {k: words(AT_CONST + a, CONST_COLS[k]) for k, a in CONST_AT.items()}
        ident, ones = const["ident"], const["ones"]
        _small = [AT_SMALL]

        def small(*shape):
            at = _small[0]
            _small[0] += int(np.prod(shape))
            assert _small[0] <= AT_H
            return words(at, *shape)

        cmp_w2 = small(2, P)
        cmp_pe = small(2, 32)
        pe_bias = small(2)
        prompt_kcmp = small(NG, 16)
        prompt_vcmp = small(NG, P)
        prompt_gate = small(2, 24)
        smp_gate_tok = small(24)
        smp_gate = small(2, 3)
        gate_tmp = small(2, 24)
        soft = small(64)
        pages_sb = sb[0:1, _small[0]:_small[0] + P].bitcast(I32)
        _small[0] += P
        _ = small(1)

        proj = words(AT_PROJ, NM, T)
        x_t = words(AT_X, KT, T)
        mix_t = x_t
        ring = [words(AT_RING + 2048 * s, 2048) for s in range(RING)]

        vcmp = words(AT_H, NB, NG * P)
        kcmp_t = words(AT_H + 2048, NB, NG * P)
        v_new = words(AT_H + 4608, 12, P)
        w_gate = words(AT_H + 4096, KT, 24)
        x_cmp = words(AT_H + 4096, 256)
        e_cmp = words(AT_H + 4352, 256)
        w1 = words(AT_T, 2, 32, P)
        rope = words(AT_T + 8192, 2, T)
        h_cmp = [words(AT_T + 8192 + 256 * k, 256) for k in range(2)]
        u_cmp = words(AT_T + 8704, 256)
        rope_tmp = words(AT_H, 2, T)
        gates_t = words(AT_H + 2 * T, T)
        pe_prod = words(AT_H + 1024, 8, P)
        pe_quarter = words(AT_H + 4608, 4, P)
        pe_part = words(AT_H + 5120, 2, P)

        item_used = sem("item_used")
        ring_full = [sem(f"ring_full{s}") for s in range(FULL_SEMS)]
        consts_in, x_in, wg_in, rope_in, w1_in, pages_in = (sem(n) for n in (
            "consts_in", "x_in", "wg_in", "rope_in", "w1_in", "pages_in"))
        dve_step, act_step = sem("dve_step"), sem("act_step")
        proj_evac = sem("proj_evac")
        gate_raw, gate_exp, gate_tok, gate_rows = (sem(n) for n in ("gate_raw", "gate_exp", "gate_tok", "gate_rows"))
        gate_turned, bias_part = sem("gate_turned"), sem("bias_part")
        swapped, roped = sem("swapped"), sem("roped")
        rows_out = sem("rows_out")
        bias_ready, bias_sb = sem("bias_ready"), sem("bias_sb")
        v_turned, v_new_in = sem("v_turned"), sem("v_new_in")
        ab_free, gelu_arg, gelu_exp, gelu_out = (sem(n) for n in ("ab_free", "gelu_arg", "gelu_exp", "gelu_out"))
        cmp_mm, cmp_in = sem("cmp_mm"), sem("cmp_in")

        def page(eng, n):
            return eng.value_load(pages_sb[0:1, bass.ds(n, 1)], min_val=0, max_val=dram["a_k"].shape[0] - 1)

        s_slc = words(AT_T, 2, 2080)
        p_slc_t = words(AT_T + 4160, 17, 2, P)
        q_pad = words(AT_T + 8512, NB, NG, 32)
        s_win = words(AT_H + 2048, 2, 544)
        p_win_t = words(AT_H + 3136, 5, 2, P)
        s_cmp = words(AT_X, 2, P)
        sum_cmp_t = words(AT_X + 256, 2, P)
        p_cmp_t = words(AT_X + 512, 2, P)
        imp = words(AT_X + 768, 2, NSEL)
        rank = words(AT_X + 840, 2, NSEL)
        sel_add = words(AT_X + 912, 2, NSEL)
        above = words(AT_X + 984, NSEL, NSEL)
        ties = words(AT_X + 984 + 1089, NSEL, NSEL)
        rows_c = words(AT_X + 2048, 2, 16, 32)
        pc_rows, pc_turned = sem("pc_rows"), sem("pc_turned")
        pc_ab, pc_mm, pc_in = sem("pc_ab"), sem("pc_mm"), sem("pc_in")
        q_pad_in, cmp_scored, cmp_neg, cmp_exp, cmp_p = (sem(n) for n in ("q_pad_in", "cmp_scored", "cmp_neg", "cmp_exp", "cmp_p"))
        cmp_sum, cmp_sum_in, imp_ready, imp_in = (sem(n) for n in ("cmp_sum", "cmp_sum_in", "imp_ready", "imp_in"))
        cmp_pg, slc_evac, new_scored, new_evac, win_evac = (sem(n) for n in (
            "cmp_pg", "slc_evac", "new_scored", "new_evac", "win_evac"))
        soft_neg, soft_exp, soft_p, turned, turned_in = (sem(n) for n in (
            "soft_neg", "soft_exp", "soft_p", "turned", "turned_in"))
        mix_nsa, held = sem("mix_nsa"), sem("held")
        o_nsa = words(AT_T, 2, NG * P)
        o_nsa_in, o_nsa_t, padded = sem("o_nsa_in"), sem("o_nsa_t"), sem("padded")

        def selected_pages(eng, name, odd, room):
            with eng.Fori(0, 2) as it:
                for k in range(odd, 8, 2):
                    s = stream.slot(name, k)
                    at = it * 64 + ((k % 4) * 16 + (k // 4) * 8)
                    found = [page(eng, at + j) for j in range(8)]
                    room(name, it, k)
                    for j, pg in enumerate(found):
                        src = dram["nsa_t"][bass.ds(pg, 1), 2] if name == "ks" else dram["nsa_v"][bass.ds(pg, 1)]
                        eng.dma_start(ring[s][:, 256 * j:256 * j + 256], src.rearrange("a p n -> (a p) n")
                                      ).then_inc(ring_full[stream.full_index(name, k)], 16)
        v_a = words(AT_H + 2048, 2, NH, P)
        v_b = words(AT_H + 4096, 2, 4, P)
        s_pr = words(AT_H + 5120, 2, 2, 2 * P)
        p_pr_t = words(AT_T + 4096, 2, 2, 2, P)
        p_prc_t = words(AT_T + 5120, 2, P)
        s_prc = words(AT_T + 5376, 2, 16)
        e_pr = words(AT_T + 4096, 4, 3 * P)
        z_pr = words(AT_T + 5632, 4, 3 * P)
        sp_pr = words(AT_T + 7168, 4, 3 * P)
        pr_max = words(AT_T + 8704, 6)
        pr_sum = words(AT_T + 8710, 6)
        vp_turned, vp_in = sem("vp_turned"), sem("vp_in")
        pb_scored, pb_neg, pb_negc, pb_exp, pb_p, pb_turned, pb_turned_in, pb_pv, pb_out = (sem(n) for n in (
            "pb_scored", "pb_neg", "pb_negc", "pb_exp", "pb_p", "pb_turned", "pb_turned_in", "pb_pv", "pb_out"))
        pa_z, pa_z_in, pa_neg, pa_log, pa_sp, pa_g, pa_arg, pa_exp, pa_w, pa_pv, pa_out = (sem(n) for n in (
            "pa_z", "pa_z_in", "pa_neg", "pa_log", "pa_sp", "pa_g", "pa_arg", "pa_exp", "pa_w", "pa_pv", "pa_out"))

        def prompt_unit(u):
            return u // 4, (u // 2) % 2, 2 * (u % 2)
        z_t = words(AT_T, 2, NPAGE, P)
        sp_t = words(AT_T + 4096, 2, NPAGE, P)
        e_t = words(AT_H, 2, NPAGE, P)
        later = e_t
        o_a = words(AT_H, 2, 2, 512)
        q_pad_a = words(AT_H + 4096, 4, NH, 32)
        z_nat = [words(AT_H + 5120 + 512 * k, 512) for k in range(2)]
        z_new = words(AT_PROJ + KC * T, NH, NSMP)
        sp_new = words(AT_PROJ + KC * T + 256, NH, NSMP)
        e_new = words(AT_PROJ + KC * T + 512, NH, NSMP)
        sn_z, sn_z_in, sn_neg, sn_log, sn_sp, sn_g, sn_arg, sn_exp, sn_w, sn_pv, sn_out = (sem(n) for n in (
            "sn_z", "sn_z_in", "sn_neg", "sn_log", "sn_sp", "sn_g", "sn_arg", "sn_exp", "sn_w", "sn_pv", "sn_out"))
        q_pad_a_in, z_nat_in, z_turned, z_t_in, sa_neg, sa_log, sa_later, sa_g, sa_arg, sa_w = (sem(n) for n in (
            "q_pad_a_in", "z_nat_in", "z_turned", "z_t_in", "sa_neg", "sa_log", "sa_later", "sa_g", "sa_arg", "sa_w"))
        o_a_in, o_a_t, mix_a = sem("o_a_in"), sem("o_a_t"), sem("mix_a")
        h_nat = words(AT_H, 3, DM)
        h_t = x_t
        norm = words(AT_PROJ, 4, DM)
        s_key = [words(AT_T, 16, P), words(AT_T + 2048, 16, P), words(AT_PROJ + 8192, 16, P)]
        q_t = words(AT_T + 4096, 16, T)
        out_parts = [words(AT_T + 2048 + 512 * k, 512) for k in range(2)]
        h_rep = words(AT_T + 6144, DM)
        y_quarter = words(AT_T + 2048, 4, 512)
        _tail = [AT_PROJ + 10240]

        def tail(*shape):
            at = _tail[0]
            _tail[0] += int(np.prod(shape))
            return words(at, *shape)

        top_s = tail(3, 16, 16)
        top_i = tail(3, 16, 16).bitcast(U32)
        best_s = tail(3, P)
        best_j = tail(3, P).bitcast(U32)
        assert _tail[0] <= AT_X
        _tail[0] = AT_PROJ
        work, cand, top_f = tail(256), tail(256), tail(16, 16)
        j_a, j_b = tail(P).bitcast(U32), tail(P).bitcast(U32)
        f_a, f_b, i_a, i_b, soft_sum = tail(P), tail(P), tail(P), tail(P), tail(16)
        expert = tail(288).bitcast(U32)
        peer_gate = tail(288)
        expert_s, gate_s = tail(P).bitcast(U32), tail(P)
        act16, w16 = tail(2, 16), tail(2, 16)
        u16, e16 = tail(16), tail(16)
        idx_u, idx_v = tail(2, 16).bitcast(U32), tail(2, 16).bitcast(U32)
        diag = [tail(P) for _ in range(4)]
        zeros = tail(P)
        one_hot = tail(32, 16)
        assert _tail[0] <= AT_PROJ + 4096
        ln = words(AT_SMALL + 512, 64)
        sub_keys = words(AT_SMALL, 2, P)
        u_ring, v_ring = ring[4:8], ring[0:4]

        tok_in, norm_in, sub_in = sem("tok_in"), sem("norm_in"), sem("sub_in")
        wo_evac, ln_mu, ln_sq, ln_var, ln_sd, h_in, h_turned, h_t_in = (sem(n) for n in (
            "wo_evac", "ln_mu", "ln_sq", "ln_var", "ln_sd", "h_in", "h_turned", "h_t_in"))
        q_in, s_mm, s_in, picked, gate_arg, gate_e, chosen = (sem(n) for n in ("q_in", "s_mm", "s_in", "picked", "gate_arg", "gate_e", "chosen"))
        u_full = [sem(f"u_full{k}") for k in range(4)]
        v_full = [sem(f"v_full{k}") for k in range(4)]
        idx_in, u_used, v_used, act_arg, act_e, w_ready, diag_in, tile_out, y_out = (sem(n) for n in (
            "idx_in", "u_used", "v_used", "act_arg", "act_e", "w_ready", "diag_in", "tile_out", "y_out"))
        parts_in, folded_out = sem("parts_in"), sem("folded_out")
        y_ready = sem("y_ready")
        rows_of = [P, P, NSMP]
        TOPK_IN = {}
        TOPK_IN[0] = {5: [(0, 2), (0, 3)], 9: [(0, 4), (0, 5)], 15: [(0, 6), (0, 7)]}
        TOPK_IN[1] = {2: [(1, 0)], 7: [(1, 1)], 12: [(1, 2)]}
        TOPK_IN[2] = {2: [(1, 3)], 7: [(1, 4)], 12: [(1, 5)]}
        TOPK_IN[3] = {3: [(1, 6)], 11: [(1, 7)]}
        TOPK_IN[4] = {7: [(2, 0)], 12: [(2, 1)]}
        TOPK_IN[5] = {2: [(2, 2)], 7: [(2, 3)], 12: [(2, 4)]}
        TOPK_IN[6] = {2: [(2, 5)], 7: [(2, 6)], 12: [(2, 7)]}
        GATES_IN = {4: 1, 7: 2}
        block = ctx.enter_context(nc.Block())

        @block.sync
        def _(sp):
            def room(name, it, k):
                sp.wait_ge(item_used, stream.room(name, it, k))

            sp.dma_start(pages_sb, dram["pages"]).then_inc(pages_in, 16)

            def load_w(it, k):
                room("w_in", it, k)
                s = stream.slot("w_in", k)
                src = dram["w_in"][bass.ds(8 * it + k, 1)].rearrange("m p k n -> (m p) (k n)")
                sp.dma_start(ring[s], src).then_inc(ring_full[s], 16)

            with sp.Fori(0, 5) as it:
                for k in range(8):
                    load_w(it, k)
            for k in range(4):
                load_w(5, k)
            sp.dma_start(outs["out_win_k"], dram["win_k"]).then_inc(rows_out, 16)
            sp.dma_start(outs["out_win_v"], dram["win_v"]).then_inc(rows_out, 16)

            sp.wait_ge(pages_in, 16)
            with sp.Fori(0, 4) as it:
                for k in range(8):
                    s = stream.slot("cmp", k)
                    b2, kv, half = k // 4, (k // 2) % 2, k % 2
                    found = [page(sp, it * 32 + (b2 * 16 + half * 8 + j)) for j in range(8)]
                    room("cmp", it, k)
                    for j, pg in enumerate(found):
                        sp.dma_start(ring[s][:, 256 * j:256 * j + 256],
                                     dram["nsa_t"][bass.ds(pg, 1), kv].rearrange("a p n -> (a p) n")
                                     ).then_inc(ring_full[s], 16)
            sp.wait_ge(roped, len(ROPED))
            sp.dma_start(outs["out_a"], proj[:, KA:QB, :]).then_inc(rows_out, 16)
            sp.dma_start(outs["out_n"], proj[:, KC:NM, :]).then_inc(rows_out, 16)
            selected_pages(sp, "ks", 0, room)
            for k in range(4):
                room("kw", 0, k)
                s = stream.slot("kw", k)
                sp.dma_start(ring[s], dram["win_k"][k].rearrange("p b n -> p (b n)")).then_inc(ring_full[s], 16)
            selected_pages(sp, "vs", 0, room)
            for k in range(4):
                room("vw", 0, k)
                s = stream.slot("vw", k)
                sp.dma_start(ring[s], dram["win_v"][k].rearrange("p b k n -> p (b k n)")).then_inc(ring_full[s], 16)
            def load_pair(name, src, it, k, half):
                s = stream.slot(name, k)
                found = [page(sp, it * 4 + (48 * half + (k % 4) * 16 + (k // 4) * 2 + j)) for j in range(2)]
                room(name, it, k)
                for j, pg in enumerate(found):
                    sp.dma_start(ring[s][:, 1024 * j:1024 * j + 1024],
                                 dram[src][bass.ds(pg, 1)].rearrange("a p n -> (a p) n")).then_inc(ring_full[s], 16)

            for name, src in (("ak", "a_k"), ("av", "a_v")):
                for half in range(2):
                    with sp.Fori(4 * half, 4 * half + 4) as it:
                        for k in range(8):
                            load_pair(name, src, it, k, half)
            with sp.Fori(0, 2) as it:
                for k in range(8):
                    room("wo", it, k)
                    s = stream.slot("wo", k)
                    src = dram["w_out"].rearrange("n q p k c -> (n q) p (k c)")[bass.ds(8 * it + k, 1)].rearrange("a p c -> (a p) c")
                    sp.dma_start(ring[s], src).then_inc(ring_full[s], 16)
            with sp.Fori(0, 2) as it:
                for k in range(8):
                    room("wq", it, k)
                    s = stream.slot("wq", k)
                    src = dram["w_query"][bass.ds(8 * it + k, 1)].rearrange("m p k n -> (m p) (k n)")
                    sp.dma_start(ring[s], src).then_inc(ring_full[s], 16)
            for tt in range(3):
                n = rows_of[tt]
                sp.wait_ge(y_ready, tt + 1)
                sp.dma_start(outs["out_y"][P * tt:P * tt + n, :], h_nat[0:n, tt, :]).then_inc(y_out, 16)
            sp.wait_ge(y_out, 48)
            sp.wait_ge(rows_out, 64)

        @block.scalar
        def _(act):
            ch = Chain(act, act_step)
            act.dma_start(x_t, dram["tokens_t"]).then_inc(x_in, 16)
            act.sem_inc(proj_evac, 2)
            act.sem_inc(cmp_in, 2)

            def evacuate(it, k):
                act.wait_ge(item_used, stream.used("w_in", it, k))
                act.activation(proj[:, bass.ds(8 * it + k, 1), :], bank[k % 2][:, None, 0:T], ACT.Copy).then_inc(proj_evac, 1)

            with act.Fori(0, 5) as it:
                for k in range(8):
                    evacuate(it, k)
            for k in range(4):
                evacuate(5, k)
            act.wait_ge(gate_raw, 1)
            act.activation(gates_t[0:24], bank[0][0:24, 0:T], ACT.Exp, scale=-1.0).then_inc(gate_exp, 1)

            with act.Fori(0, 4) as it:
                for st in range(4):
                    b2, kv = st // 2, st % 2
                    act.wait_ge(gelu_arg, 4 * it + st + 1)
                    act.activation(e_cmp, u_cmp, ACT.Exp, scale=-GELU_C).then_inc(gelu_exp, 1)
                    act.wait_ge(cmp_mm, 4 * it + st + 3)
                    dst = vcmp if kv else kcmp_t
                    act.activation(dst[:, bass.ds(2 * it + b2, 1), :], bank[4 + kv][:, None, 0:256], ACT.Copy).then_inc(cmp_in, 1)
            act.wait_ge(pc_ab, 1)
            act.activation(e_cmp[:, 0:P], bank[6][:, 0:P], ACT.Copy).then_inc(pc_rows, 1)
            act.wait_ge(gelu_arg, 17)
            act.activation(e_cmp[:, 0:64], u_cmp[:, 0:64], ACT.Exp, scale=-GELU_C).then_inc(gelu_exp, 1)
            act.wait_ge(pc_mm, 1)
            act.activation(prompt_kcmp, bank[6][:, 0:32].rearrange("p (g n) -> p g n", g=NG), ACT.Copy).then_inc(pc_in, 1)
            act.activation(prompt_vcmp[0:NCP], bank[7][0:NCP, 0:256].rearrange("p (g n) -> p g n", g=NG), ACT.Copy).then_inc(pc_in, 1)

            for h in range(2):
                act.wait_ge(cmp_neg, h + 1)
                act.activation(s_cmp[:, h, 0:NCS], bank[h][:, 0:NCS], ACT.Exp, bias=soft[:, 2 + h:3 + h], scale=SCALE,
                               accum_out=soft[:, 4 + h:5 + h]).then_inc(cmp_exp, 1)
            act.wait_ge(cmp_sum, 1)
            act.activation(sum_cmp_t[0:NCS], bank[2][0:NCS, 0:256].rearrange("p (h n) -> p h n", h=2), ACT.Copy).then_inc(cmp_sum_in, 1)

            def soft_exps(h):
                act.wait_ge(soft_neg, 2 * h + 1)
                act.activation(s_slc[:, h], s_slc[:, h], ACT.Exp, bias=soft[:, 8 + h:9 + h], scale=SCALE,
                               accum_out=soft[:, 12 + h:13 + h]).then_inc(soft_exp, 1)
                act.wait_ge(soft_neg, 2 * h + 2)
                act.activation(s_win[:, h], s_win[:, h], ACT.Exp, bias=soft[:, 10 + h:11 + h], scale=SCALE,
                               accum_out=soft[:, 14 + h:15 + h]).then_inc(soft_exp, 1)

            soft_exps(0)
            soft_exps(1)
            for h in range(2):
                for n in range(6):
                    act.wait_ge(turned, 6 * h + n + 1)
                    src = bank[n % 4]
                    if n < 4:
                        ins = act.activation(p_slc_t[:, 4 * n:4 * n + 4, h, :], src[:, :].rearrange("p (a b) -> p a b", a=4), ACT.Copy)
                    elif n == 4:
                        ins = act.activation(p_win_t[:, 0:4, h, :], src[:, :].rearrange("p (a b) -> p a b", a=4), ACT.Copy)
                    else:
                        act.wait_ge(padded, 2)
                        ch.do(act.activation(p_slc_t[0:NSMP, 16, h, :], src[0:NSMP, 0:P], ACT.Copy))
                        ch.do(act.activation(p_win_t[0:NSMP, 4, h, :], src[0:NSMP, P:2 * P], ACT.Copy))
                        ins = act.activation(p_cmp_t[0:NCS, h, :], src[0:NCS, 2 * P:3 * P], ACT.Copy)
                    ins.then_inc(turned_in, 1)
            def prompt_act():
                for n in range(6):
                    act.wait_ge(vp_turned, n + 1)
                    dst = (v_a[:, n // 2, 4 * (n % 2):4 * (n % 2) + 4] if n < 4 else v_b[:, n - 4])
                    act.activation(dst, bank[4 + n % 4][:, :].rearrange("p (a b) -> p a b", a=4), ACT.Copy).then_inc(vp_in, 1)
                for u in range(8):
                    nk = P * (prompt_unit(u)[0] + 1)
                    act.wait_ge(pb_neg, u + 1)
                    for n in range(4):
                        act.activation(s_pr[:, n // 2, n % 2, 0:nk], s_pr[:, n // 2, n % 2, 0:nk], ACT.Exp, bias=pr_max[:, n:n + 1], scale=SCALE,
                                       accum_out=pr_sum[:, n:n + 1]).then_inc(pb_exp, 1)
                    act.wait_ge(pb_negc, u + 1)
                    act.activation(s_prc[:, :, 0:NCP], s_prc[:, :, 0:NCP], ACT.Exp, scale=SCALE).then_inc(pb_exp, 1)
                    for br in range(2):
                        act.wait_ge(pb_turned, 3 * u + br + 1)
                        act.activation(p_pr_t[:, br].rearrange("p k h n -> p (k h n)")[:, 0:2 * nk], bank[4 + br][:, 0:2 * nk], ACT.Copy
                                       ).then_inc(pb_turned_in, 1)
                    act.wait_ge(pb_turned, 3 * u + 3)
                    act.activation(p_prc_t[0:NCP], bank[6][0:NCP, 0:256].rearrange("p (a b) -> p a b", a=2), ACT.Copy).then_inc(pb_turned_in, 1)
                for u in range(2):
                    for j in range(4):
                        act.wait_ge(pa_z, 4 * u + j + 1)
                        if u:
                            act.wait_ge(pa_pv, 4)
                        act.activation(z_pr[:, j], bank[4 + j][:, 0:3 * P], ACT.Copy, scale=SCALE).then_inc(pa_z_in, 1)
                    act.wait_ge(pa_neg, u + 1)
                    ch.do(act.activation(e_pr, e_pr, ACT.Exp))
                    act.activation(e_pr, e_pr, ACT.Ln, bias=1.0).then_inc(pa_log, 1)
                    act.wait_ge(pa_arg, 4 * u + 4)
                    act.activation(z_pr, z_pr, ACT.Exp).then_inc(pa_exp, 1)
            act.wait_ge(sn_z, 1)
            act.activation(z_new[0:NSMP], bank[0][0:NSMP, 0:256].rearrange("p (h n) -> p h n", h=NH), ACT.Copy, scale=SCALE).then_inc(sn_z_in, 1)
            act.wait_ge(sn_neg, 1)
            ch.do(act.activation(e_new[0:NSMP], e_new[0:NSMP], ACT.Exp))
            act.activation(e_new[0:NSMP], e_new[0:NSMP], ACT.Ln, bias=1.0).then_inc(sn_log, 1)
            act.wait_ge(sn_arg, 1)
            act.activation(z_new[0:NSMP], z_new[0:NSMP], ACT.Exp).then_inc(sn_exp, 1)

            def scores_out(half):
                with act.Fori(2 * half, 2 * half + 2) as it:
                    for k in range(2):
                        act.wait_ge(item_used, stream.used("ak", 2 * it + k, 7))
                        act.activation(z_nat[k], bank[3 + k][:, :], ACT.Copy, scale=SCALE).then_inc(z_nat_in, 1)

            def logs(half):
                act.wait_ge(sa_neg, half + 1)
                ch.do(act.activation(e_t[:, half], e_t[:, half], ACT.Exp))
                act.activation(e_t[:, half], e_t[:, half], ACT.Ln, bias=1.0).then_inc(sa_log, 1)

            act.sem_inc(z_nat_in, 2)
            scores_out(0)
            logs(0)
            scores_out(1)
            logs(1)
            for n in range(8):
                act.wait_ge(sa_arg, n + 1)
                zz = z_t[:, n // 4, 4 * (n % 4):4 * (n % 4) + 4]
                act.activation(zz, zz, ACT.Exp).then_inc(sa_w, 1)
            prompt_act()
            for half in range(2):
                act.wait_ge(item_used, stream.used("av", 4 * half + 3, 7))
                for c in range(2):
                    act.activation(o_a[:, half, c], bank[2 * half + c][:, :], ACT.Copy).then_inc(o_a_in, 1)
            for n in range(4):
                act.wait_ge(item_used, stream.used("wo", n // 2, 4 * (n % 2) + 3))
                if n >= 2:
                    act.wait_ge(folded_out, n - 1)
                act.activation(out_parts[n % 2], bank[3 * (n % 2) + 2][:, :], ACT.Copy).then_inc(parts_in, 1)
            def norm_square(n, tt, c):
                act.wait_ge(ln_mu, c)
                act.activation(words(AT_T + DM * tt, DM)[0:n], h_nat[0:n, tt, :], ACT.Square, bias=ln[0:n, 8 + tt:9 + tt],
                               accum_out=ln[0:n, 12 + tt:13 + tt]).then_inc(ln_sq, 1)

            def norm_root(n, tt, c):
                act.wait_ge(ln_var, c)
                act.activation(ln[0:n, 16 + tt:17 + tt], ln[0:n, 12 + tt:13 + tt], ACT.Sqrt).then_inc(ln_sd, 1)

            for tt in range(3):
                norm_square(rows_of[tt], tt, tt + 1)
            for tt in range(3):
                norm_root(rows_of[tt], tt, tt + 1)
            for tt in range(3):
                n = rows_of[tt]
                for c in range(4):
                    act.wait_ge(h_turned, 4 * tt + c + 1)
                    act.activation(h_t[:, 4 * c:4 * c + 4, P * tt:P * tt + n],
                                   bank[6 + c % 2][:, :].rearrange("p (a b) -> p a b", a=4)[:, :, 0:n], ACT.Copy).then_inc(h_t_in, 1)
            def exp_of_gates(tt, p):
                b = best_s[0:rows_of[tt], tt, 32 * p:32 * p + 32]
                act.wait_ge(gate_arg, 4 * tt + p + 1)
                act.activation(b, b, ACT.Exp).then_inc(gate_e, 1)

            for m in range(17):
                if m in (8, 12):
                    exp_of_gates(0, m // 4 - 2)
                if m < 16:
                    act.wait_ge(item_used, stream.used("wq", m // 8, m % 8))
                    act.activation(q_t[:, m, :], bank[m % 2][:, 0:T], ACT.Copy).then_inc(q_in, 1)
                if m:
                    act.wait_ge(s_mm, m)
                    for tt in range(3):
                        n = rows_of[tt]
                        act.activation(s_key[tt][0:n, m - 1, :], bank[2 + (m - 1) % 2][0:n, P * tt:P * tt + P], ACT.Copy).then_inc(s_in, 1)
            def gelu_exp16(r):
                act.wait_ge(act_arg, r + 1)
                act.activation(e16, u16, ACT.Exp, scale=-GELU_C).then_inc(act_e, 1)

            def diagonals(r, par, folded):
                for j in range(16):
                    if j == 0:
                        act.wait_ge(w_ready, r + 1)
                    act.wait_ge(v_used, 16 * r + j + 1)
                    w = w16[:, par, j:j + 1]
                    if folded:
                        act.activation(diag[j % 4][:, 0:NSMP], const["fold"], ACT.Copy, scale=w).then_inc(diag_in, 1)
                    else:
                        act.activation(diag[j % 4], ident, ACT.Copy, scale=w).then_inc(diag_in, 1)

            act.sem_inc(diag_in, 32)
            exp_of_gates(0, 2)
            for r in range(8):
                if r == 0:
                    exp_of_gates(0, 3)
                gelu_exp16(r)
                if r in GATES_IN:
                    for p in range(4):
                        exp_of_gates(GATES_IN[r], p)
                diagonals(r, r % 2, False)
            with act.Fori(4, 8) as it:
                for par in range(2):
                    gelu_exp16(2 * it + par)
                    diagonals(2 * it + par, par, False)
            for par in range(2):
                gelu_exp16(16 + par)
                if par == 0:
                    norm_square(P, 0, 4)
                    norm_root(P, 0, 4)
                diagonals(16 + par, par, True)
            norm_square(P, 1, 5)
            norm_root(P, 1, 5)
            norm_square(NSMP, 2, 6)
            norm_root(NSMP, 2, 6)

        @block.tensor
        def _(pe):
            pe.sem_inc(item_used, RING)

            def arrived(name, it, k):
                pe.wait_ge(ring_full[stream.full_index(name, k)], stream.full(name, it, k))
                return ring[stream.slot(name, k)]

            pe.wait_ge(x_in, 16)

            def project(it, k):
                w = arrived("w_in", it, k)
                pe.wait_ge(proj_evac, 8 * it + k + 1)
                for kt in range(KT):
                    mm = pe.matmul(bank[k % 2][:, 0:T], w[:, kt * P:(kt + 1) * P], x_t[:, kt, :],
                                   start=(kt == 0), stop=(kt == KT - 1))
                mm.then_inc(item_used, 1)

            def swap(m):
                if m in ROPED:
                    n = ROPED.index(m)
                    if n == 0:
                        pe.wait_ge(consts_in, 16)
                    pe.wait_ge(proj_evac, 2 + m + 1)
                    if n >= 2:
                        pe.wait_ge(roped, n - 1)
                    pe.matmul(bank[2 + n % 2][:, 0:T], const["swap"], proj[:, m, :], start=True, stop=True).then_inc(swapped, 1)

            with pe.Fori(0, 3) as it:
                for k in range(8):
                    project(it, k)
            for m in range(24, NM + 2):
                if m < NM:
                    project(m // 8, m % 8)
                swap(m - 2)
            pe.wait_ge(wg_in, 16)
            pe.wait_ge(w1_in, 48)
            pe.wait_ge(proj_evac, 2 + NM)
            for kt in range(KT):
                mm = pe.matmul(bank[0][0:24, 0:T], w_gate[:, kt, :], x_t[:, kt, :], start=(kt == 0), stop=(kt == KT - 1))
            mm.then_inc(gate_raw, 1)
            pe.wait_ge(bias_part, 1)
            for kv in range(2):
                mm = pe.matmul(bank[4][:, kv:kv + 1], pe_part[:, kv, :], ones[:, 0:1], start=True, stop=True, skip_group_check=True)
            mm.then_inc(bias_ready, 1)
            pe.wait_ge(gate_exp, 1)
            for tt in range(3):
                n = P if tt < 2 else NSMP
                mm = pe.transpose(bank[0][0:n, 24 * tt:24 * tt + 24], gates_t[0:24, P * tt:P * tt + n], ident[0:24, 0:24])
            mm.then_inc(gate_turned, 1)
            pe.wait_ge(gate_tok, 1)
            for h in range(2):
                mm = pe.matmul(bank[1][:, 24 * h:24 * h + 24], const["tok_row"][0:NSMP, P * h:P * h + P],
                               smp_gate_tok[0:NSMP], start=True, stop=True, skip_group_check=True)
            mm.then_inc(gate_rows, 1)
            for n, m in enumerate(VTILES):
                mm = pe.transpose(bank[5 + n // 4][0:NSMP, P * (n % 4):P * (n % 4) + P], proj[:, m, PTOK:T], ident)
            mm.then_inc(v_turned, 1)
            pe.wait_ge(roped, len(ROPED))
            pe.wait_ge(v_new_in, 3)
            pe.wait_ge(bias_sb, 1)
            pe.sem_inc(cmp_mm, 2)

            def halves(it, st):
                kv = st % 2
                pe.wait_ge(ab_free, 4 * it + st + 1)
                ab = bank[2 + kv]
                for half in range(2):
                    k = 2 * st + half
                    rows = arrived("cmp", it, k).rearrange("p (c l) -> p c l", l=16)
                    for part in range(2):
                        for l in range(16):
                            mm = pe.matmul(ab[:, 256 * part + 128 * half:256 * part + 128 * half + 128],
                                           w1[:, kv, 16 * part + l, :], rows[:, :, l],
                                           start=(l == 0), stop=(l == 15), skip_group_check=True)
                    mm.then_inc(item_used, 1)

            def second(it, st):
                kv = st % 2
                pe.wait_ge(gelu_out, 4 * it + st + 1)
                pe.wait_ge(cmp_in, 4 * it + st + 1)
                if kv == 0:
                    mm = pe.matmul(bank[4][:, 0:256], cmp_w2[:, 0, :], h_cmp[0], start=True, stop=True)
                else:
                    for g in range(NG):
                        mm = pe.matmul(bank[5][:, P * g:P * g + P], h_cmp[1][:, P * g:P * g + P], cmp_w2[:, 1, :],
                                       start=True, stop=True, skip_group_check=True)
                mm.then_inc(cmp_mm, 1)

            with pe.Fori(0, 4) as it:
                halves(it, 0)
                for st in range(1, 4):
                    halves(it, st)
                    second(it, st - 1)
                second(it, 3)
            pe.wait_ge(pc_rows, 2)
            for l in range(16):
                for kv in range(2):
                    for part in range(2):
                        at = 64 * kv + 32 * part
                        mm = pe.matmul(bank[6][at:at + 32, 0:P], rows_c[:, kv, l, :], w1[:, kv, 16 * part + l, :],
                                       start=(l == 0), stop=(l == 15))
            mm.then_inc(pc_ab, 1)
            pe.wait_ge(pc_rows, 3)
            pe.transpose(bank[7][:, 0:P], e_cmp[:, 0:P], ident).then_inc(pc_turned, 1)
            pe.wait_ge(gelu_out, 17)
            pe.matmul(bank[6][:, 0:32], cmp_w2[:, 0, :], h_cmp[0][:, 0:32], start=True, stop=True)
            for g in range(NG):
                mm = pe.matmul(bank[7][0:16, P * g:P * g + P], h_cmp[0][:, 32 + 16 * g:48 + 16 * g], cmp_w2[:, 1, :],
                               start=True, stop=True, skip_group_check=True)
            mm.then_inc(pc_mm, 1)

            pe.wait_ge(q_pad_in, 1)
            pe.wait_ge(cmp_in, 2 + 16)
            for h in range(2):
                for b4 in range(4):
                    for g in range(NG):
                        mm = pe.matmul(bank[h][32 * b4:32 * b4 + 32, 0:P], q_pad[:, 4 * h + b4, g], kcmp_t[:, 4 * h + b4, P * g:P * g + P],
                                       start=(g == 0), stop=(g == 1))
                mm.then_inc(cmp_scored, 1)
            pe.wait_ge(cmp_p, 2)
            for h in range(2):
                mm = pe.matmul(bank[2][0:NCS, P * h:P * h + P], s_cmp[:, h, 0:NCS], const["group"], start=True, stop=True, skip_group_check=True)
            mm.then_inc(cmp_sum, 1)
            pe.wait_ge(cmp_sum_in, 1)
            for h in range(2):
                mm = pe.matmul(bank[3][:, NSEL * h:NSEL * h + NSEL], sum_cmp_t[0:NCS, h, :], const["cmp_slc"][0:NCS], start=True, stop=True,
                               skip_group_check=True)
            mm.then_inc(imp_ready, 1)
            pe.wait_ge(pc_in, 2)
            for h in range(2):
                for ph in range(2):
                    if h:
                        pe.wait_ge(slc_evac, 2 * ph + 2)
                    for b4 in range(4):
                        rows = arrived("ks", h, 4 * ph + b4).rearrange("p (q g n) -> p q g n", q=8, g=NG)
                        for c in range(2):
                            for g in range(NG):
                                mm = pe.matmul(bank[4 + 2 * ph + c][32 * b4:32 * b4 + 32, :], q_pad[:, 4 * h + b4, g],
                                               rows[:, 4 * c:4 * c + 4, g, :], start=(g == 0), stop=(g == 1))
                        mm.then_inc(item_used, 1)
            pe.wait_ge(imp_in, 1)
            for h in range(2):
                for b4 in range(4):
                    for n, m in enumerate((KS, KW)):
                        for g in range(NG):
                            at = 64 * n + 32 * h
                            mm = pe.matmul(bank[3][32 * b4:32 * b4 + 32, at:at + 32], q_pad[:, 4 * h + b4, g], proj[:, m + g, PTOK:T],
                                           start=(g == 0), stop=(g == 1), skip_group_check=True)
            mm.then_inc(new_scored, 1)
            pe.wait_ge(cmp_exp, 2)
            for k in range(4):
                rows = arrived("kw", 0, k).rearrange("p (b g n) -> p b g n", b=2, g=NG)
                for b2 in range(2):
                    b = 2 * k + b2
                    for g in range(NG):
                        mm = pe.matmul(bank[b // 4][32 * (b % 4):32 * (b % 4) + 32, :], q_pad[:, b, g], rows[:, b2, g, :],
                                       start=(g == 0), stop=(g == 1))
                mm.then_inc(item_used, 1)
            pe.wait_ge(win_evac, 4)
            pe.wait_ge(new_evac, 4)
            pe.wait_ge(cmp_pg, 2)
            for h in range(2):
                pe.wait_ge(soft_p, 2 * h + 2)
                for n in range(6):
                    if 6 * h + n >= 4:
                        pe.wait_ge(turned_in, 6 * h + n - 3 if n >= 4 else 6 * h)
                    dst = bank[n % 4]
                    if n < 5:
                        src = s_slc[:, h, 512 * n:512 * n + 512] if n < 4 else s_win[:, h, 0:512]
                        for j in range(4):
                            mm = pe.transpose(dst[:, P * j:P * j + P], src[:, P * j:P * j + P], ident)
                    else:
                        pe.transpose(dst[0:NSMP, 0:P], s_slc[:, h, PAST:], ident)
                        pe.transpose(dst[0:NSMP, P:2 * P], s_win[:, h, WIN:], ident)
                        mm = pe.transpose(dst[0:NCS, 2 * P:3 * P], s_cmp[:, h, 0:NCS], ident)
                    mm.then_inc(turned, 1)
            pe.wait_ge(turned_in, 12)
            pe.wait_ge(slc_evac, 8)
            pv = bank[7]
            for h in range(2):
                out = pv[:, 256 * h:256 * h + 256]
                parts = [(p_cmp_t[0:NCS, h], lambda b: vcmp[0:NCS, b, :]),
                         (p_slc_t[:, 16, h], lambda b: v_new[:, 8:10, :]),
                         (p_win_t[:, 4, h], lambda b: v_new[:, 10:12, :])]
                for n, (wt, val) in enumerate(parts):
                    for b4 in range(4):
                        r = slice(32 * b4, 32 * b4 + 32)
                        pe.matmul(out[r], wt[:, r], val(4 * h + b4), start=(n == 0 and h == 0), stop=False, skip_group_check=True)
            for h in range(2):
                out = pv[:, 256 * h:256 * h + 256]
                for ph in range(2):
                    rows = [arrived("vs", h, 4 * ph + b4) for b4 in range(4)]
                    for j in range(8):
                        for b4 in range(4):
                            r = slice(32 * b4, 32 * b4 + 32)
                            mm = pe.matmul(out[r], p_slc_t[:, 8 * ph + j, h, r], rows[b4][:, 256 * j:256 * j + 256], start=False, stop=False,
                                           skip_group_check=True)
                            if j == 7:
                                mm.then_inc(item_used, 1)
            for h in range(2):
                out = pv[:, 256 * h:256 * h + 256]
                rows = [arrived("vw", 0, 2 * h + k).rearrange("p (b k n) -> p b k n", b=2, k=4) for k in range(2)]
                for j in range(4):
                    for b4 in range(4):
                        r = slice(32 * b4, 32 * b4 + 32)
                        mm = pe.matmul(out[r], p_win_t[:, j, h, r], rows[b4 // 2][:, b4 % 2, j, :], start=False, stop=(j == 3),
                                       skip_group_check=True)
                        if j == 3 and b4 % 2:
                            mm.then_inc(item_used, 1)
            pe.wait_ge(o_nsa_in, 1)
            for h in range(2):
                for g in range(NG):
                    mm = pe.transpose(bank[h][:, P * g:P * g + P], o_nsa[:, h, P * g:P * g + P], ident)
            mm.then_inc(o_nsa_t, 1)
            def prompt_values():
                pe.wait_ge(sa_arg, 8)
                for n in range(6):
                    if n >= 4:
                        pe.wait_ge(vp_in, n - 3)
                    for j in range(4):
                        kt, m = (n // 2, VA + 4 * (n % 2) + j) if n < 4 else (n - 4, (VS, VS + 1, VW, VW + 1)[j])
                        mm = pe.transpose(bank[4 + n % 4][:, P * j:P * j + P], proj[:, m, P * kt:P * kt + P], ident)
                    mm.then_inc(vp_turned, 1)

            def sparse_scores(u):
                qt, g, h0 = prompt_unit(u)
                nk = P * (qt + 1)
                pe.wait_ge(vp_in, 6)
                if u:
                    pe.wait_ge(pb_turned_in, 3 * u)
                for i in range(2):
                    q = proj[:, QB + HPG * g + h0 + i, P * qt:P * qt + P]
                    pe.matmul(bank[4 + i][:, 0:nk], q, proj[:, KS + g, 0:nk], start=True, stop=True, skip_group_check=True)
                    pe.matmul(bank[4 + i][:, 256:256 + nk], q, proj[:, KW + g, 0:nk], start=True, stop=True, skip_group_check=True)
                    mm = pe.matmul(bank[6][:, 16 * i:16 * i + NCP], q, prompt_kcmp[:, g, 0:NCP], start=True, stop=True, skip_group_check=True)
                mm.then_inc(pb_scored, 1)

            def sparse_turned(u):
                qt = prompt_unit(u)[0]
                pe.wait_ge(pb_p, 2 * u + 2)
                for br in range(2):
                    for kt in range(qt + 1):
                        for i in range(2):
                            at = P * (2 * kt + i)
                            mm = pe.transpose(bank[4 + br][:, at:at + P], s_pr[:, i, br, P * kt:P * kt + P], ident)
                    mm.then_inc(pb_turned, 1)
                for i in range(2):
                    mm = pe.transpose(bank[6][0:NCP, P * i:P * i + P], s_prc[:, i, 0:NCP], ident)
                mm.then_inc(pb_turned, 1)

            def sparse_values(u):
                qt, g, h0 = prompt_unit(u)
                pe.wait_ge(pb_turned_in, 3 * u + 3)
                if u:
                    pe.wait_ge(pb_out, u)
                out = bank[7][:, 0:2 * P]
                for br in range(2):
                    for kt in range(qt + 1):
                        pe.matmul(out, v_b[:, kt, 2 * br + g, :], p_pr_t[:, br, kt], start=(br == 0 and kt == 0), stop=False)
                pe.matmul(out, prompt_vcmp[0:NCP, g, :], p_prc_t[0:NCP], start=False, stop=True).then_inc(pb_pv, 1)

            def stick_scores(u):
                pe.wait_ge(pb_out, 8)
                if u:
                    pe.wait_ge(pa_out, 4)
                for j in range(4):
                    h = 4 * u + j
                    pe.matmul(bank[4 + j][:, 0:2 * P], proj[:, KA + h, 0:P], proj[:, QA + h, 0:2 * P], start=True, stop=True, skip_group_check=True)
                    pe.matmul(bank[4 + j][:, 2 * P:3 * P], proj[:, KA + h, P:2 * P], proj[:, QA + h, P:2 * P], start=True, stop=True,
                              skip_group_check=True).then_inc(pa_z, 1)

            def stick_sums(u):
                pe.wait_ge(pa_sp, u + 1)
                for j in range(4):
                    pe.wait_ge(pa_z_in, 4 * u + j + 1)
                    pe.matmul(bank[4 + j][:, 0:2 * P], const["suffix"], sp_pr[:, j, 0:2 * P], start=True, stop=False, skip_group_check=True)
                    pe.matmul(bank[4 + j][:, P:2 * P], ones, sp_pr[:, j, 2 * P:3 * P], start=False, stop=False, skip_group_check=True)
                    pe.matmul(bank[4 + j][:, 2 * P:3 * P], const["suffix"], sp_pr[:, j, 2 * P:3 * P], start=False, stop=True,
                              skip_group_check=True).then_inc(pa_g, 1)

            def stick_values(u):
                pe.wait_ge(pa_w, u + 1)
                for j in range(4):
                    pe.matmul(bank[4 + j][:, 0:2 * P], v_a[:, 0, 4 * u + j, :], z_pr[:, j, 0:2 * P], start=True, stop=False, skip_group_check=True)
                    pe.matmul(bank[4 + j][:, P:2 * P], v_a[:, 1, 4 * u + j, :], z_pr[:, j, 2 * P:3 * P], start=False, stop=True,
                              skip_group_check=True).then_inc(pa_pv, 1)

            def prompt_piece(i):
                if i == 0:
                    prompt_values()
                elif i <= 24:
                    u, step = (i - 1) // 3, (i - 1) % 3
                    if step == 0:
                        if u:
                            sparse_values(u - 1)
                        sparse_scores(u)
                    elif step == 2:
                        sparse_turned(u)
                elif i == 25:
                    sparse_values(7)
                    stick_scores(0)
                elif i == 27:
                    stick_sums(0)
                elif i == 29:
                    stick_values(0)
                    stick_scores(1)
                elif i == 31:
                    stick_sums(1)
            pe.wait_ge(mix_nsa, 4)
            for h in range(NH):
                mm = pe.matmul(bank[0][0:NSMP, NSMP * h:NSMP * h + NSMP], proj[:, KA + h, PTOK:T], proj[:, QA + h, PTOK:T], start=True, stop=True,
                               skip_group_check=True)
            mm.then_inc(sn_z, 1)
            pe.wait_ge(sn_sp, 1)
            pe.matmul(bank[1][0:NSMP, 0:256], const["suffix"][0:NSMP, 0:NSMP], sp_new[0:NSMP].rearrange("p h n -> p (h n)"), start=True,
                      stop=True).then_inc(sn_g, 1)
            pe.wait_ge(sn_w, 1)
            for h in range(NH):
                mm = pe.matmul(bank[2][:, NSMP * h:NSMP * h + NSMP], v_new[0:NSMP, h, :], z_new[0:NSMP, h, :], start=True, stop=True,
                               skip_group_check=True)
            mm.then_inc(sn_pv, 1)
            for half in range(2):
                pe.wait_ge(q_pad_a_in, half + 1)
                with pe.Fori(2 * half, 2 * half + 2) as it:
                    for k in range(2):
                        pe.wait_ge(z_nat_in, 2 * it + k + 1)
                        for pp in range(2):
                            rows = [arrived("ak", 2 * it + k, 4 * pp + b4).rearrange("p (q h n) -> p q h n", q=2, h=NH) for b4 in range(4)]
                            for h in range(NH):
                                for b4 in range(4):
                                    mm = pe.matmul(bank[3 + k][32 * b4:32 * b4 + 32, 256 * pp:256 * pp + 256], q_pad_a[:, b4, h],
                                                   rows[b4][:, :, h, :], start=(h == 0), stop=(h == NH - 1), skip_group_check=True)
                                    if h == NH - 1:
                                        mm.then_inc(item_used, 1)
                    for k in range(2):
                        pe.wait_ge(z_nat_in, 2 * it + k + 3)
                        pe.wait_ge(z_t_in, 2 * it + k + 1)
                        for j in range(4):
                            mm = pe.transpose(bank[5 + k][:, P * j:P * j + P], z_nat[k][:, P * j:P * j + P], ident)
                        mm.then_inc(z_turned, 1)
            for n in range(8):
                half, q = n // 4, n % 4
                if q == 0:
                    pe.wait_ge(sa_later, half + 1)
                    pe.wait_ge(z_t_in, 2 + 8)
                if n >= 4:
                    pe.wait_ge(sa_arg, n - 3)
                bk = bank[4 + n % 4]
                pe.matmul(bk[:, :], const["suffix"], sp_t[:, half, 4 * q:4 * q + 4].rearrange("p q r -> p (q r)"), start=True, stop=False)
                pe.matmul(bk[:, :], ones, later[:, half, 4 * q:4 * q + 4].rearrange("p q r -> p (q r)"), start=False, stop=True).then_inc(sa_g, 1)
            for half in range(2):
                for pp in range(8):
                    if pp % 2 == 0:
                        pe.wait_ge(sa_w, 4 * half + pp // 2 + 1)
                    rows = [arrived("av", 4 * half + pp // 2, 4 * (pp % 2) + b4) for b4 in range(4)]
                    for j in range(2):
                        for c in range(2):
                            for b4 in range(4):
                                r = slice(32 * b4, 32 * b4 + 32)
                                mm = pe.matmul(bank[2 * half + c][r, :], z_t[:, half, 2 * pp + j, r],
                                               rows[b4][:, 1024 * j + 512 * c:1024 * j + 512 * c + 512],
                                               start=(pp == 0 and j == 0), stop=(pp == 7 and j == 1))
                                if j == 1 and c == 1:
                                    mm.then_inc(item_used, 1)
                        prompt_piece(16 * half + 2 * pp + j)
            stick_values(1)
            pe.wait_ge(pa_out, 8)
            for half in range(2):
                pe.wait_ge(o_a_in, 2 * half + 2)
                for c in range(2):
                    for j in range(4):
                        mm = pe.transpose(bank[4 + 2 * half + c][:, P * j:P * j + P], o_a[:, half, c, P * j:P * j + P], ident)
                    mm.then_inc(o_a_t, 1)
            pe.wait_ge(mix_a, 16)

            def fold_out(n):
                pe.wait_ge(parts_in, n + 1)
                pe.matmul(bank[6 + n % 2][0:NSMP, :], const["fold"], out_parts[n % 2], start=True, stop=True).then_inc(folded_out, 1)

            for it in range(2):
                for k in range(8):
                    n, kq = (8 * it + k) // 4, k % 4
                    w = arrived("wo", it, k).rearrange("p (k c) -> p k c", k=4)
                    if kq == 0 and n >= 2:
                        pe.wait_ge(wo_evac, 3 * (n - 1))
                    for kt in range(4):
                        for tt in range(2):
                            pe.matmul(bank[3 * (n % 2) + tt][:, :], mix_t[:, 4 * kq + kt, P * tt:P * tt + P], w[:, kt, :],
                                      start=(kq == 0 and kt == 0), stop=(kq == 3 and kt == 3))
                    for kt in range(4):
                        mm = pe.matmul(bank[3 * (n % 2) + 2][32 * kt:32 * kt + 32, :], mix_t[:, 4 * kq + kt, PTOK:T], w[:, kt, :],
                                       start=(kq == 0), stop=(kq == 3))
                    mm.then_inc(item_used, 1)
                    if kq == 0 and n:
                        fold_out(n - 1)
            fold_out(3)
            for tt in range(3):
                n = rows_of[tt]
                pe.wait_ge(h_in, tt + 1)
                for c in range(4):
                    if 4 * tt + c >= 2:
                        pe.wait_ge(h_t_in, 4 * tt + c - 1)
                    for j in range(4):
                        kt = 4 * c + j
                        mm = pe.transpose(bank[6 + c % 2][:, P * j:P * j + n], h_nat[0:n, tt, P * kt:P * kt + P], ident[0:n, 0:n])
                    mm.then_inc(h_turned, 1)
            pe.wait_ge(h_t_in, 12)
            pe.wait_ge(sub_in, 16)

            def score(m):
                pe.wait_ge(q_in, m + 1)
                if m >= 2:
                    pe.wait_ge(s_in, 3 * (m - 1))
                for tt in range(3):
                    n = rows_of[tt]
                    mm = pe.matmul(bank[2 + m % 2][0:n, P * tt:P * tt + P], q_t[:, m, P * tt:P * tt + n], sub_keys[:, m % 2, :],
                                   start=True, stop=True, skip_group_check=True)
                mm.then_inc(s_mm, 1)

            for m in range(16):
                w = arrived("wq", m // 8, m % 8)
                if m >= 2:
                    pe.wait_ge(q_in, m - 1)
                for kt in range(KT):
                    mm = pe.matmul(bank[m % 2][:, 0:T], w[:, P * kt:P * kt + P], h_t[:, kt, :], start=(kt == 0), stop=(kt == KT - 1))
                mm.then_inc(item_used, 1)
                if m:
                    score(m - 1)
            score(15)
            pe.wait_ge(s_in, 48)
            pe.wait_ge(chosen, 1)
            pe.sem_inc(v_used, 4)

            def value_rows(r, tt, it_r):
                n = rows_of[tt]
                banks = bank[4 * (tt % 2):4 * (tt % 2) + 4]
                for j in range(16):
                    pe.wait_ge(v_full[j % 4], 16 * (4 * r + j // 4 + 1))
                    pe.wait_ge(diag_in, 32 + 16 * r + j + 1)
                    for c in range(4):
                        out = banks[c][0:n, :] if tt < 2 else bank[0][32 * c:32 * c + 32, :]
                        mm = pe.matmul(out, diag[j % 4][:, 0:n], v_ring[j % 4][:, 512 * c:512 * c + 512], start=False, stop=True,
                                       skip_group_check=True)
                    mm.then_inc(v_used, 1)

            def open_banks(tt):
                n = rows_of[tt]
                for c in range(4):
                    pe.matmul(bank[4 * (tt % 2) + c][0:n, :], zeros[:, 0:n], h_nat[:, 0, 512 * c:512 * c + 512] if tt == 0 else norm[:, 2, 512 * c:512 * c + 512],
                              start=True, stop=True, skip_group_check=True)

            for tt in range(2):
                open_banks(tt)
                with pe.Fori(4 * tt, 4 * tt + 4) as it:
                    for par in range(2):
                        value_rows(2 * it + par, tt, None)
            pe.wait_ge(tile_out, 1)
            pe.matmul(bank[0][:, :], zeros, norm[:, 2, 0:512], start=True, stop=True, skip_group_check=True)
            for par in range(2):
                value_rows(16 + par, 2, None)

        @block.vector
        def _(dve):
            ch = Chain(dve, dve_step)
            dve.wait_ge(w1_in, 48)
            for kv in range(2):
                for q in range(4):
                    ls = slice(8 * q, 8 * q + 8)
                    ch.do(dve.tensor_tensor(pe_prod, w1[:, kv, ls, :], cmp_pe[:, kv, ls, None].to_broadcast([P, 8, P]), ALU.mult))
                    ch.do(dve.tensor_reduce(pe_quarter[:, q], pe_prod.rearrange("p l e -> p e l"), AX.X, ALU.add))
                ins = dve.tensor_reduce(pe_part[:, kv], pe_quarter.rearrange("p q e -> p e q"), AX.X, ALU.add)
                ch.do(ins) if kv == 0 else ch.tell(ins, bias_part, 1)
            dve.wait_ge(consts_in, 16)
            dve.wait_ge(rope_in, 16)
            for n, m in enumerate(ROPED):
                dve.wait_ge(swapped, n + 1)
                ch.do(dve.tensor_tensor(rope_tmp[:, n % 2], bank[2 + n % 2][:, 0:T], rope[:, 1, :], ALU.mult))
                ch.do(dve.tensor_tensor(proj[:, m, :], proj[:, m, :], rope[:, 0, :], ALU.mult))
                ch.tell(dve.tensor_tensor(proj[:, m, :], proj[:, m, :], rope_tmp[:, n % 2], ALU.add), roped, n + 1)
            dve.wait_ge(gate_turned, 1)
            ch.do(dve.tensor_scalar_add(smp_gate_tok[0:NSMP], bank[0][0:NSMP, 48:72], 1.0))
            ch.tell(dve.reciprocal(smp_gate_tok[0:NSMP], smp_gate_tok[0:NSMP]), gate_tok, 1)
            ch.do(dve.tensor_scalar_add(gate_tmp, bank[0][:, 0:48].rearrange("p (a b) -> p a b", a=2), 1.0))
            ch.do(dve.reciprocal(prompt_gate, gate_tmp))
            dve.wait_ge(gate_rows, 1)
            for h in range(2):
                own = gate_tmp[:, h].rearrange("p (h b) -> p h b", b=3)
                ch.do(dve.tensor_tensor(own, bank[1][:, 24 * h:24 * h + 24].rearrange("p (h b) -> p h b", b=3),
                                        const["head_row"][:, :, None].to_broadcast([P, NH, 3]), ALU.mult))
                ch.do(dve.tensor_reduce(smp_gate[:, h], gate_tmp[:, h].rearrange("p (h b) -> p b h", b=3), AX.X, ALU.add))
            dve.wait_ge(v_turned, 1)
            dve.wait_ge(bias_ready, 1)
            ch.do(dve.memset(v_new, 0.0))
            for n in range(3):
                dve.tensor_copy(v_new[0:NSMP, 4 * n:4 * n + 4, :],
                                bank[5 + n][0:NSMP, :].rearrange("p (a b) -> p a b", a=4)).then_inc(v_new_in, 1)
            dve.tensor_copy(pe_bias, bank[4][:, 0:2]).then_inc(bias_sb, 1)
            for kv in range(2):
                src = proj[:, KC + 2 * kv:KC + 2 * kv + 2, 0:NPROMPT].rearrange("p g (c l) -> p l g c", l=16)
                dve.tensor_copy(rows_c[:, kv].rearrange("p l (g c) -> p l g c", g=NG), src).then_inc(pc_rows, 1)
            dve.wait_ge(bias_sb, 1)
            ch.do(dve.memset(h_cmp[0], 0.0))
            ch.do(dve.memset(h_cmp[1], 0.0))
            dve.sem_inc(ab_free, 2)

            def gelu(x, u, e, h, arg, exp, out, done):
                ch.do(dve.tensor_tensor(u, x, x, ALU.mult))
                ch.do(dve.tensor_scalar(u, u, GELU_A, 1.0, ALU.mult, ALU.add))
                ch.tell(dve.tensor_tensor(u, u, x, ALU.mult), arg, done)
                dve.wait_ge(exp, done)
                ch.do(dve.tensor_scalar_add(e, e, 1.0))
                ch.do(dve.reciprocal(e, e))
                ch.tell(dve.tensor_tensor(h, x, e, ALU.mult), out, done)

            with ch.rounds(4, 28) as it:
                for st in range(4):
                    kv = st % 2
                    ab = bank[2 + kv]
                    a = ab[:, 0:256].rearrange("p (q g j) -> p q g j", g=NG, j=8)
                    b = x_cmp.rearrange("p (q g j) -> p q g j", g=NG, j=8)
                    h = h_cmp[kv].rearrange("p (g q j) -> p q g j", g=NG, j=8)
                    dve.wait_ge(item_used, stream.used("cmp", it, 2 * st + 1))
                    dve.wait_ge(cmp_mm, 4 * it + st + 1)
                    ch.do(dve.tensor_copy(x_cmp, ab[:, 256:512]))
                    ch.do(dve.tensor_tensor(h[:, :, :, 0:7], a[:, :, :, 0:7], b[:, :, :, 1:8], ALU.add))
                    ch.tell(dve.tensor_tensor(h[:, 0:15, :, 7], a[:, 0:15, :, 7], b[:, 1:16, :, 0], ALU.add), ab_free,
                            4 * it + st + 3)
                    ch.do(dve.tensor_scalar(x_cmp, h_cmp[kv], pe_bias[:, kv:kv + 1], None, ALU.add))
                    gelu(x_cmp, u_cmp, e_cmp, h_cmp[kv], gelu_arg, gelu_exp, gelu_out, 4 * it + st + 1)
            dve.wait_ge(cmp_mm, 2 + 16)
            ch.do(dve.memset(h_cmp[0][:, 0:64], 0.0))
            dve.wait_ge(pc_turned, 1)
            for kv in range(2):
                at = 64 * kv
                a = bank[7][:, at:at + 32].rearrange("p (g c) -> p g c", g=NG)
                b = x_cmp[:, 0:32].rearrange("p (g c) -> p g c", g=NG)
                h = h_cmp[0][:, 32 * kv:32 * kv + 32].rearrange("p (g c) -> p g c", g=NG)
                ch.do(dve.tensor_copy(x_cmp[:, 0:32], bank[7][:, at + 32:at + 64]))
                ch.do(dve.tensor_tensor(h[:, :, 0:NCP], a[:, :, 0:NCP], b[:, :, 1:NCP + 1], ALU.add))
            for kv in range(2):
                ch.do(dve.tensor_scalar(x_cmp[:, 32 * kv:32 * kv + 32], h_cmp[0][:, 32 * kv:32 * kv + 32], pe_bias[:, kv:kv + 1], None, ALU.add))
            gelu(x_cmp[:, 0:64], u_cmp[:, 0:64], e_cmp[:, 0:64], h_cmp[0][:, 0:64], gelu_arg, gelu_exp, gelu_out, 17)
            dve.wait_ge(pc_mm, 1)
            ch.tell(dve.memset(p_slc_t[:, 16], 0.0), padded, 1)
            ch.do(dve.memset(q_pad, 0.0))
            for g in range(NG):
                dst = q_pad[:, :, g, 16 * g:16 * g + 16].rearrange("p b (h t) -> p b h t", t=NT)
                src = proj[:, QB + HPG * g:QB + HPG * g + HPG, PTOK:T].rearrange("p h (b t) -> p b h t", t=NT)
                ins = dve.tensor_copy(dst, src)
                ch.do(ins) if g == 0 else ch.tell(ins, q_pad_in, 1)
            for h in range(2):
                dve.wait_ge(cmp_scored, h + 1)
                ch.do(dve.tensor_reduce(soft[:, h:h + 1], bank[h][:, 0:NCS], AX.X, ALU.max))
                ch.tell(dve.tensor_scalar(soft[:, 2 + h:3 + h], soft[:, h:h + 1], -SCALE, None, ALU.mult), cmp_neg, h + 1)
            dve.wait_ge(cmp_exp, 2)
            ch.do(dve.tensor_scalar_max(soft[:, 4:6], soft[:, 4:6], 1e-30))
            ch.do(dve.reciprocal(soft[:, 4:6], soft[:, 4:6]))
            for h in range(2):
                ch.tell(dve.tensor_scalar(s_cmp[:, h, 0:NCS], s_cmp[:, h, 0:NCS], soft[:, 4 + h:5 + h], None, ALU.mult), cmp_p, h + 1)
            dve.wait_ge(imp_ready, 1)
            ch.tell(dve.tensor_copy(imp, bank[3][:, 0:2 * NSEL].rearrange("p (h n) -> p h n", h=2)), imp_in, 1)
            ch.do(dve.memset(imp[:, :, 0:1], FORCE))
            ch.do(dve.memset(imp[:, :, NSEL - 2:NSEL], FORCE))
            for h in range(2):
                other = imp[:, h, None, :].to_broadcast([P, NSEL, NSEL])
                own = imp[:, h, :, None].to_broadcast([P, NSEL, NSEL])
                ch.do(dve.tensor_tensor(above, other, own, ALU.is_gt))
                ch.do(dve.tensor_tensor(ties, other, own, ALU.is_equal))
                ch.do(dve.tensor_tensor(ties, ties, const["lower"].rearrange("p (a b) -> p a b", a=NSEL), ALU.mult))
                ch.do(dve.tensor_tensor(above, above, ties, ALU.add))
                ch.do(dve.tensor_reduce(rank[:, h], above, AX.X, ALU.add))
            ch.do(dve.tensor_scalar(sel_add, rank, NTOP - 0.5, NEG, ALU.is_gt, ALU.mult))
            for h in range(2):
                dve.wait_ge(cmp_sum, 1)
                ch.tell(dve.tensor_scalar(s_cmp[:, h, 0:NCS], s_cmp[:, h, 0:NCS], smp_gate[:, h, 0:1], None, ALU.mult), cmp_pg, h + 1)

            def slc_out(h):
                for ph in range(2):
                    dve.wait_ge(item_used, stream.used("ks", h, 4 * ph + 3))
                    for c in range(2):
                        at = 1024 * ph + 512 * c
                        add = sel_add[:, h, at // SEL_BLOCK:at // SEL_BLOCK + 8, None].to_broadcast([P, 8, SEL_BLOCK])
                        ch.tell(dve.tensor_tensor(s_slc[:, h, at:at + 512].rearrange("p (a b) -> p a b", a=8),
                                                  bank[4 + 2 * ph + c][:, :].rearrange("p (a b) -> p a b", a=8), add, ALU.add),
                                slc_evac, 4 * h + 2 * ph + c + 1)

            slc_out(0)
            slc_out(1)
            new_add = const["new_add"].rearrange("p (h n) -> p h n", h=2)
            dve.wait_ge(new_scored, 1)
            for h in range(2):
                for n, s in enumerate((s_slc[:, h, PAST:], s_win[:, h, WIN:])):
                    ch.tell(dve.tensor_tensor(s, bank[3][:, 64 * n + 32 * h:64 * n + 32 * h + 32], new_add[:, h], ALU.add),
                            new_evac, 2 * h + n + 1)
            ch.tell(dve.memset(p_win_t[:, 4], 0.0), padded, 2)
            for h in range(2):
                dve.wait_ge(item_used, stream.used("kw", 0, 2 * h + 1))
                ch.tell(dve.tensor_copy(s_win[:, h, 4:WIN], bank[h][:, 4:WIN]), win_evac, 2 * h + 1)
                ch.tell(dve.tensor_tensor(s_win[:, h, 0:4], bank[h][:, 0:4], const["win_add"], ALU.add), win_evac, 2 * h + 2)
            for h in range(2):
                for n, s in enumerate((s_slc, s_win)):
                    ch.do(dve.tensor_reduce(soft[:, 16:17], s[:, h], AX.X, ALU.max))
                    ch.tell(dve.tensor_scalar(soft[:, 8 + 2 * n + h:9 + 2 * n + h], soft[:, 16:17], -SCALE, None, ALU.mult),
                            soft_neg, 2 * h + n + 1)
            for h in range(2):
                for n, s in enumerate((s_slc, s_win)):
                    dve.wait_ge(soft_exp, 2 * h + n + 1)
                    f = soft[:, 12 + 2 * n + h:13 + 2 * n + h]
                    ch.do(dve.tensor_scalar_max(f, f, 1e-30))
                    ch.do(dve.reciprocal(f, f))
                    ch.do(dve.tensor_tensor(f, f, smp_gate[:, h, 1 + n:2 + n], ALU.mult))
                    ch.tell(dve.tensor_scalar(s[:, h], s[:, h], f, None, ALU.mult), soft_p, 2 * h + n + 1)
            dve.wait_ge(item_used, stream.used("vw", 0, 3))
            ch.tell(dve.tensor_copy(o_nsa, bank[7][:, :].rearrange("p (h n) -> p h n", h=2)), o_nsa_in, 1)
            dve.wait_ge(o_nsa_t, 1)
            for h in range(2):
                for g in range(NG):
                    src = bank[h][:, P * g:P * g + P].rearrange("p (b g h t) -> p g h b t", b=4, g=NG, h=HPG)[:, g]
                    dst = mix_t[:, NH + HPG * g:NH + HPG * g + HPG, PTOK + 16 * h:PTOK + 16 * h + 16].rearrange("p h (b t) -> p h b t", t=NT)
                    ch.tell(dve.tensor_copy(dst, src), mix_nsa, 2 * h + g + 1)

            causal = const["causal"]
            cmp_add = const["cmp_add"].rearrange("p (q n) -> p q n", q=2)
            cmp_mul = const["cmp_mul"].rearrange("p (q n) -> p q n", q=2)
            strict = const["strict"][:, None, None, :].to_broadcast([P, 4, 2, P])

            def diagonal(t):
                return t.rearrange("p h (a n) -> p h a n", a=3)[:, :, 0:3:2, :]

            def prompt_dve():
                for u in range(8):
                    qt, g, h0 = prompt_unit(u)
                    nk = P * (qt + 1)
                    dve.wait_ge(pb_scored, u + 1)
                    for i in range(2):
                        src = bank[4 + i][:, :].rearrange("p (r k) -> p r k", r=2)[:, :, 0:nk]
                        ch.do(dve.tensor_tensor(s_pr[:, i, :, 0:nk], src, causal[:, None, 2 * P - nk:].to_broadcast([P, 2, nk]), ALU.add))
                    src = bank[6][:, 0:32].rearrange("p (h n) -> p h n", n=16)[:, :, 0:NCP]
                    sc = s_prc[:, :, 0:NCP]
                    ch.do(dve.tensor_tensor(sc, src, cmp_add[:, qt, None, :].to_broadcast([P, 2, NCP]), ALU.add))
                    ch.do(dve.tensor_reduce(pr_max[:, 0:4].rearrange("p (a b) -> p a b", a=2), s_pr[:, :, :, 0:nk], AX.X, ALU.max))
                    ch.tell(dve.tensor_scalar(pr_max[:, 0:4], pr_max[:, 0:4], -SCALE, None, ALU.mult), pb_neg, u + 1)
                    ch.do(dve.tensor_reduce(pr_max[:, 4:6], sc, AX.X, ALU.max))
                    ch.tell(dve.tensor_tensor(sc, sc, pr_max[:, 4:6, None].to_broadcast([P, 2, NCP]), ALU.subtract), pb_negc, u + 1)
                    dve.wait_ge(pb_exp, 5 * u + 5)
                    ch.do(dve.tensor_tensor(sc, sc, cmp_mul[:, qt, None, :].to_broadcast([P, 2, NCP]), ALU.mult))
                    ch.do(dve.tensor_reduce(pr_sum[:, 4:6], sc, AX.X, ALU.add))
                    ch.do(dve.tensor_scalar_max(pr_sum, pr_sum, 1e-30))
                    ch.do(dve.reciprocal(pr_sum, pr_sum))
                    at = 3 * (HPG * g + h0)
                    gate = prompt_gate[:, qt, at:at + 6].rearrange("p (h b) -> p h b", b=3)
                    f = pr_sum[:, 0:4].rearrange("p (h b) -> p h b", b=2)
                    ch.do(dve.tensor_tensor(f, f, gate[:, :, 1:3], ALU.mult))
                    ch.do(dve.tensor_tensor(pr_sum[:, 4:6], pr_sum[:, 4:6], gate[:, :, 0], ALU.mult))
                    sv = s_pr.rearrange("p h b n -> p (h b) n")[:, :, 0:nk]
                    ch.tell(dve.tensor_tensor(sv, sv, pr_sum[:, 0:4, None].to_broadcast([P, 4, nk]), ALU.mult), pb_p, 2 * u + 1)
                    ch.tell(dve.tensor_tensor(sc, sc, pr_sum[:, 4:6, None].to_broadcast([P, 2, NCP]), ALU.mult), pb_p, 2 * u + 2)
                    dve.wait_ge(pb_pv, u + 1)
                    at = NH + HPG * g + h0
                    ch.tell(dve.tensor_copy(mix_t[:, at:at + 2, P * qt:P * qt + P], bank[7][:, 0:2 * P].rearrange("p (a b) -> p a b", a=2)),
                            pb_out, u + 1)
                for u in range(2):
                    dve.wait_ge(pa_z_in, 4 * u + 4)
                    ch.tell(dve.scalar_tensor_tensor(out=e_pr, in0=z_pr, scalar=-1.0, in1=z_pr, op0=ALU.mult, op1=ALU.min), pa_neg, u + 1)
                    dve.wait_ge(pa_log, u + 1)
                    ch.do(dve.scalar_tensor_tensor(out=sp_pr, in0=z_pr, scalar=0.0, in1=e_pr, op0=ALU.max, op1=ALU.add))
                    ch.tell(dve.tensor_tensor(diagonal(sp_pr), diagonal(sp_pr), strict, ALU.mult), pa_sp, u + 1)
                    for j in range(4):
                        dve.wait_ge(pa_g, 4 * u + j + 1)
                        ch.tell(dve.tensor_tensor(z_pr[:, j], z_pr[:, j], bank[4 + j][:, 0:3 * P], ALU.subtract), pa_arg, 4 * u + j + 1)
                    dve.wait_ge(pa_exp, u + 1)
                    ch.tell(dve.tensor_tensor(diagonal(z_pr), diagonal(z_pr), strict, ALU.mult), pa_w, u + 1)
                    for j in range(4):
                        dve.wait_ge(pa_pv, 4 * u + j + 1)
                        dve.tensor_copy(mix_t[:, 4 * u + j, 0:NPROMPT], bank[4 + j][:, 0:NPROMPT]).then_inc(pa_out, 1)

            dve.wait_ge(mix_nsa, 4)
            ch.do(dve.memset(sp_new, 0.0))
            dve.wait_ge(sn_z_in, 1)
            zn, en, sn = z_new[0:NSMP], e_new[0:NSMP], sp_new[0:NSMP]
            seen = const["new_sb"][0:NSMP, None, :].to_broadcast([NSMP, NH, NSMP])
            ch.tell(dve.scalar_tensor_tensor(out=en, in0=zn, scalar=-1.0, in1=zn, op0=ALU.mult, op1=ALU.min), sn_neg, 1)
            dve.wait_ge(sn_log, 1)
            ch.do(dve.scalar_tensor_tensor(out=sn, in0=zn, scalar=0.0, in1=en, op0=ALU.max, op1=ALU.add))
            ch.tell(dve.tensor_tensor(sn, sn, seen, ALU.mult), sn_sp, 1)
            dve.wait_ge(sn_g, 1)
            ch.tell(dve.tensor_tensor(zn, zn, bank[1][0:NSMP, 0:256].rearrange("p (h n) -> p h n", h=NH), ALU.subtract), sn_arg, 1)
            dve.wait_ge(sn_exp, 1)
            ch.tell(dve.tensor_tensor(zn, zn, seen, ALU.mult), sn_w, 1)
            dve.wait_ge(sn_pv, 1)
            ch.tell(dve.tensor_copy(mix_t[:, 0:NH, PTOK:T], bank[2][:, 0:256].rearrange("p (h n) -> p h n", h=NH)), sn_out, 1)
            dve.sem_inc(z_t_in, 2)
            ch.do(dve.memset(q_pad_a, 0.0))
            for half in range(2):
                if half:
                    dve.wait_ge(item_used, stream.used("ak", 3, 7))
                for h in range(NH):
                    src = proj[:, QA + h, PTOK + 16 * half:PTOK + 16 * half + 16].rearrange("p (b t) -> p b t", t=NT)
                    ins = dve.tensor_copy(q_pad_a[:, :, h, NT * h:NT * h + NT], src)
                    ch.do(ins) if h < NH - 1 else ch.tell(ins, q_pad_a_in, half + 1)
                with dve.Fori(2 * half, 2 * half + 2) as it:
                    for k in range(2):
                        dve.wait_ge(z_turned, 2 * it + k + 1)
                        dst = z_t.rearrange("p a q r -> p (a q) r")[:, bass.ds(8 * it + 4 * k, 4), :]
                        ch.tell(dve.tensor_copy(dst, bank[5 + k][:, :].rearrange("p (q r) -> p q r", q=4)), z_t_in, 2 * it + k + 3)
                z, e, s, lt = z_t[:, half], e_t[:, half], sp_t[:, half], later[:, half]
                ch.tell(dve.scalar_tensor_tensor(out=e, in0=z, scalar=-1.0, in1=z, op0=ALU.mult, op1=ALU.min), sa_neg, half + 1)
                dve.wait_ge(sa_log, half + 1)
                ch.do(dve.scalar_tensor_tensor(out=s, in0=z, scalar=0.0, in1=e, op0=ALU.max, op1=ALU.add))
                ch.do(dve.tensor_copy(lt[:, NPAGE - 1].rearrange("p (b h t) -> p h b t", b=4, h=NH),
                                      sp_new[:, :, 16 * half:16 * half + 16].rearrange("p h (b t) -> p h b t", t=NT)))
                for q in range(NPAGE - 2, -1, -1):
                    ins = dve.tensor_tensor(lt[:, q], lt[:, q + 1], s[:, q + 1], ALU.add)
                    ch.do(ins) if q else ch.tell(ins, sa_later, half + 1)
            for n in range(8):
                dve.wait_ge(sa_g, n + 1)
                zz = z_t[:, n // 4, 4 * (n % 4):4 * (n % 4) + 4]
                dve.tensor_tensor(zz, zz, bank[4 + n % 4][:, :].rearrange("p (q r) -> p q r", q=4), ALU.subtract).then_inc(sa_arg, 1)
            prompt_dve()
            for half in range(2):
                for h in range(NH):
                    if h % 4 == 0:
                        dve.wait_ge(o_a_t, 2 * half + h // 4 + 1)
                    rows = mix_t[:, h, PTOK + 16 * half:PTOK + 16 * half + 16].rearrange("p (b t) -> p b t", t=NT)
                    own = bank[4 + 2 * half + h // 4][:, P * (h % 4):P * (h % 4) + P].rearrange("p (b h t) -> p b h t", b=4, h=NH)[:, :, h]
                    dve.tensor_tensor(rows, rows, own, ALU.add).then_inc(mix_a, 1)

            dve.wait_ge(tok_in, 32)
            for n in range(4):
                dve.wait_ge(item_used, stream.used("wo", n // 2, 4 * (n % 2) + 3))
                for tt in range(3):
                    r = rows_of[tt]
                    src = bank[3 * (n % 2) + tt][:, :] if tt < 2 else bank[6 + n % 2][0:NSMP, :]
                    if tt == 2:
                        dve.wait_ge(folded_out, n + 1)
                    hh = h_nat[0:r, tt, 512 * n:512 * n + 512]
                    ch.tell(dve.scalar_tensor_tensor(out=hh, in0=hh, scalar=ALPHA, in1=src, op0=ALU.mult, op1=ALU.add,
                                                     accum_out=ln[0:r, 20 + 4 * tt + n:21 + 4 * tt + n]), wo_evac, 3 * n + tt + 1)
            dve.wait_ge(norm_in, 64)

            def norm_mean(n, tt, c):
                ch.do(dve.tensor_reduce(ln[0:n, 4 + tt:5 + tt], ln[0:n, 20 + 4 * tt:24 + 4 * tt], AX.X, ALU.add))
                ch.tell(dve.tensor_scalar(ln[0:n, 8 + tt:9 + tt], ln[0:n, 4 + tt:5 + tt], -1.0 / DM, None, ALU.mult), ln_mu, c)

            def norm_var(n, tt, c):
                dve.wait_ge(ln_sq, c)
                v = ln[0:n, 12 + tt:13 + tt]
                ch.tell(dve.tensor_scalar(v, v, 1.0 / DM, EPS, ALU.mult, ALU.add), ln_var, c)

            def norm_scale(n, tt, gain, c, done, count):
                x, sd, mu = h_nat[0:n, tt, :], ln[0:n, 16 + tt:17 + tt], ln[0:n, 8 + tt:9 + tt]
                dve.wait_ge(ln_sd, c)
                ch.do(dve.reciprocal(sd, sd))
                ch.do(dve.scalar_tensor_tensor(out=x, in0=x, scalar=mu, in1=norm[0:n, gain, :], op0=ALU.add, op1=ALU.mult))
                ch.tell(dve.scalar_tensor_tensor(out=x, in0=x, scalar=sd, in1=norm[0:n, gain + 1, :], op0=ALU.mult, op1=ALU.add), done, count)

            for tt in range(3):
                norm_mean(rows_of[tt], tt, tt + 1)
            for tt in range(3):
                norm_var(rows_of[tt], tt, tt + 1)
            for tt in range(3):
                norm_scale(rows_of[tt], tt, 0, tt + 1, h_in, tt + 1)

            def top16(n, values, s, i):
                ch.do(dve.max(s[:, 0:8], values))
                ch.do(dve.max_index(i[:, 0:8], s[:, 0:8], values))
                w = work[0:n, 0:values.shape[-1]]
                ch.do(dve.match_replace(w, s[:, 0:8], values, -3.0e38))
                ch.do(dve.max(s[:, 8:16], w))
                ch.do(dve.max_index(i[:, 8:16], s[:, 8:16], w))

            def head_topk(tt, h):
                n = rows_of[tt]
                for m in (2 * h, 2 * h + 1):
                    dve.wait_ge(s_in, 3 * m + tt + 1)
                    top16(n, s_key[tt][0:n, m, :], top_s[0:n, tt, m, :], top_i[0:n, tt, m, :])
                ch.do(dve.tensor_tensor(cand[0:n].rearrange("p (a b) -> p a b", a=16),
                                        top_s[0:n, tt, 2 * h, :, None].to_broadcast([n, 16, 16]),
                                        top_s[0:n, tt, 2 * h + 1, None, :].to_broadcast([n, 16, 16]), ALU.add))
                top16(n, cand[0:n], best_s[0:n, tt, 16 * h:16 * h + 16], best_j[0:n, tt, 16 * h:16 * h + 16])

            def experts_of(tt, p):
                n = rows_of[tt]
                at = slice(32 * p, 32 * p + 32)
                bs = best_s[0:n, tt, at].rearrange("p (h k) -> p h k", h=2)
                ch.do(dve.tensor_copy(f_a[0:n, 0:2], bs[:, :, 0]))
                ch.tell(dve.tensor_tensor(bs, bs, f_a[0:n, 0:2, None].to_broadcast([n, 2, 16]), ALU.subtract), gate_arg, 4 * tt + p + 1)
                ch.do(dve.tensor_single_scalar(j_a[0:n, at], best_j[0:n, tt, at], 4, ALU.logical_shift_right))
                ch.do(dve.tensor_single_scalar(j_b[0:n, at], best_j[0:n, tt, at], 15, ALU.bitwise_and))
                ch.do(dve.tensor_copy(f_a[0:n, at], j_a[0:n, at]))
                ch.do(dve.tensor_copy(f_b[0:n, at], j_b[0:n, at]))
                ch.do(dve.tensor_copy(top_f[0:n, 4 * p:4 * p + 4], top_i[0:n, tt, 4 * p:4 * p + 4]))
                for f, i, c in ((f_a, i_a, 0), (f_b, i_b, 1)):
                    oh = one_hot[0:n]
                    ch.do(dve.tensor_tensor(oh, f[0:n, at, None].to_broadcast([n, 32, 16]),
                                            const["iota16"][0:n, None, :].to_broadcast([n, 32, 16]), ALU.is_equal))
                    for h in range(2):
                        keys = top_f[0:n, 4 * p + 2 * h + c, None, :].to_broadcast([n, 16, 16])
                        ch.do(dve.tensor_tensor(oh[:, 16 * h:16 * h + 16], oh[:, 16 * h:16 * h + 16], keys, ALU.mult))
                    ch.do(dve.tensor_reduce(i[0:n, at], oh, AX.X, ALU.add))
                ex = expert[:, P * tt + 32 * p:P * tt + 32 * p + 32] if tt < 2 else expert_s[0:n, at]
                ins = dve.scalar_tensor_tensor(out=ex, in0=i_a[0:n, at], scalar=float(P), in1=i_b[0:n, at], op0=ALU.mult, op1=ALU.add)
                ch.tell(ins, chosen, 4 * tt + p + 1) if tt < 2 else ch.do(ins)

            def gates_of(tt, p):
                n = rows_of[tt]
                at = slice(32 * p, 32 * p + 32)
                bs = best_s[0:n, tt, at].rearrange("p (h k) -> p h k", h=2)
                gt = peer_gate[:, P * tt + 32 * p:P * tt + 32 * p + 32] if tt < 2 else gate_s[0:n, at]
                dve.wait_ge(gate_e, 4 * tt + p + 1)
                ch.do(dve.tensor_reduce(soft_sum[0:n, 0:2], bs, AX.X, ALU.add))
                ch.do(dve.reciprocal(soft_sum[0:n, 0:2], soft_sum[0:n, 0:2]))
                ch.do(dve.tensor_tensor(gt.rearrange("p (h k) -> p h k", h=2), bs, soft_sum[0:n, 0:2, None].to_broadcast([n, 2, 16]), ALU.mult))

            def fold_samples():
                for q in range(4):
                    r = slice(32 * q, 32 * q + 32)
                    ch.do(dve.tensor_copy(expert[r, 256:288], expert_s[0:NSMP, 32 * q:32 * q + 32]))
                    ch.do(dve.tensor_copy(peer_gate[r, 256:288], gate_s[0:NSMP, 32 * q:32 * q + 32]))
                    ins = dve.tensor_copy(h_rep[r], h_nat[0:NSMP, 2, :])
                    ch.do(ins) if q < 3 else ch.tell(ins, chosen, 9)

            ch.do(dve.memset(zeros, 0.0))
            head_topk(0, 0)
            head_topk(0, 1)
            experts_of(0, 0)

            dve.sem_inc(u_used, 4)

            def slots(r, par, x, between={}, experts_at=None):
                for j in range(16):
                    dve.wait_ge(u_full[j % 4], 16 * (4 * r + j // 4 + 1))
                    dve.tensor_tensor_reduce(out=u_ring[j % 4], in0=u_ring[j % 4], in1=x, scale=1.0, scalar=0.0, op0=ALU.mult, op1=ALU.add,
                                             accum_out=act16[:, par, j:j + 1]).then_inc(u_used, 1)
                    for tt, h in between.get(j, ()):
                        head_topk(tt, h)
                        if tt == 0 and h % 2:
                            experts_of(0, h // 2)
                            gates_of(0, h // 2 - 1)
                    if j == 3 and experts_at is not None:
                        for p in range(4):
                            experts_of(experts_at, p)
                dve.wait_ge(u_used, 4 + 16 * r + 16)
                a = act16[:, par]
                ch.do(dve.tensor_tensor(u16, a, a, ALU.mult))
                ch.do(dve.tensor_scalar(u16, u16, GELU_A, 1.0, ALU.mult, ALU.add))
                ch.tell(dve.tensor_tensor(u16, u16, a, ALU.mult), act_arg, r + 1)
                ch.do(dve.tensor_tensor(a, a, peer_gate[:, bass.ds(16 * r, 16)], ALU.mult))
                dve.wait_ge(act_e, r + 1)
                ch.do(dve.tensor_scalar_add(e16, e16, 1.0))
                ch.do(dve.reciprocal(e16, e16))
                dve.wait_ge(diag_in, 16 * r + 16)
                ch.tell(dve.tensor_tensor(w16[:, par], a, e16, ALU.mult), w_ready, r + 1)

            def finish(tt, c):
                n = rows_of[tt]
                for q in range(4):
                    hh = h_nat[0:n, tt, 512 * q:512 * q + 512]
                    y = bank[4 * tt + q][:, :] if tt < 2 else y_quarter[0:n, q]
                    if tt == 2:
                        ch.do(dve.tensor_copy(y, bank[0][32 * q:32 * q + 32, :]))
                    ins = dve.scalar_tensor_tensor(out=hh, in0=hh, scalar=ALPHA, in1=y, op0=ALU.mult, op1=ALU.add,
                                                   accum_out=ln[0:n, 20 + 4 * tt + q:21 + 4 * tt + q])
                    ch.do(ins) if q < 3 else ch.tell(ins, tile_out, tt + 1)
                norm_mean(n, tt, c)
                norm_var(n, tt, c)
                norm_scale(n, tt, 2, c, y_ready, tt + 1)

            for r in range(8):
                slots(r, r % 2, h_nat[:, 0, :], TOPK_IN.get(r, {}), GATES_IN.get(r))
                if r == 0:
                    gates_of(0, 3)
                if r in GATES_IN:
                    for p in range(4):
                        gates_of(GATES_IN[r], p)
            dve.wait_ge(s_mm, 16)
            fold_samples()
            with ch.rounds(4, 10) as it:
                for par in range(2):
                    slots(8 + 2 * it + par, par, h_nat[:, 1, :])
            slots(16, 0, h_rep)
            dve.wait_ge(v_used, 4 + 16 * 8)
            finish(0, 4)
            slots(17, 1, h_rep)
            dve.wait_ge(v_used, 4 + 16 * 16)
            finish(1, 5)
            dve.wait_ge(v_used, 4 + 16 * 18)
            finish(2, 6)

        @block.gpsimd
        def _(pool):
            pool.wait_ge(item_used, RING + 1)
            pool.dma_start(words(AT_CONST, NCONST), dram["consts"]).then_inc(consts_in, 16)
            pool.dma_start(w_gate, dram["w_gate"]).then_inc(wg_in, 16)
            pool.dma_start(rope, dram["rope"]).then_inc(rope_in, 16)
            pool.dma_start(w1, dram["cmp_w1"]).then_inc(w1_in, 16)
            pool.dma_start(cmp_w2, dram["cmp_w2"]).then_inc(w1_in, 16)
            pool.dma_start(cmp_pe, dram["cmp_pe"]).then_inc(w1_in, 16)
            pool.wait_ge(consts_in, 16)
            def hold(signal, value):
                pool.wait_ge(signal, value)
                pool.sem_inc(held, 1)

            pool.wait_ge(pages_in, 16)
            for name in ("ks", "vs"):
                selected_pages(pool, name, 1, lambda name, it, k: hold(item_used, stream.room(name, it, k)))

            pool.wait_ge(o_a_t, 4)
            pool.wait_ge(mix_a, 16)
            pool.dma_start(h_nat[:, 0:2, :], dram["tokens"][0:NPROMPT].rearrange("(t p) d -> p t d", p=P)).then_inc(tok_in, 16)
            pool.dma_start(h_nat[0:NSMP, 2, :], dram["tokens"][NPROMPT:T]).then_inc(tok_in, 16)
            for i in range(4):
                pool.dma_start(norm[:, i, :], dram["norms"][i:i + 1, :].to_broadcast([P, DM])).then_inc(norm_in, 16)
            pool.dma_start(sub_keys, dram["sub_keys"]).then_inc(sub_in, 16)
            pool.wait_ge(chosen, 1)
            pool.wait_ge(item_used, stream.used("wo", 1, 7))

            def indices(dst, r, par, n):
                pool.tensor_copy(dst[:, par], expert[:, bass.ds(16 * r, 16)]).then_inc(idx_in, 1)
                hold(idx_in, n)

            def gather(table, rows, idx, full, used, r, j):
                hold(used, 16 * r + j + 1)
                pool.indirect_dma_start(rows[j % 4], None, dram[table], bass.IndirectOffsetOnAxis(ap=idx, axis=0)).then_inc(full[j % 4], 16)

            def u_of(r, par, j):
                gather("peer_u", u_ring, idx_u[:, par, j:j + 1], u_full, u_used, r, j)

            def v_of(r, par, j):
                gather("peer_v", v_ring, idx_v[:, par, j:j + 1], v_full, v_used, r, j)

            def both(r, par):
                indices(idx_u, r, par, 2 * r)
                indices(idx_v, r - 1, 1 - par, 2 * r + 1)
                for j in range(16):
                    u_of(r, par, j)
                    v_of(r - 1, 1 - par, j)

            indices(idx_u, 0, 0, 1)
            for j in range(16):
                u_of(0, 0, j)
            pool.wait_ge(item_used, RING + stream.total)
            both(1, 1)
            pool.wait_ge(chosen, 4)
            for tt in range(2):
                with pool.Fori(1 + 3 * tt, 4 + 4 * tt) as it:
                    for par in range(2):
                        both(2 * it + par, par)
                pool.wait_ge(chosen, 8 + tt)
            for par in range(2):
                both(16 + par, par)
            indices(idx_v, 17, 1, 36)
            for j in range(16):
                v_of(17, 1, j)


def kernel(**inputs):
    import numpy as _np
    import concourse.bacc as _bacc
    from concourse import mybir as _mybir
    from concourse.bass_utils import run_bass_kernel_spmd as _run

    x = {k: _np.asarray(v) for k, v in inputs.items()}
    w = x["w_in"][0]
    n_pool = x["cache_a"].shape[1]
    tokens = _np.concatenate([x["x_prompt"].reshape(NPROMPT, DM), x["x_sample"].reshape(NSMP, DM)])
    by_tile = lambda a: a.reshape(KT, P, -1).transpose(1, 0, 2)
    ca, cn, sw = x["cache_a"][0], x["cache_nsa"][0], x["state_win"][0]
    arrays = {
        "tokens": tokens,
        "tokens_t": by_tile(tokens.T),
        "w_in": w[:, :NM * P].reshape(KT, P, NM, P).transpose(2, 1, 0, 3),
        "w_gate": by_tile(w[:, NM * P:]),
        "rope": rope_tables(),
        "consts": constants(),
        "pages": x["page_table"].reshape(1, -1),
        "a_k": ca[:, :, 0].transpose(0, 3, 2, 1).reshape(n_pool, P, NH * P),
        "a_v": ca[:, :, 1].reshape(n_pool, P, NH * P),
        "nsa_t": cn[:, :, 0:3].transpose(0, 2, 4, 3, 1).reshape(n_pool, 3, P, NG * P),
        "nsa_v": cn[:, :, 3].reshape(n_pool, P, NG * P),
        "win_k": sw[:, :, 0].transpose(0, 3, 2, 1).reshape(NB // 2, 2, P, NG * WIN).transpose(0, 2, 1, 3),
        "win_v": sw[:, :, 1].reshape(NB // 2, 2, 4, P, NG * P).transpose(0, 3, 1, 2, 4),
        "cmp_w1": _np.stack([x["cmp_w1_k"][0], x["cmp_w1_v"][0]]).transpose(2, 0, 1, 3),
        "cmp_w2": _np.stack([x["cmp_w2_k"][0], x["cmp_w2_v"][0]]).transpose(1, 0, 2),
        "cmp_pe": _np.stack([x["cmp_pe_k"][0], x["cmp_pe_v"][0]]).transpose(2, 0, 1),
        "w_out": x["w_out"][0].reshape(4, 4, P, 4, 512).transpose(3, 0, 2, 1, 4),
        "w_query": x["peer_w_query"][0].reshape(KT, P, 16, P).transpose(2, 1, 0, 3),
        "sub_keys": x["peer_sub_keys"][0].transpose(2, 0, 1),
        "norms": _np.stack([x[k][0] for k in ("ln1_g", "ln1_b", "ln2_g", "ln2_b")]),
        "peer_u": x["peer_u"][0],
        "peer_v": x["peer_v"][0],
    }
    arrays = {k: _np.ascontiguousarray(a) for k, a in arrays.items()}
    nc = _bacc.Bacc("TRN2", target_bir_lowering=False, num_devices=1)
    dram = {k: nc.dram_tensor("in_" + k, a.shape, _mybir.dt.from_np(a.dtype), kind="ExternalInput").ap()
            for k, a in arrays.items()}
    outs = {k: nc.dram_tensor(k, s, F32, kind="ExternalOutput").ap() for k, s in OUTS.items()}
    hybrid_step(nc, dram, outs)
    r = _run(nc, [{"in_" + k: a for k, a in arrays.items()}], core_ids=[0]).results[0]
    y, pa, pn = r["out_y"], r["out_a"], r["out_n"]
    kw, vw = r["out_win_k"], r["out_win_v"]
    rows_a = pa.transpose(2, 1, 0).reshape(T, 2, NH, HD)
    rows_n = pn.transpose(2, 1, 0)
    nsa = rows_n[:, :8].reshape(T, 4, NG, HD)
    new_win = rows_n[:, 8:].reshape(T, 2, NG, HD)
    old_k = kw.transpose(0, 2, 1, 3).reshape(NB, P, NG, WIN).transpose(0, 3, 2, 1)
    old_v = vw.transpose(0, 2, 3, 1, 4).reshape(NB, WIN, NG, P)
    old = _np.stack([old_k, old_v], axis=2)
    smp = lambda a: a[NPROMPT:].reshape((1, NB, NT) + a.shape[1:])
    win_s = _np.concatenate([old[:, NT:], new_win[NPROMPT:].reshape(NB, NT, 2, NG, HD)], axis=1)[None]
    return (y[:NPROMPT].reshape(1, NPROMPT, DM), y[NPROMPT:].reshape(NB, NT, DM),
            rows_a[:NPROMPT][None, None], nsa[:NPROMPT][None, None], new_win[:NPROMPT][None, None],
            smp(rows_a), smp(nsa), win_s)
```
